# Optimizing a Trainium2 kernel written in Bass

```python
import math
import jax, jax.numpy as jnp
from jax import lax
import numpy as np
import jax
import jax.numpy as jnp

D_MODEL = 1024
BATCH = 1
SEQ = 256
DEPTH = 1

GRID_W = 64
CTX_LEN = 256
BLK = 128
WINDOW = 128
ROPE_BASE = 10000.0
EPS = 1e-6
NEG = -1e30

A_HEADS = 8
A_KV = 2
A_DH = 64
B_GROUPS = 4
B_DG = 64
B_CHUNK = 128
C_HEADS = 4
C_DQ = 32
C_DV = 64

D_MIX = A_HEADS * A_DH + B_GROUPS * B_DG + C_HEADS * C_DV
OFF_AQ = 0
OFF_AK = OFF_AQ + A_HEADS * A_DH
OFF_AV = OFF_AK + A_KV * A_DH
OFF_BU = OFF_AV + A_KV * A_DH
OFF_BV = OFF_BU + B_GROUPS * B_DG
OFF_CQ = OFF_BV + B_GROUPS * B_DG
OFF_CK = OFF_CQ + C_HEADS * 2 * C_DQ
OFF_CV = OFF_CK + C_HEADS * 2 * C_DQ
D_IN = OFF_CV + C_HEADS * C_DV

MOE_GROUPS = 4
MOE_PER_GROUP = 4
N_EXPERTS = MOE_GROUPS * MOE_PER_GROUP
MOE_TOPK = 2
D_EXPERT = 512


def rmsnorm(x, g):
    xf = x.astype(jnp.float32)
    y = xf * lax.rsqrt(jnp.mean(xf * xf, axis=-1, keepdims=True) + EPS)
    return (y * g.astype(jnp.float32)).astype(x.dtype)

def axial_rope(x, rows, cols):
    dh = x.shape[-1]
    n = dh // 4
    inv = ROPE_BASE ** (-jnp.arange(n, dtype=jnp.float32) / n)
    xf = x.astype(jnp.float32)

    def rot(xp, pos):
        ang = pos[:, None] * inv
        cs = jnp.cos(ang)[None, :, None, :]
        sn = jnp.sin(ang)[None, :, None, :]
        x1, x2 = xp[..., :n], xp[..., n:]
        return jnp.concatenate([x1 * cs - x2 * sn, x1 * sn + x2 * cs], axis=-1)

    out = jnp.concatenate([rot(xf[..., :2 * n], rows), rot(xf[..., 2 * n:], cols)], axis=-1)
    return out.astype(x.dtype)

def _sink_probs(scores, sink):
    m = sink
    for s in scores:
        m = jnp.maximum(m, jnp.max(s, axis=-1, keepdims=True))
    es = [jnp.exp(s - m) for s in scores]
    den = jnp.exp(sink - m)
    for e in es:
        den = den + jnp.sum(e, axis=-1, keepdims=True)
    return [e / den for e in es]

def window_sink_attn(q, k, v, kc, vc, sink):
    Bn, S, Hq, dh = q.shape
    Hkv = k.shape[2]
    G = Hq // Hkv
    nb = S // BLK
    scale = dh ** -0.5
    qb = q.reshape(Bn, nb, BLK, Hkv, G, dh)

    def band(t):
        tp = jnp.pad(t, ((0, 0), (BLK, BLK), (0, 0), (0, 0))).reshape(Bn, nb + 2, BLK, Hkv, dh)
        return jnp.concatenate([tp[:, :-2], tp[:, 1:-1], tp[:, 2:]], axis=2)

    kb, vb = band(k), band(v)
    s_loc = jnp.einsum('bnqhgd,bnkhd->bnhgqk', qb, kb).astype(jnp.float32) * scale
    bi = jnp.arange(nb)[:, None, None]
    qpos = bi * BLK + jnp.arange(BLK)[None, :, None]
    kpos = (bi - 1) * BLK + jnp.arange(3 * BLK)[None, None, :]
    mask = (jnp.abs(kpos - qpos) <= WINDOW) & (kpos >= 0) & (kpos < S)
    s_loc = jnp.where(mask[None, :, None, None], s_loc, NEG)
    s_ctx = jnp.einsum('bnqhgd,bchd->bnhgqc', qb, kc).astype(jnp.float32) * scale
    p_loc, p_ctx = _sink_probs([s_loc, s_ctx], sink.astype(jnp.float32).reshape(Hkv, G, 1, 1))
    o = (jnp.einsum('bnhgqk,bnkhd->bnqhgd', p_loc.astype(v.dtype), vb)
         + jnp.einsum('bnhgqc,bchd->bnqhgd', p_ctx.astype(v.dtype), vc))
    return o.reshape(Bn, S, Hq * dh)

def ctx_sink_attn(qc, kc, vc, sink):
    Bn, L, Hq, dh = qc.shape
    Hkv = kc.shape[2]
    G = Hq // Hkv
    qg = qc.reshape(Bn, L, Hkv, G, dh)
    s = jnp.einsum('bqhgd,bkhd->bhgqk', qg, kc).astype(jnp.float32) * dh ** -0.5
    (p,) = _sink_probs([s], sink.astype(jnp.float32).reshape(Hkv, G, 1, 1))
    o = jnp.einsum('bhgqk,bkhd->bqhgd', p.astype(vc.dtype), vc)
    return o.reshape(Bn, L, Hq * dh)

def chunk_gmlp(u, v, ws, bs, gtok):
    Bn, L, _ = u.shape
    nc = L // B_CHUNK
    u = jax.nn.gelu(u).reshape(Bn, nc, B_CHUNK, B_GROUPS, B_DG)
    vf = jax.nn.gelu(v).astype(jnp.float32).reshape(Bn, nc, B_CHUNK, B_GROUPS, B_DG)
    mu = jnp.mean(vf, axis=-1, keepdims=True)
    var = jnp.mean(jnp.square(vf - mu), axis=-1, keepdims=True)
    vn = ((vf - mu) * lax.rsqrt(var + EPS) * gtok.astype(jnp.float32)).astype(u.dtype)
    s = jnp.einsum('gpq,bnqgd->bnpgd', ws, vn) + bs.T[:, :, None]
    return (u * s).reshape(Bn, L, B_GROUPS * B_DG)

def _diff_core(q1, q2, k1, k2, v, lam):
    scale = C_DQ ** -0.5
    p1 = jax.nn.softmax(jnp.einsum('bqhd,bkhd->bhqk', q1, k1).astype(jnp.float32) * scale, axis=-1)
    p2 = jax.nn.softmax(jnp.einsum('bqhd,bkhd->bhqk', q2, k2).astype(jnp.float32) * scale, axis=-1)
    w = p1 - lam * p2
    return jnp.einsum('bhqk,bkhe->bqhe', w.astype(v.dtype), v)

def diff_attn(q1, q2, k1, k2, v, lam):
    Bn, Lq, H, dq = q1.shape
    nb = Lq // BLK
    qb1 = q1.reshape(Bn, nb, BLK, H, dq).swapaxes(0, 1)
    qb2 = q2.reshape(Bn, nb, BLK, H, dq).swapaxes(0, 1)
    out = lax.map(lambda qs: _diff_core(qs[0], qs[1], k1, k2, v, lam), (qb1, qb2))
    return out.swapaxes(0, 1).reshape(Bn, Lq, H, v.shape[-1])

def diff_out(o, gsub, lam_init):
    Bn, L, H, dv = o.shape
    return (rmsnorm(o, gsub) * (1.0 - lam_init)).reshape(Bn, L, H * dv)

def token_mixers(h, hc, w_in, w_out, sink, ws, bs, gtok, gsub, lam, lam_init, rows, cols, ctx_out):
    Bn, S, _ = h.shape
    Lc = hc.shape[1]
    p = h @ w_in

    def heads(lo, hi, n, d):
        return p[..., lo:hi].reshape(Bn, S, n, d)

    def cproj(lo, hi, n, d):
        return (hc @ w_in[:, lo:hi]).reshape(Bn, Lc, n, d)

    qa = axial_rope(heads(OFF_AQ, OFF_AK, A_HEADS, A_DH), rows, cols)
    ka = axial_rope(heads(OFF_AK, OFF_AV, A_KV, A_DH), rows, cols)
    va = heads(OFF_AV, OFF_BU, A_KV, A_DH)
    ka_c = cproj(OFF_AK, OFF_AV, A_KV, A_DH)
    va_c = cproj(OFF_AV, OFF_BU, A_KV, A_DH)
    ya = window_sink_attn(qa, ka, va, ka_c, va_c, sink)
    yb = chunk_gmlp(p[..., OFF_BU:OFF_BV], p[..., OFF_BV:OFF_CQ], ws, bs, gtok)
    qd = axial_rope(heads(OFF_CQ, OFF_CK, 2 * C_HEADS, C_DQ), rows, cols).reshape(Bn, S, C_HEADS, 2, C_DQ)
    kd = axial_rope(heads(OFF_CK, OFF_CV, 2 * C_HEADS, C_DQ), rows, cols).reshape(Bn, S, C_HEADS, 2, C_DQ)
    vd = heads(OFF_CV, D_IN, C_HEADS, C_DV)
    kd_c = cproj(OFF_CK, OFF_CV, 2 * C_HEADS, C_DQ).reshape(Bn, Lc, C_HEADS, 2, C_DQ)
    vd_c = cproj(OFF_CV, D_IN, C_HEADS, C_DV)
    k1 = jnp.concatenate([kd_c[..., 0, :], kd[..., 0, :]], axis=1)
    k2 = jnp.concatenate([kd_c[..., 1, :], kd[..., 1, :]], axis=1)
    vall = jnp.concatenate([vd_c, vd], axis=1)
    yc = diff_out(diff_attn(qd[..., 0, :], qd[..., 1, :], k1, k2, vall, lam), gsub, lam_init)
    y = jnp.concatenate([ya, yb, yc], axis=-1) @ w_out
    if not ctx_out:
        return y, None
    ya_c = ctx_sink_attn(cproj(OFF_AQ, OFF_AK, A_HEADS, A_DH), ka_c, va_c, sink)
    yb_c = chunk_gmlp(hc @ w_in[:, OFF_BU:OFF_BV], hc @ w_in[:, OFF_BV:OFF_CQ], ws, bs, gtok)
    qd_c = cproj(OFF_CQ, OFF_CK, 2 * C_HEADS, C_DQ).reshape(Bn, Lc, C_HEADS, 2, C_DQ)
    yc_c = diff_out(diff_attn(qd_c[..., 0, :], qd_c[..., 1, :], kd_c[..., 0, :], kd_c[..., 1, :], vd_c, lam), gsub, lam_init)
    y_c = jnp.concatenate([ya_c, yb_c, yc_c], axis=-1) @ w_out
    return y, y_c

def hier_moe(h, w_rg, b_rg, w_re, b_re, w_gate, w_up, w_down):
    Bn, L, D = h.shape
    t = h.reshape(-1, D)
    pg = jax.nn.softmax((t @ w_rg).astype(jnp.float32) + b_rg.astype(jnp.float32), axis=-1)
    ptop, gsel = lax.top_k(pg, 1)
    le = ((t @ w_re).astype(jnp.float32) + b_re.astype(jnp.float32)).reshape(-1, MOE_GROUPS, MOE_PER_GROUP)
    le_g = jnp.sum(le * jax.nn.one_hot(gsel[:, 0], MOE_GROUPS, dtype=jnp.float32)[:, :, None], axis=1)
    lv, li = lax.top_k(le_g, MOE_TOPK)
    w = jax.nn.softmax(lv, axis=-1) * ptop
    eid = gsel * MOE_PER_GROUP + li
    gates = jnp.sum(jax.nn.one_hot(eid, N_EXPERTS, dtype=jnp.float32) * w[..., None], axis=1)
    y = jnp.zeros(t.shape, jnp.float32)
    for e in range(N_EXPERTS):
        he = jax.nn.silu(t @ w_gate[e]) * (t @ w_up[e])
        y = y + gates[:, e:e + 1] * (he @ w_down[e]).astype(jnp.float32)
    return y.astype(h.dtype).reshape(Bn, L, D)

def first_inputs(seed: int = 0) -> dict:
    key = jax.random.key(seed)
    ks = jax.random.split(key, 32)

    def nrm(k, shape, s):
        return jax.random.normal(k, shape, jnp.float32) * s

    D = D_MODEL
    return {
        'x': nrm(ks[0], (BATCH, SEQ, D), 1.0),
        'c': nrm(ks[1], (BATCH, D), 1.0),
        'ctx': nrm(ks[2], (BATCH, CTX_LEN, D), 1.0),
        'c_ctx': nrm(ks[3], (D,), 1.0),
        'w_ada': nrm(ks[4], (DEPTH, D, 6 * D), 0.2 * D ** -0.5),
        'b_ada': nrm(ks[5], (DEPTH, 6 * D), 0.01),
        'g_mix': 1.0 + nrm(ks[6], (DEPTH, D), 0.01),
        'w_in': nrm(ks[7], (DEPTH, D, D_IN), D ** -0.5),
        'sink': nrm(ks[8], (DEPTH, A_HEADS), 0.5),
        'ws_tok': nrm(ks[9], (DEPTH, B_GROUPS, B_CHUNK, B_CHUNK), B_CHUNK ** -0.5),
        'bs_tok': 1.0 + nrm(ks[10], (DEPTH, B_GROUPS, B_CHUNK), 0.02),
        'g_tok': 1.0 + nrm(ks[11], (DEPTH, B_GROUPS, B_DG), 0.01),
        'lam_q1': nrm(ks[12], (DEPTH, C_DQ), 0.1),
        'lam_k1': nrm(ks[13], (DEPTH, C_DQ), 0.1),
        'lam_q2': nrm(ks[14], (DEPTH, C_DQ), 0.1),
        'lam_k2': nrm(ks[15], (DEPTH, C_DQ), 0.1),
        'g_sub': 1.0 + nrm(ks[16], (DEPTH, C_DV), 0.01),
        'w_out': nrm(ks[17], (DEPTH, D_MIX, D), D_MIX ** -0.5),
        'g_ffn': 1.0 + nrm(ks[18], (DEPTH, D), 0.01),
        'w_rg': nrm(ks[19], (DEPTH, D, MOE_GROUPS), D ** -0.5),
        'b_rg': nrm(ks[20], (DEPTH, MOE_GROUPS), 0.01),
        'w_re': nrm(ks[21], (DEPTH, D, N_EXPERTS), D ** -0.5),
        'b_re': nrm(ks[22], (DEPTH, N_EXPERTS), 0.01),
        'w_gate': nrm(ks[23], (DEPTH, N_EXPERTS, D, D_EXPERT), D ** -0.5),
        'w_up': nrm(ks[24], (DEPTH, N_EXPERTS, D, D_EXPERT), D ** -0.5),
        'w_down': nrm(ks[25], (DEPTH, N_EXPERTS, D_EXPERT, D), D_EXPERT ** -0.5),
        'g_final': 1.0 + nrm(ks[26], (D,), 0.01),
    }

def first_block(x, c, ctx, c_ctx, w_ada, b_ada, g_mix, w_in, sink, ws_tok, bs_tok, g_tok,
              lam_q1, lam_k1, lam_q2, lam_k2, g_sub, w_out, g_ffn, w_rg, b_rg, w_re, b_re,
              w_gate, w_up, w_down, g_final):
    S = x.shape[1]
    ROWS = S // GRID_W
    rows = jnp.repeat(jnp.arange(ROWS, dtype=jnp.float32), GRID_W)
    cols = jnp.broadcast_to(jnp.arange(GRID_W, dtype=jnp.float32)[None, :], (ROWS, GRID_W)).reshape(-1)
    xc = ctx
    for l in range(DEPTH):
        last = l == DEPTH - 1
        mod = jax.nn.silu(c) @ w_ada[l] + b_ada[l]
        modc = jax.nn.silu(c_ctx) @ w_ada[l] + b_ada[l]
        sh1, sc1, gt1, sh2, sc2, gt2 = jnp.split(mod[:, None, :], 6, axis=-1)
        csh1, csc1, cgt1, csh2, csc2, cgt2 = jnp.split(modc[None, None, :], 6, axis=-1)
        lam_init = 0.8 - 0.6 * math.exp(-0.3 * l)
        lam = (jnp.exp(jnp.sum(lam_q1[l].astype(jnp.float32) * lam_k1[l].astype(jnp.float32)))
               - jnp.exp(jnp.sum(lam_q2[l].astype(jnp.float32) * lam_k2[l].astype(jnp.float32))) + lam_init)
        h = rmsnorm(x, g_mix[l]) * (1.0 + sc1) + sh1
        hc = rmsnorm(xc, g_mix[l]) * (1.0 + csc1) + csh1
        y, y_c = token_mixers(h, hc, w_in[l], w_out[l], sink[l], ws_tok[l], bs_tok[l], g_tok[l],
                              g_sub[l], lam, lam_init, rows, cols, not last)
        x = x + gt1 * y
        h2 = rmsnorm(x, g_ffn[l]) * (1.0 + sc2) + sh2
        x = x + gt2 * hier_moe(h2, w_rg[l], b_rg[l], w_re[l], b_re[l], w_gate[l], w_up[l], w_down[l])
        if not last:
            xc = xc + cgt1 * y_c
            hc2 = rmsnorm(xc, g_ffn[l]) * (1.0 + csc2) + csh2
            xc = xc + cgt2 * hier_moe(hc2, w_rg[l], b_rg[l], w_re[l], b_re[l], w_gate[l], w_up[l], w_down[l])
    return rmsnorm(x, g_final)


DEPTH_2 = 2

HEAD_DIM = 64
ROPE_DIM = HEAD_DIM // 4
ROPE_THETA = 500000.0
Q_BLOCK = 128
NEG_INF = -1e30
RMS_EPS = 1e-6

NSA_HEADS = 4
NSA_CMP_LEN = 32
NSA_CMP_STRIDE = 16
NSA_CMP_HIDDEN = 128
NSA_SEL_LEN = 64
NSA_SEL_TOPK = 16
NSA_WINDOW = 512
NSA_FORCE_SCORE = 1e4

DIL_PATTERNS = ((128, 1), (512, 4), (2048, 16))
DIL_HEADS_PER_GROUP = 2
DIL_HEADS = DIL_HEADS_PER_GROUP * len(DIL_PATTERNS)

FOX_HEADS = 6

D_FF = 2816

NSA_Q_W = NSA_HEADS * HEAD_DIM
NSA_KV_W = 6 * HEAD_DIM
NSA_GATE_W = 3 * NSA_HEADS
DIL_W = DIL_HEADS * HEAD_DIM
DIL_OUT_W = DIL_HEADS_PER_GROUP * HEAD_DIM
FOX_W = FOX_HEADS * HEAD_DIM
IN_WIDTHS = (NSA_Q_W, NSA_KV_W, NSA_GATE_W, 3 * DIL_W, 3 * FOX_W, FOX_HEADS, 3 * D_MODEL)
IN_COLS = sum(IN_WIDTHS)


def _split_cols(x, widths):
    offsets = [int(o) for o in np.cumsum(widths)[:-1]]
    return jnp.split(x, offsets, axis=-1)

def _rms_norm(x, g):
    xf = x.astype(jnp.float32)
    y = xf * lax.rsqrt(jnp.mean(xf * xf, axis=-1, keepdims=True) + RMS_EPS)
    return (y * g.astype(jnp.float32)).astype(x.dtype)

def _modulate(x, shift, scale):
    return x * (1.0 + scale) + shift

def _swiglu(x, w_in, w_out):
    gate, up = jnp.split(x @ w_in, 2, axis=-1)
    return (jax.nn.silu(gate) * up) @ w_out

def _rope_tables(seq_len):
    inv_freq = ROPE_THETA ** (-jnp.arange(0, ROPE_DIM, 2, dtype=jnp.float32) / ROPE_DIM)
    ang = jnp.arange(seq_len, dtype=jnp.float32)[:, None] * inv_freq[None, :]
    return jnp.cos(ang), jnp.sin(ang)

def _partial_rope(x, cos, sin):
    half = ROPE_DIM // 2
    c = cos[None, :, None, :]
    s = sin[None, :, None, :]
    x1 = x[..., :half].astype(jnp.float32)
    x2 = x[..., half:ROPE_DIM].astype(jnp.float32)
    rot = jnp.concatenate([x1 * c - x2 * s, x2 * c + x1 * s], axis=-1).astype(x.dtype)
    return jnp.concatenate([rot, x[..., ROPE_DIM:]], axis=-1)

def _masked_softmax(s, mask):
    s = jnp.where(mask, s, NEG_INF)
    m = jnp.max(s, axis=-1, keepdims=True)
    e = jnp.where(mask, jnp.exp(s - m), 0.0)
    den = jnp.sum(e, axis=-1, keepdims=True)
    den = jnp.where(den > 0, den, 1.0)
    return e / den, m + jnp.log(den)

def _nsa_attention(q, k_cmp, v_cmp, k_sel, v_sel, k_win, v_win, gate_logits,
                   cmp_pe, cmp_w1, cmp_w2):
    B, S = q.shape[0], q.shape[1]
    scale = HEAD_DIM ** -0.5
    n_cmp = (S - NSA_CMP_LEN) // NSA_CMP_STRIDE + 1
    cmp_start = np.arange(n_cmp) * NSA_CMP_STRIDE
    cmp_idx = cmp_start[:, None] + np.arange(NSA_CMP_LEN)[None, :]

    def compress(t, j):
        blk = t[:, cmp_idx] + cmp_pe[j]
        hid = jax.nn.silu(blk.reshape(B, n_cmp, NSA_CMP_LEN * HEAD_DIM) @ cmp_w1[j])
        return hid @ cmp_w2[j]

    kc = compress(k_cmp, 0)
    vc = compress(v_cmp, 1)
    cmp_end = jnp.asarray(cmp_start + NSA_CMP_LEN - 1)
    n_sel = S // NSA_SEL_LEN
    sel_start = np.arange(n_sel) * NSA_SEL_LEN
    ov = np.minimum(cmp_start[:, None] + NSA_CMP_LEN, sel_start[None, :] + NSA_SEL_LEN) \
        - np.maximum(cmp_start[:, None], sel_start[None, :])
    overlap = jnp.asarray(np.clip(ov, 0, None) / NSA_CMP_LEN, dtype=jnp.float32)
    top_k = min(NSA_SEL_TOPK, n_sel)
    sel_ids = jnp.arange(n_sel)
    kw_pad = jnp.pad(k_win, ((0, 0), (NSA_WINDOW, 0), (0, 0)))
    vw_pad = jnp.pad(v_win, ((0, 0), (NSA_WINDOW, 0), (0, 0)))
    win_len = NSA_WINDOW + Q_BLOCK
    gather = jax.vmap(lambda a, i: a[i])

    def block(qb):
        q0 = qb * Q_BLOCK
        t = q0 + jnp.arange(Q_BLOCK)
        qblk = lax.dynamic_slice_in_dim(q, q0, Q_BLOCK, axis=1)
        s = jnp.einsum('bqhd,bnd->bhqn', qblk, kc).astype(jnp.float32) * scale
        p_cmp, _ = _masked_softmax(s, cmp_end[None, :] <= t[:, None])
        o_cmp = jnp.einsum('bhqn,bnd->bqhd', p_cmp.astype(vc.dtype), vc)
        imp = jnp.einsum('bhqn,nj->bqj', p_cmp, overlap)
        valid = (sel_ids[None, :] * NSA_SEL_LEN) <= t[:, None]
        forced = (sel_ids[None, :] == (t // NSA_SEL_LEN)[:, None]) | (sel_ids[None, :] == 0)
        imp = jnp.where(forced, NSA_FORCE_SCORE, jnp.where(valid, imp, -1.0))
        _, blk_idx = lax.top_k(imp, top_k)
        tok = (blk_idx[..., None] * NSA_SEL_LEN + jnp.arange(NSA_SEL_LEN)).reshape(B, Q_BLOCK * top_k * NSA_SEL_LEN)
        ks = gather(k_sel, tok).reshape(B, Q_BLOCK, top_k * NSA_SEL_LEN, HEAD_DIM)
        vs = gather(v_sel, tok).reshape(B, Q_BLOCK, top_k * NSA_SEL_LEN, HEAD_DIM)
        s = jnp.einsum('bqhd,bqkd->bhqk', qblk, ks).astype(jnp.float32) * scale
        smask = (tok.reshape(B, Q_BLOCK, top_k * NSA_SEL_LEN) <= t[None, :, None])[:, None]
        p, _ = _masked_softmax(s, smask)
        o_sel = jnp.einsum('bhqk,bqkd->bqhd', p.astype(vs.dtype), vs)
        kw = lax.dynamic_slice_in_dim(kw_pad, q0, win_len, axis=1)
        vw = lax.dynamic_slice_in_dim(vw_pad, q0, win_len, axis=1)
        kpos = q0 - NSA_WINDOW + jnp.arange(win_len)
        wmask = (kpos[None, :] <= t[:, None]) & (kpos[None, :] > t[:, None] - NSA_WINDOW) & (kpos[None, :] >= 0)
        s = jnp.einsum('bqhd,bkd->bhqk', qblk, kw).astype(jnp.float32) * scale
        p, _ = _masked_softmax(s, wmask)
        o_win = jnp.einsum('bhqk,bkd->bqhd', p.astype(vw.dtype), vw)
        g = jax.nn.sigmoid(lax.dynamic_slice_in_dim(gate_logits, q0, Q_BLOCK, axis=1).astype(jnp.float32)).astype(q.dtype)
        return g[..., 0:1] * o_cmp + g[..., 1:2] * o_sel + g[..., 2:3] * o_win

    out = lax.map(block, jnp.arange(S // Q_BLOCK))
    return out.transpose(1, 0, 2, 3, 4).reshape(B, S, NSA_Q_W)

def _dilated_attention(q, k, v):
    B, S = q.shape[0], q.shape[1]
    scale = HEAD_DIM ** -0.5
    hpg = DIL_HEADS_PER_GROUP
    qg_all = [q[:, :, g * hpg:(g + 1) * hpg] for g in range(len(DIL_PATTERNS))]
    kg_all = [k[:, :, g * hpg:(g + 1) * hpg] for g in range(len(DIL_PATTERNS))]
    vg_all = [v[:, :, g * hpg:(g + 1) * hpg] for g in range(len(DIL_PATTERNS))]

    def block(qb):
        q0 = qb * Q_BLOCK
        t = q0 + jnp.arange(Q_BLOCK)
        outs, lses = [], []
        for g, (window, dil) in enumerate(DIL_PATTERNS):
            qg = lax.dynamic_slice_in_dim(qg_all[g], q0, Q_BLOCK, axis=1)
            pos = t[:, None] - dil * jnp.arange(window // dil + 1)[None, :]
            valid = pos >= 0
            idx = jnp.maximum(pos, 0)
            kk = kg_all[g][:, idx]
            vv = vg_all[g][:, idx]
            s = jnp.einsum('bqhd,bqkhd->bhqk', qg, kk).astype(jnp.float32) * scale
            p, lse = _masked_softmax(s, valid)
            outs.append(jnp.einsum('bhqk,bqkhd->bqhd', p.astype(vv.dtype), vv))
            lses.append(lse[..., 0])
        wts = jax.nn.softmax(jnp.stack(lses, axis=0), axis=0)
        wts = wts.transpose(0, 1, 3, 2)[..., None].astype(q.dtype)
        return jnp.sum(wts * jnp.stack(outs, axis=0), axis=0)

    out = lax.map(block, jnp.arange(S // Q_BLOCK))
    return out.transpose(1, 0, 2, 3, 4).reshape(B, S, DIL_OUT_W)

def _forgetting_attention(q, k, v, f_logit, f_bias):
    B, S = q.shape[0], q.shape[1]
    scale = HEAD_DIM ** -0.5
    log_f = jax.nn.log_sigmoid(f_logit.astype(jnp.float32) + f_bias.astype(jnp.float32))
    cum = jnp.cumsum(log_f, axis=1)
    cum_k = cum.transpose(0, 2, 1)[:, :, None, :]
    kpos = jnp.arange(S)

    def block(qb):
        q0 = qb * Q_BLOCK
        t = q0 + jnp.arange(Q_BLOCK)
        qblk = lax.dynamic_slice_in_dim(q, q0, Q_BLOCK, axis=1)
        cq = lax.dynamic_slice_in_dim(cum, q0, Q_BLOCK, axis=1).transpose(0, 2, 1)[..., None]
        s = jnp.einsum('bqhd,bkhd->bhqk', qblk, k).astype(jnp.float32) * scale + (cq - cum_k)
        p, _ = _masked_softmax(s, kpos[None, :] <= t[:, None])
        return jnp.einsum('bhqk,bkhd->bqhd', p.astype(v.dtype), v)

    out = lax.map(block, jnp.arange(S // Q_BLOCK))
    return out.transpose(1, 0, 2, 3, 4).reshape(B, S, FOX_W)

def _token_mixing(n, w_in, cmp_pe, cmp_w1, cmp_w2, fox_bias, br_nsa, br_dil, br_fox, w_out, cos, sin):
    B, S = n.shape[0], n.shape[1]
    proj = n @ w_in
    nsa_q, nsa_kv, nsa_g, dil_qkv, fox_qkv, fox_f, merge_g = _split_cols(proj, IN_WIDTHS)

    def heads(t, h):
        return t.reshape(B, S, h, HEAD_DIM)

    def rope_single(t):
        return _partial_rope(t[:, :, None, :], cos, sin)[:, :, 0, :]

    q_a = _partial_rope(heads(nsa_q, NSA_HEADS), cos, sin)
    kc, vc, ks, vs, kw, vw = jnp.split(nsa_kv, 6, axis=-1)
    y_a = _nsa_attention(q_a, rope_single(kc), vc, rope_single(ks), vs, rope_single(kw), vw,
                         nsa_g.reshape(B, S, NSA_HEADS, 3), cmp_pe, cmp_w1, cmp_w2)
    dq, dk, dv = jnp.split(dil_qkv, 3, axis=-1)
    y_b = _dilated_attention(_partial_rope(heads(dq, DIL_HEADS), cos, sin),
                             _partial_rope(heads(dk, DIL_HEADS), cos, sin),
                             heads(dv, DIL_HEADS))
    fq, fk, fv = jnp.split(fox_qkv, 3, axis=-1)
    y_c = _forgetting_attention(heads(fq, FOX_HEADS), heads(fk, FOX_HEADS), heads(fv, FOX_HEADS),
                                fox_f, fox_bias)
    g_a, g_b, g_c = jnp.split(jax.nn.sigmoid(merge_g), 3, axis=-1)
    merged = g_a * (y_a @ br_nsa) + g_b * (y_b @ br_dil) + g_c * (y_c @ br_fox)
    return merged @ w_out

def second_inputs(seed: int = 0) -> dict:
    key = jax.random.key(seed)
    ks = jax.random.split(key, 17)
    L, D = DEPTH_2, D_MODEL

    def nrm(k, shape, scale):
        return jax.random.normal(k, shape, jnp.float32) * scale

    return {
        'x': nrm(ks[0], (BATCH, SEQ, D), 1.0),
        'c': nrm(ks[1], (BATCH, D), 1.0),
        'ada_w': nrm(ks[2], (L, D, 9 * D), 0.5 * D ** -0.5),
        'ada_b': nrm(ks[3], (L, 9 * D), 0.02),
        'norm_g': 1.0 + nrm(ks[4], (L, 3, D), 0.05),
        'final_norm_g': 1.0 + nrm(ks[5], (D,), 0.05),
        'ffn_w_in': nrm(ks[6], (L, 2, D, 2 * D_FF), D ** -0.5),
        'ffn_w_out': nrm(ks[7], (L, 2, D_FF, D), D_FF ** -0.5),
        'mix_w_in': nrm(ks[8], (L, D, IN_COLS), D ** -0.5),
        'nsa_cmp_pe': nrm(ks[9], (L, 2, NSA_CMP_LEN, HEAD_DIM), 0.1),
        'nsa_cmp_w1': nrm(ks[10], (L, 2, NSA_CMP_LEN * HEAD_DIM, NSA_CMP_HIDDEN), (NSA_CMP_LEN * HEAD_DIM) ** -0.5),
        'nsa_cmp_w2': nrm(ks[11], (L, 2, NSA_CMP_HIDDEN, HEAD_DIM), NSA_CMP_HIDDEN ** -0.5),
        'fox_f_bias': jax.random.uniform(ks[12], (L, FOX_HEADS), jnp.float32, 1.0, 6.0),
        'br_w_nsa': nrm(ks[13], (L, NSA_Q_W, D), NSA_Q_W ** -0.5),
        'br_w_dil': nrm(ks[14], (L, DIL_OUT_W, D), DIL_OUT_W ** -0.5),
        'br_w_fox': nrm(ks[15], (L, FOX_W, D), FOX_W ** -0.5),
        'mix_w_out': nrm(ks[16], (L, D, D), D ** -0.5),
    }

def second_block(x, c, ada_w, ada_b, norm_g, final_norm_g, ffn_w_in, ffn_w_out, mix_w_in,
              nsa_cmp_pe, nsa_cmp_w1, nsa_cmp_w2, fox_f_bias, br_w_nsa, br_w_dil, br_w_fox,
              mix_w_out):
    S = x.shape[1]
    cos, sin = _rope_tables(S)
    cond = jax.nn.silu(c)
    h = x
    for l in range(DEPTH_2):
        mod = cond @ ada_w[l] + ada_b[l]
        sh1, sc1, ga1, sh2, sc2, ga2, sh3, sc3, ga3 = [m[:, None, :] for m in jnp.split(mod, 9, axis=-1)]
        n = _modulate(_rms_norm(h, norm_g[l, 0]), sh1, sc1)
        h = h + 0.5 * ga1 * _swiglu(n, ffn_w_in[l, 0], ffn_w_out[l, 0])
        n = _modulate(_rms_norm(h, norm_g[l, 1]), sh2, sc2)
        h = h + ga2 * _token_mixing(n, mix_w_in[l], nsa_cmp_pe[l], nsa_cmp_w1[l], nsa_cmp_w2[l],
                                    fox_f_bias[l], br_w_nsa[l], br_w_dil[l], br_w_fox[l],
                                    mix_w_out[l], cos, sin)
        n = _modulate(_rms_norm(h, norm_g[l, 2]), sh3, sc3)
        h = h + 0.5 * ga3 * _swiglu(n, ffn_w_in[l, 1], ffn_w_out[l, 1])
    return _rms_norm(h, final_norm_g)


def setup_inputs(seed=0):
    out = dict(first_inputs(seed))
    for name, value in second_inputs(seed + 1).items():
        if name != "x":
            out[name + "_2"] = value
    return out


def reference(
    x, c, ctx, c_ctx, w_ada, b_ada, g_mix, w_in, sink, ws_tok, bs_tok, g_tok, lam_q1, lam_k1,
    lam_q2, lam_k2, g_sub, w_out, g_ffn, w_rg, b_rg, w_re, b_re, w_gate, w_up, w_down, g_final,
    c_2, ada_w_2, ada_b_2, norm_g_2, final_norm_g_2, ffn_w_in_2, ffn_w_out_2, mix_w_in_2,
    nsa_cmp_pe_2, nsa_cmp_w1_2, nsa_cmp_w2_2, fox_f_bias_2, br_w_nsa_2, br_w_dil_2, br_w_fox_2,
    mix_w_out_2,
):
    x = first_block(
        x, c, ctx, c_ctx, w_ada, b_ada, g_mix, w_in, sink, ws_tok, bs_tok, g_tok, lam_q1,
        lam_k1, lam_q2, lam_k2, g_sub, w_out, g_ffn, w_rg, b_rg, w_re, b_re, w_gate, w_up,
        w_down, g_final,
    )
    return second_block(
        x, c_2, ada_w_2, ada_b_2, norm_g_2, final_norm_g_2, ffn_w_in_2, ffn_w_out_2, mix_w_in_2,
        nsa_cmp_pe_2, nsa_cmp_w1_2, nsa_cmp_w2_2, fox_f_bias_2, br_w_nsa_2, br_w_dil_2,
        br_w_fox_2, mix_w_out_2,
    )


_drawn_inputs = setup_inputs


def setup_inputs(seed=0):
    import zlib

    import numpy as np

    out = dict(_drawn_inputs(seed))
    spreads = {}
    factors = {'b_ada': 6.269,
     'g_mix': 8.0,
     'sink': 8.0,
     'bs_tok': 8.0,
     'g_tok': 8.0,
     'lam_q1': 64.0,
     'lam_k1': 8.0,
     'lam_q2': 8.0,
     'lam_k2': 8.0,
     'g_sub': 64.0,
     'g_ffn': 8.0,
     'b_rg': 8.0,
     'b_re': 27.483,
     'g_final': 106.017,
     'norm_g_2': 10.852,
     'nsa_cmp_pe_2': 64.0,
     'ada_b_2': 5.283,
     'nsa_cmp_w1_2': 3.788,
     'nsa_cmp_w2_2': 3.224,
     'fox_f_bias_2': 3.517}
    for name, (base, spread) in spreads.items():
        noise = np.random.default_rng([zlib.crc32(name.encode()), seed]).standard_normal(out[name].shape)
        drawn = base * np.exp(spread * noise) if base else spread * noise
        out[name] = jnp.asarray(drawn.astype(out[name].dtype))
    for name, factor in factors.items():
        out[name] = (out[name] * factor).astype(out[name].dtype)
    return out
```

```python
from contextlib import ExitStack

import numpy as np
import concourse.bass as bass
from concourse import mybir

F32 = mybir.dt.float32
F32R = mybir.dt.float32r
BF16 = mybir.dt.bfloat16
ACT = mybir.ActivationFunctionType
ALU = mybir.AluOpType
AX = mybir.AxisListType

P = 128
S = 256
NT = S // P
D = 1024
DC = D // P
UNIT = 2048
RING = 3
GW = 256
EPS = 1e-6
NEG = -1e30

A_Q, A_KV, A_D = 8, 2, 64
B_G, B_D = 4, 64
C_H, C_Q, C_V = 4, 32, 64
OFF_AQ, OFF_AK, OFF_AV, OFF_BU, OFF_BV, OFF_CQ, OFF_CK, OFF_CV, D_IN = 0, 512, 640, 768, 1024, 1280, 1536, 1792, 2048
LAM_INIT = 0.8 - 0.6
MG, MPG = 4, 4
NE = MG * MPG
DE = 512
MOE_GROUPS = NE * DE // GW
A_ORDER = [h for i in range(4) for h in (i, i + 4)]

LAYERS = 2
FF = 2816
FFN_GROUPS = FF // GW
NSA_H, DIL_H, FOX_H, HD = 4, 6, 6, 64
CMP_LEN, CMP_STRIDE, CMP_HID = 32, 16, 128
N_CMP = (S - CMP_LEN) // CMP_STRIDE + 1
ROPE2 = 16
PATTERNS = ((128, 1), (512, 4), (2048, 16))
QKV = 3072
C_DQ, C_DK, C_NQ, C_KS, C_KW, C_KS2, C_KC = 0, 384, 768, 1024, 1088, 1152, 1216
C_VC, C_VS, C_VW, C_FQ, C_FK, C_FV, C_DV, C_G, C_F = 1280, 1344, 1408, 1472, 1856, 2240, 2624, 3008, 3020
N_ROT = 20
T_COLS = ([C_DQ + 128 * i for i in range(3)] + [C_DK + 128 * i for i in range(3)] + [C_NQ, C_NQ + 128]
          + [C_KS, C_KW, C_KC] + [C_FQ + 128 * i for i in range(3)] + [C_FK + 128 * i for i in range(3)])
T_DQ, T_DK, T_NQ, T_SW, T_WS, T_CV, T_FQ, T_FK = 0, 3, 6, 8, 9, 10, 11, 14
T_SCALED = {0, 1, 2, 6, 7, 11, 12, 13}
NTB = len(T_COLS)

B1_UNITS = 12
MOE_UNITS = 3 * MOE_GROUPS
FFN_UNITS = 3 * FFN_GROUPS
MIX_UNITS = QKV // 256 + 2 + 3 * D // 256 + 3 + 4
LAYER_UNITS = 2 * FFN_UNITS + MIX_UNITS
LAYER0 = B1_UNITS + MOE_UNITS
N_UNITS = LAYER0 + LAYERS * LAYER_UNITS + RING
assert MIX_UNITS % RING == 0 and LAYER_UNITS % RING == 0 and LAYER0 % RING == 0
B1_HALVES, B2_HALVES = 12, LAYERS * 18
N_HALVES = B1_HALVES + B2_HALVES
PE_HALVES = 4
EARLY_HALVES = N_HALVES - (MOE_GROUPS - 1)


def columns(fields):
    at, n = {}, 0
    for name, width in fields:
        at[name] = slice(n, n + width)
        n += width
    return at, n


S1, S1_W = columns([("c", 8), ("cc", 8), ("c2", 8), ("gmix", 8), ("gffn", 8), ("bada", 48 + 72 * LAYERS), ("wr", 160), ("br", 20),
                    ("sink", 8), ("lam", 128), ("gtok", 256), ("gsub", 64), ("ws", 512), ("bs", 4)])
S2, S2_W = columns([("pe", 32), ("w2", 192), ("ng", 24), ("fb", 6)])
K1, K1_W = columns([("id", 128), ("ones", 128), ("tri", 128), ("cosA", 64), ("sinA", 64), ("cosC", 32), ("sinC", 32),
                    ("cos2", 16), ("sin2", 16), ("code", 20), ("cmpm", 32), ("cmp01", 32), ("cmpno", 2), ("half", 2), ("eps", 2)])


class Signal:

    def __init__(self, sem, per=1):
        self.sem, self.per = sem, per
        self.up = (sem, 1)

    def at(self, k=0, layer=0):
        return self.sem, layer * self.per + (k + 1)


def bass_network(nc, W, AD, x_in, ctx_in, s1_in, s2_in, k1_in, masks_in, gf_in, out):
    with ExitStack() as ctx:
        def sb(name, shape, dt=F32):
            return ctx.enter_context(nc.sbuf_tensor(name, shape, dt))

        def sem(name):
            return ctx.enter_context(nc.semaphore(name))

        def sig(name, per=1):
            return Signal(sem(name), per)

        raw = sb("raw", [P, RING, UNIT])
        whi = sb("whi", [P, RING, UNIT], F32R)
        wlo = sb("wlo", [P, RING, UNIT], F32R)
        ada = sb("ada", [P, 2, UNIT])
        acc = sb("acc", [P, 2, 512])
        xs = sb("xs", [P, NT, D])
        xn = sb("xn", [P, NT, D])
        hhi = sb("hhi", [P, DC, S], F32R)
        hlo = sb("hlo", [P, DC, S], F32R)
        zr = sb("zr", [P, 2, DC, S], F32R)
        row = sb("row", [P, D])
        s1 = sb("s1", [P, S1_W])
        s2_all = sb("s2_all", [P, LAYERS, S2_W])
        s2 = sb("s2", [P, S2_W])
        k1 = sb("k1", [P, K1_W])
        masks = sb("masks", [P, 4, 512], BF16)
        idb = sb("idb", [P, P], BF16)
        zb = sb("zb", [P, 512], BF16)
        mod1 = sb("mod1", [P, 4 * B1_HALVES])
        modc = sb("modc", [P, 16])
        mod2 = sb("mod2", [P, 4 * B2_HALVES])
        modl = sb("modl", [P, 72])
        am = sb("am", [P, 8])
        am2 = sb("am2", [P, 8])
        gcol = sb("gcol", [P, 8])
        st = sb("st", [P, 16])
        rh = sb("rh", [P, 8, 20], F32R)
        rl = sb("rl", [P, 8, 20], F32R)
        sm = sb("sm", [P, 256])
        cs = sb("cs", [P, 24])
        Z = sb("Z", [P, 10752])
        PS = ctx.enter_context(nc.psum_tensor("PS", [P, 8, 512], F32))

        ident, ones, tri = k1[:, K1["id"]], k1[:, K1["ones"]], k1[:, K1["tri"]]

        def z(a, n):
            return Z[:, a:a + n]

        ntmp = z(0, 1024).rearrange("p (b n) -> p b n", b=2)
        diag = z(1024, 1024).rearrange("p (c n) -> p c n", c=8)
        gfin = z(2048, 1024)
        ytmp = z(8704, 2048).rearrange("p (t n) -> p t n", t=2)
        hs = z(3072, 512).rearrange("p (c n) -> p c n", c=2)
        hg = z(3584, 512).rearrange("p (c n) -> p c n", c=2)
        hf = z(9216, 1024).rearrange("p (b c n) -> p b c n", b=2, c=2)
        gb = z(4096, 4096)
        hid_hi = zr[:, 0, :, :].rearrange("p (b c) n -> p b c n", b=4)
        hid_lo = zr[:, 1, :, :].rearrange("p (b c) n -> p b c n", b=4)
        pj = z(0, 4096).rearrange("p (t n) -> p t n", t=2)
        pc = z(4096, 1536).rearrange("p (t n) -> p t n", t=2)
        aq = z(5632, 1024).rearrange("p (b n) -> p b n", b=4)
        ak = z(6656, 512)
        cq = z(7168, 512).rearrange("p (b n) -> p b n", b=2)
        ck = z(7680, 1024).rearrange("p (b n) -> p b n", b=2)
        pr = z(8704, 1024).rearrange("p (b n) -> p b n", b=2)
        pt = z(9728, 1024).rearrange("p (b n) -> p b n", b=2)
        arow = z(0, 2048)
        qj = z(0, 2 * QKV).rearrange("p (t n) -> p t n", t=2)
        tb = z(6144, NTB * S).rearrange("p (b n) -> p b n", b=NTB)
        mg = z(6144, 2048).rearrange("p (t n) -> p t n", t=2)
        a2 = ada[:, :, :].rearrange("p r n -> p (r n)")
        pr2 = a2[:, 0:1024].rearrange("p (b n) -> p b n", b=2)
        pt2 = a2[:, 1024:2048].rearrange("p (b n) -> p b n", b=2)
        rt2 = xn[:, :, :].rearrange("p t n -> p (t n)")[:, 0:4 * 2 * N_ROT * 8].rearrange("p (k t h n) -> p k t h n", k=4, t=2, h=N_ROT)
        fl, fr = a2[:, 2048:2048 + 1536].rearrange("p (h n) -> p h n", h=6), a2[:, 3584:3840]
        mt2 = [a2[:, 2048 * i:2048 * i + 2048].rearrange("p (t n) -> p t n", t=2) for i in range(2)]

        landed = [sem(f"unit_landed{i}") for i in range(RING)]
        hi_ready, lo_ready, unit_used = sem("hi_ready"), sem("lo_ready"), sem("unit_used")
        ada_landed = [sem("ada_landed0"), sem("ada_landed1")]
        ada_used, ada_used_pe = sem("ada_used"), sem("ada_used_pe")
        acc_step = sem("acc_step")
        ada_sum, ada_out, ada_rows_out, ada_cols, mod_ready = (
            sig(n) for n in ("ada_sum", "ada_out", "ada_rows_out", "ada_cols", "mod_ready"))
        small_in, mask_in, x_landed, s2_landed, gf_landed, out_landed = (
            sem(n) for n in ("small_in", "mask_in", "x_landed", "s2_landed", "gf_landed", "out_landed"))
        const_made = sig("const_made")
        silu_done, gated, h_made, hhi_done, hlo_done, y_sum = (
            sem(n) for n in ("silu_done", "gated", "h_made", "hhi_done", "hlo_done", "y_sum"))

        def load(sp, c, e=0, first=False):
            if not first:
                sp.wait_ge(lo_ready, e * 3 + (c - RING + 1))
            u = e * 3 + c
            src = W[c] if isinstance(e, int) and e == 0 else W[bass.ds(u, 1)].rearrange("o p n -> p (o n)")
            sp.dma_start(raw[:, c % RING], src).then_inc(landed[c % RING], 16)

        def conv_hi(act, c, e=0):
            s = c % RING
            act.wait_ge(landed[s], e * 16 + 16 * (c // RING + 1))
            if not (isinstance(e, int) and c + 3 * e < RING):
                act.wait_ge(unit_used, e * 3 + (c - RING + 1))
            nc.scalar.activation(whi[:, s], raw[:, s], ACT.Copy).then_inc(hi_ready, 1)

        def conv_lo(dve, c, e=0):
            s = c % RING
            dve.wait_ge(hi_ready, e * 3 + (c + 1))
            nc.vector.tensor_tensor(wlo[:, s], raw[:, s], whi[:, s].bitcast(F32), ALU.subtract).then_inc(lo_ready, 1)

        def unit(pe, c, e=0):
            pe.wait_ge(lo_ready, e * 3 + (c + 1))
            return whi[:, c % RING], wlo[:, c % RING]

        def load_half(sp, v, e=0):
            for i in range(2):
                if v > PE_HALVES:
                    sp.wait_ge(ada_used, e * 4 + (2 * (v - 1 - PE_HALVES) + i + 1))
                elif v > 0:
                    sp.wait_ge(ada_used_pe, 2 * (v - 1) + i + 1)
                src = AD[2 * v + i] if isinstance(e, int) else AD[bass.ds(e * 4 + (2 * v + i), 1)].rearrange(
                    "o p n -> p (o n)")
                sp.dma_start(ada[:, i], src).then_inc(ada_landed[i], 16)

        def half_steps(dve, v, i, e=0):
            vv = v - PE_HALVES
            cond = 0 if v < B1_HALVES else 16
            dve.wait_ge(ada_landed[i], e * 32 + 16 * (v + 1))
            for k in range(4):
                n = 4 * i + k
                w, c, a = ada[:, i, 512 * k:512 * k + 512], cs[:, cond + n:cond + n + 1], acc[:, v % 2]
                if n == 0:
                    if vv >= 2:
                        dve.wait_ge(ada_sum.sem, e * 2 + (vv - 1))
                    ins = nc.vector.tensor_scalar(a, w, c, None, ALU.mult)
                else:
                    if n == 4:
                        dve.wait_ge(ada_used, e * 4 + (2 * vv + 1))
                    else:
                        dve.wait_ge(acc_step, e * 12 + (6 * vv + (n if n < 4 else n - 1)))
                    ins = nc.vector.scalar_tensor_tensor(a, w, c, a, ALU.mult, ALU.add)
                ins.then_inc(ada_used if k == 3 else acc_step, 1)

        def half_sum(pe, v, bank, e=0):
            vv = v - PE_HALVES
            pe.wait_ge(ada_used, e * 4 + (2 * vv + 2))
            if vv >= 2:
                pe.wait_ge(ada_out.sem, e * 2 + (vv - 1))
            for c in range(4):
                ins = nc.tensor.matmul(PS[:, bank, c:c + 1], acc[:, v % 2, c * P:(c + 1) * P], ones[:, 0:1],
                                       start=True, stop=True)
            ins.then_inc(*ada_sum.up)

        def half_out(dve, v, bank, e=0):
            dve.wait_ge(ada_sum.sem, e * 2 + (v - PE_HALVES + 1))
            b0 = S1["bada"].start
            if isinstance(e, int):
                dst = mod1[:, 4 * v:4 * v + 4] if v < B1_HALVES else mod2[:, 4 * (v - B1_HALVES):4 * (v - B1_HALVES) + 4]
                bias = s1[:, b0 + 4 * v:b0 + 4 * v + 4]
            else:
                dst = mod2[:, bass.ds(e * 8 + 4 * (v - B1_HALVES), 4)]
                bias = s1[:, bass.ds(e * 8 + (b0 + 4 * v), 4)]
            nc.vector.tensor_tensor(dst, PS[:, bank, 0:4], bias, ALU.add).then_inc(*ada_out.up)

        def mm3(out_, ah, al, bh, bl, start, stop, check=False):
            nc.tensor.matmul(out_, ah, bh, start=start, stop=False, skip_group_check=check)
            nc.tensor.matmul(out_, ah, bl, start=False, stop=False, skip_group_check=check)
            return nc.tensor.matmul(out_, al, bh, start=False, stop=stop, skip_group_check=check)

        def project(u, xh, xl, bank, tiles=range(NT)):
            wh, wl = (w.rearrange("p (k n) -> p k n", k=DC) for w in u)
            for t in tiles:
                for k in range(DC):
                    ins = mm3(PS[:, bank, t * 256:(t + 1) * 256], xh[:, k, t * P:(t + 1) * P], xl[:, k, t * P:(t + 1) * P],
                              wh[:, k], wl[:, k], k == 0, k == DC - 1)
            return ins

        def rows_product(u, kk, xh, xl, bank, start, stop, check=False):
            wh, wl = (w.rearrange("p (k n) -> p k n", k=2)[:, kk] for w in u)
            for t in range(NT):
                for half in range(2):
                    ins = mm3(PS[:, bank + 2 * t + half], xh[:, t * P:(t + 1) * P], xl[:, t * P:(t + 1) * P],
                              wh[:, half * 512:(half + 1) * 512], wl[:, half * 512:(half + 1) * 512], start, stop, check)
            return ins

        class Norm:
            def __init__(self, name, per):
                self.ss, self.rstd, self.xa, self.xd, self.am = (sig(f"{name}_{n}", per) for n in
                                                                 ("squares", "rstd", "scaled0", "scaled1", "factors"))
                self.turned, self.hi, self.lo = (sig(f"{name}_{n}", 4 * per) for n in ("turned", "hi", "lo"))
                self.gcol, self.diag, self.row_mm, self.row = (sig(f"{name}_{n}", per) for n in
                                                               ("gate", "diag", "row_mm", "row"))
                self.x_new = sig(f"{name}_x_new", per)

        def norm_act(act, N, k, l, src, dst):
            for t in range(NT):
                ins = nc.scalar.activation(dst[:, t], src[:, t], ACT.Square, scale=D ** -0.5, accum_out=st[:, t:t + 1])
            ins.then_inc(*N.ss.up)
            act.wait_ge(*N.rstd.at(k, l))
            nc.scalar.activation(dst[:, 0], src[:, 0], ACT.Copy, scale=st[:, 4:5]).then_inc(*N.xa.up)

        def norm_pool(pool, N, k, l):
            pool.wait_ge(*N.ss.at(k, l))
            nc.gpsimd.tensor_tensor(st[:, 2:4], st[:, 0:2], k1[:, K1["eps"]], ALU.add)
            pool.drain()
            nc.gpsimd.tensor_tensor(st[:, 4:6], st[:, 2:4], k1[:, K1["half"]], ALU.pow).then_inc(*N.rstd.up)

        def norm_dve(dve, N, k, l, src, dst):
            dve.wait_ge(*N.rstd.at(k, l))
            nc.vector.tensor_scalar(dst[:, 1], src[:, 1], st[:, 5:6], None, ALU.mult).then_inc(*N.xd.up)

        def turn(pe, done, src, bank, n):
            for c in range(n):
                for t in range(NT):
                    o = (c % 2) * 256 + t * P
                    ins = nc.tensor.transpose(PS[:, bank + c // 2, o:o + P], src[:, t, c * P:(c + 1) * P], ident)
                if c % 2:
                    ins.then_inc(*done.up)

        def norm_pe(pe, N, k, l, src, bank):
            pe.wait_ge(*N.xa.at(k, l))
            pe.wait_ge(*N.xd.at(k, l))
            turn(pe, N.turned, src, bank, DC)

        def spread_act(act, N, k, l, hi, shift, bank, am_):
            act.wait_ge(*N.am.at(k, l))
            for b in range(4):
                act.wait_ge(*N.turned.at(4 * k + b, l))
                for c in range(2):
                    ins = nc.scalar.activation(hi[:, 2 * b + c], PS[:, bank + b, c * 256:(c + 1) * 256], ACT.Identity,
                                               scale=am_[:, 2 * b + c:2 * b + c + 1], bias=shift[:, 2 * b + c:2 * b + c + 1])
                ins.then_inc(*N.hi.up)

        def factors_dve(dve, N, scale, g, am_):
            nc.vector.scalar_tensor_tensor(am_[:, :], scale, 1.0, g, ALU.add, ALU.mult).then_inc(*N.am.up)

        def spread_dve(dve, N, k, l, hi, lo, shift, bank, am_):
            dve.wait_ge(*N.am.at(k, l))
            for b in range(4):
                dve.wait_ge(*N.hi.at(4 * k + b, l))
                for c in range(2):
                    nc.vector.tensor_scalar(ntmp[:, b % 2, c * 256:(c + 1) * 256], PS[:, bank + b, c * 256:(c + 1) * 256],
                                            am_[:, 2 * b + c:2 * b + c + 1], shift[:, 2 * b + c:2 * b + c + 1],
                                            ALU.mult, ALU.add)
                dve.drain()
                nc.vector.tensor_tensor(lo[:, 2 * b:2 * b + 2].rearrange("p c n -> p (c n)"), ntmp[:, b % 2],
                                        hi[:, 2 * b:2 * b + 2].bitcast(F32).rearrange("p c n -> p (c n)"),
                                        ALU.subtract).then_inc(*N.lo.up)

        def split_act(act, turned, hi_sig, base, n, l):
            for b in range(n):
                act.wait_ge(*turned.at(base + b, l))
                nc.scalar.activation(hhi[:, 2 * b:2 * b + 2].rearrange("p c n -> p (c n)"), PS[:, b],
                                     ACT.Copy).then_inc(*hi_sig.up)

        def split_dve(dve, hi_sig, lo_sig, base, n, l):
            for b in range(n):
                dve.wait_ge(*hi_sig.at(base + b, l))
                nc.vector.tensor_tensor(hlo[:, 2 * b:2 * b + 2].rearrange("p c n -> p (c n)"), PS[:, b],
                                        hhi[:, 2 * b:2 * b + 2].bitcast(F32).rearrange("p c n -> p (c n)"),
                                        ALU.subtract).then_inc(*lo_sig.up)

        def gate_dve(dve, N, src, factor):
            nc.vector.tensor_scalar(gcol[:, :], src, factor, None, ALU.mult).then_inc(*N.gcol.up)

        def gate_pool(pool, N, k, l):
            pool.wait_ge(*N.gcol.at(k, l))
            nc.gpsimd.tensor_tensor(diag, mid(ident, [P, DC, P]), bc(gcol[:, :], [P, DC, P]), ALU.mult).then_inc(*N.diag.up)

        def gate_pe(pe, N, k, l):
            pe.wait_ge(*N.diag.at(k, l))
            for c in range(DC):
                o = (c % 4) * P
                ins = nc.tensor.matmul(PS[:, 4 + c // 4, o:o + P], ones, diag[:, c], start=True, stop=True)
            ins.then_inc(*N.row_mm.up)

        def gate_act(act, N, k, l):
            act.wait_ge(*N.row_mm.at(k, l))
            nc.scalar.activation(row[:, :], PS[:, 4:6].rearrange("p b n -> p (b n)"), ACT.Copy).then_inc(*N.row.up)

        def residual(dve, done, y_at):
            dve.wait_ge(*y_at)
            for t in range(NT):
                nc.vector.tensor_tensor(ytmp[:, t], PS[:, 4 + 2 * t:6 + 2 * t].rearrange("p b n -> p (b n)"), row[:, :],
                                        ALU.mult)
            dve.drain()
            for t in range(NT):
                ins = nc.vector.tensor_tensor(xs[:, t], xs[:, t], ytmp[:, t], ALU.add)
            ins.then_inc(*done.up)

        def at_gate(c0, g):
            return c0 + (3 * g - 1 if g else 0)

        def pe_gate_up(pe, g, c0, E0, h0, e=0):
            for j in range(2):
                wh, wl = (w.rearrange("p (k n) -> p k n", k=DC) for w in unit(pe, at_gate(c0, g) + j, E0 + e * 2))
                for f in range(2):
                    for k in range(DC):
                        w = slice(f * P, (f + 1) * P)
                        ins = mm3(PS[:, 2 * (g % 2) + f, j * 256:(j + 1) * 256], wh[:, k, w], wl[:, k, w],
                                  hhi[:, k], hlo[:, k], k == 0, k == DC - 1)
                ins.then_inc(unit_used, 1)

        def pe_down(pe, g, c, E0, h0, e=0):
            pe.wait_ge(hlo_done, h0 + e * 2 + (g + 1))
            u = unit(pe, c, E0 + e * 2)
            for kk in range(2):
                ins = rows_product(u, kk, hid_hi[:, g % 2, kk], hid_lo[:, g % 2, kk], 4, False, False, True)
            ins.then_inc(unit_used, 1)

        def clear_sums(pe):
            for b in range(4, 8):
                nc.tensor.matmul(PS[:, b], zb[:, 0:P], zb[:, :], start=True, stop=False, skip_group_check=True)

        def close_sums(pe):
            for b in range(4, 8):
                ins = nc.tensor.matmul(PS[:, b], zb[:, 0:P], zb[:, :], start=False, stop=True, skip_group_check=True)
            ins.then_inc(y_sum, 1)

        def act_silu(act, g, c0, E0, h0, moe, e=0):
            p = 2 * (g % 2)
            act.wait_ge(unit_used, (E0 + e * 2) * 3 + (at_gate(c0, g) + 2))
            if g >= 1:
                act.wait_ge(gated if moe else h_made, h0 + e * 2 + g)
            nc.scalar.activation(hs, PS[:, p:p + 2, 0:256], ACT.Silu).then_inc(silu_done, 1)

        def act_hi(act, g, c_down, E0, h0, e=0):
            act.wait_ge(h_made, h0 + e * 2 + (g + 1))
            if c_down is not None:
                act.wait_ge(unit_used, (E0 + e * 2) * 3 + (c_down + 1))
            nc.scalar.activation(hid_hi[:, g % 2], hf[:, g % 2], ACT.Copy).then_inc(hhi_done, 1)

        def dve_h(dve, g, h0, moe, e=0):
            p = 2 * (g % 2)
            dve.wait_ge(gated if moe else silu_done, h0 + e * 2 + (g + 1))
            nc.vector.tensor_tensor(hf[:, g % 2], hg if moe else hs, PS[:, p:p + 2, 256:512], ALU.mult).then_inc(h_made, 1)

        def dve_lo(dve, g, h0, e=0):
            dve.wait_ge(hhi_done, h0 + e * 2 + (g + 1))
            nc.vector.tensor_tensor(hid_lo[:, g % 2], hf[:, g % 2], hid_hi[:, g % 2].bitcast(F32), ALU.subtract).then_inc(hlo_done, 1)

        def hidden_loop(eng, n, body):
            with eng.Fori(0, (n - 1) // 2) as e:
                for g in (1, 2):
                    body(g, e)
            if n % 2 == 0:
                body(n - 1, 0)

        def hidden_pe(pe, n, c0, E0, h0, moe):
            clear_sums(pe)
            pe_gate_up(pe, 0, c0, E0, h0)
            if moe:
                gates_pe(pe)

            def body(g, e):
                if moe:
                    pe.wait_ge(ada_out.sem, e * 2 + (EARLY_HALVES - PE_HALVES - 2 + g))
                pe_gate_up(pe, g, c0, E0, h0, e)
                if moe:
                    pe.wait_ge(h_made, h0 + e * 2 + g)
                    half_sum(pe, EARLY_HALVES - 2 + g, 2 * (1 - g % 2), e)
                pe_down(pe, g - 1, at_gate(c0, g) + 2, E0, h0, e)

            hidden_loop(pe, n, body)
            pe_down(pe, n - 1, c0 + 3 * n - 1, E0, h0)
            close_sums(pe)
            if moe:
                half_sum(pe, N_HALVES - 1, 0)

        def hidden_act(act, n, c0, E0, h0, moe):
            def body(g, e):
                c = at_gate(c0, g)
                conv_hi(act, c + RING, E0 + e * 2)
                act_silu(act, g, c0, E0, h0, moe, e)
                conv_hi(act, c + 1 + RING, E0 + e * 2)
                act_hi(act, g, c - 1, E0, h0, e)
                conv_hi(act, c + 2 + RING, E0 + e * 2)

            conv_hi(act, c0 + RING, E0)
            if moe:
                gates_act(act)
            act_silu(act, 0, c0, E0, h0, moe)
            conv_hi(act, c0 + 1 + RING, E0)
            act_hi(act, 0, None, E0, h0)
            hidden_loop(act, n, body)
            conv_hi(act, c0 + 3 * n - 1 + RING, E0)

        def hidden_dve(dve, n, c0, E0, h0, moe):
            def body(g, e):
                c, v = at_gate(c0, g), EARLY_HALVES - 1 + g
                conv_lo(dve, c + RING, E0 + e * 2)
                if moe:
                    half_steps(dve, v, 0, e)
                dve_h(dve, g, h0, moe, e)
                conv_lo(dve, c + 1 + RING, E0 + e * 2)
                dve_lo(dve, g, h0, e)
                if moe:
                    half_out(dve, v - 1, 2 * (1 - g % 2), e)
                    half_steps(dve, v, 1, e)
                conv_lo(dve, c + 2 + RING, E0 + e * 2)

            conv_lo(dve, c0 + RING, E0)
            dve_h(dve, 0, h0, moe)
            conv_lo(dve, c0 + 1 + RING, E0)
            dve_lo(dve, 0, h0)
            hidden_loop(dve, n, body)
            if moe:
                half_out(dve, N_HALVES - 1, 0)

        N1, N3 = Norm("n1", 3), Norm("n3", 2)
        proj_mm, proj_out, rope_a, rope_c, t1_mm, t1_out = (
            sig(n) for n in ("proj_mm", "proj_out", "rope_a", "rope_c", "t1_mm", "t1_out"))
        s_mm, negmax, exp_done, p_turned, pt_out, pv_done, o_out = (
            sig(f"b1_{n}") for n in ("scores", "negmax", "exp", "p_turned", "pt_out", "pv", "o_out"))
        sink_sum, sink_exp, lam_sum, lam_exp, gelu_done, var_done, vn_scale, vn_done, gm_mm, yb_done, yc_var, yc_scale = (
            sig(n) for n in ("sink_sum", "sink_exp", "lam_sum", "lam_exp", "gelu_done", "var_done", "vn_scale", "vn_done",
                             "gm_mm", "yb_done", "yc_var", "yc_scale"))
        y1_turned, y1_hi, y1_lo = sig("y1_turned"), sig("y1_hi"), sig("y1_lo")
        router_hi, router_lo, logits, route_d, route_a, gates_done, gt_mm, gt_out, gb_mm, gb_out = (
            sig(n) for n in ("router_hi", "router_lo", "logits", "route_d", "route_a", "gates_done", "gt_mm", "gt_out",
                             "gb_mm", "gb_out"))
        cond_done = sig("cond_done")

        xc_tok = z(0, 2048).rearrange("p (t n) -> p t n", t=2)
        crow = z(2048, 2048)
        xcn = z(4096, 2048).rearrange("p (t n) -> p t n", t=2)
        zhi, zlo = zr[:, 0], zr[:, 1]
        nm1, nms, den1, rd1 = sm[:, 0:32], sm[:, 32:48], sm[:, 48:80], sm[:, 80:112]
        lsum, lexp, lam, nsink, stmp, vstat, gsub8 = (sm[:, 112:114], sm[:, 114:116], sm[:, 116:117], sm[:, 120:128],
                                                      sm[:, 128:144], sm[:, 144:168], sm[:, 192:256])
        IN_UNITS = [(OFF_AK, 0), (OFF_CK, 256), (OFF_CV, 512), (OFF_AQ, None), (OFF_AQ + 256, None), (OFF_CQ, None),
                    (OFF_BU, None), (OFF_BV, None)]
        FILL = {}
        for u_, (_, c_) in enumerate(IN_UNITS):
            for src_ in (("c", "x") if c_ is not None else ("x",)):
                FILL[u_, src_] = len(FILL)
        TURNS = [(pc[:, :, 0:P], ak[:, 0:256], 1.0), (pj[:, :, OFF_AK:OFF_AK + P], ak[:, 256:512], 1.0)]
        TURNS += [(pj[:, :, P * b:P * b + P], aq[:, b], A_D ** -0.5) for b in range(4)]
        for b_ in range(2):
            TURNS += [(pc[:, :, 256 + P * b_:256 + P * b_ + P], ck[:, b_, 0:256], 1.0),
                      (pj[:, :, OFF_CK + P * b_:OFF_CK + P * b_ + P], ck[:, b_, 256:512], 1.0),
                      (pj[:, :, OFF_CQ + P * b_:OFF_CQ + P * b_ + P], cq[:, b_], C_Q ** -0.5)]
        PASSES = 32

        def bc(ap, shape):
            return ap.unsqueeze(len(shape) - 1).to_broadcast(shape)

        def mid(ap, shape):
            return ap.unsqueeze(1).to_broadcast(shape)

        def rope(eng, ops, x, cos, sin, tmp):
            x1, x2 = x
            t1, t2, t3, t4 = tmp
            ops.tensor_tensor(t1, x1, cos, ALU.mult)
            ops.tensor_tensor(t2, x2, sin, ALU.mult)
            ops.tensor_tensor(t3, x1, sin, ALU.mult)
            ops.tensor_tensor(t4, x2, cos, ALU.mult)
            eng.drain()
            ops.tensor_tensor(x1, t1, t2, ALU.subtract)
            return ops.tensor_tensor(x2, t3, t4, ALU.add)

        def a_scores(p):
            t, j = (p % 16) // 8, p % 8
            if p < 16:
                r = slice(64 * (j % 2), 64 * (j % 2) + 64)
                kv = j % 2
                v = [pc[:, c, P + 64 * kv:P + 64 * kv + 64] for c in range(2)]
                v += [pj[:, c, OFF_AV + 64 * kv:OFF_AV + 64 * kv + 64] for c in range(2)]
                return aq[r, j // 2, t * P:(t + 1) * P], ak[r, :], v
            r, h = slice(32 * (j % 4), 32 * (j % 4) + 32), j // 2
            v = [pc[:, c, 512 + 64 * h:512 + 64 * h + 64] for c in range(2)]
            v += [pj[:, c, OFF_CV + 64 * h:OFF_CV + 64 * h + 64] for c in range(2)]
            return cq[r, j // 4, t * P:(t + 1) * P], ck[r, j // 4, :], v

        ATT_STEPS = {1 + 6 * k: B1_UNITS + k for k in range(EARLY_HALVES - B1_UNITS)}
        ATT_SUMS = {5 + 6 * k: B1_UNITS + k for k in range(EARLY_HALVES - 1 - B1_UNITS)}
        L = sm[:, 0:40].rearrange("p (t n) -> p t n", t=2)
        gates = sm[:, 40:72].rearrange("p (t g j) -> p t g j", t=2, g=MG)
        gateT = z(8704, 256)

        def gates_pe(pe):
            pe.wait_ge(*gates_done.at(0))
            for t in range(NT):
                ins = nc.tensor.transpose(PS[0:NE, 3, t * P:(t + 1) * P], sm[:, 40 + NE * t:40 + NE * t + NE], ident)
            ins.then_inc(*gt_mm.up)
            pe.wait_ge(*gt_out.at(0))
            for i in range(NE // 2):
                if i >= 2:
                    pe.wait_ge(*gb_out.at(i - 2))
                for j in range(2):
                    e = 2 * i + j
                    ins = nc.tensor.matmul(PS[:, 2 + i % 2, j * 256:(j + 1) * 256], ident[0:NE, e:e + 1].to_broadcast([NE, P]),
                                           gateT[0:NE, :], start=True, stop=True)
                ins.then_inc(*gb_mm.up)
            pe.wait_ge(*gb_out.at(NE // 2 - 1))

        def gates_act(act):
            act.wait_ge(*gt_mm.at(0))
            nc.scalar.activation(gateT[0:NE, :], PS[0:NE, 3, 0:256], ACT.Copy).then_inc(*gt_out.up)
            for i in range(NE // 2):
                act.wait_ge(*gb_mm.at(i))
                nc.scalar.activation(gb[:, 512 * i:512 * i + 512], PS[:, 2 + i % 2], ACT.Copy).then_inc(*gb_out.up)

        def route_dve(dve):
            code4 = s_code
            L4, E16 = L[:, :, 0:4], L[:, :, 4:20]
            a = [sm[:, 80 + 8 * i:88 + 8 * i].rearrange("p (t n) -> p t n", t=2) for i in range(12)]
            m = [sm[:, 176 + 2 * i:178 + 2 * i] for i in range(12)]
            prod = sm[:, 208:240].rearrange("p (t g j) -> p t g j", t=2, g=MG)
            s4 = [P, 2, 4]

            def best(x, top, mask, eq, cm):
                nc.vector.tensor_reduce(top, x, AX.X, ALU.max)
                dve.drain()
                nc.vector.tensor_tensor(eq, x, bc(top, s4), ALU.is_ge)
                dve.drain()
                nc.vector.tensor_tensor(eq, eq, mid(code4, s4), ALU.mult)
                dve.drain()
                nc.vector.tensor_reduce(cm, eq, AX.X, ALU.max)
                dve.drain()
                nc.vector.tensor_tensor(mask, eq, bc(cm, s4), ALU.is_equal)
                dve.drain()

            dve.wait_ge(*logits.at(0))
            nc.vector.tensor_tensor(L, PS[:, 2, 0:64].rearrange("p (t n) -> p t n", t=2)[:, :, 0:20],
                                    mid(s1[:, S1["br"]], [P, 2, 20]), ALU.add)
            dve.drain()
            best(L4, m[0], a[0], a[1], m[1])
            nc.vector.tensor_tensor(a[2], L4, bc(m[0], s4), ALU.subtract).then_inc(*route_d.up)
            nc.vector.tensor_tensor(prod, E16.rearrange("p t (g j) -> p t g j", g=MG), bc(a[0], [P, 2, 4, 4]), ALU.mult)
            dve.drain()
            nc.vector.tensor_reduce(a[4], prod.rearrange("p t g j -> p t j g"), AX.X, ALU.add)
            dve.drain()
            best(a[4], m[2], a[5], a[6], m[3])
            nc.vector.scalar_tensor_tensor(a[7], a[5], NEG, a[4], ALU.mult, ALU.add)
            dve.drain()
            best(a[7], m[4], a[8], a[9], m[5])
            nc.vector.tensor_tensor(m[6], m[4], m[2], ALU.subtract).then_inc(*route_d.up)
            dve.wait_ge(*route_a.at(1))
            nc.vector.tensor_reduce(m[8], a[3], AX.X, ALU.add)
            nc.vector.tensor_scalar(m[9], m[7], 1.0, None, ALU.add)
            dve.drain()
            nc.vector.tensor_tensor(m[10], m[8], m[9], ALU.mult)
            dve.drain()
            nc.vector.reciprocal(m[8], m[10])
            dve.drain()
            nc.vector.tensor_tensor(m[9], m[8], m[7], ALU.mult)
            dve.drain()
            nc.vector.tensor_tensor(a[5], a[5], bc(m[8], s4), ALU.mult)
            nc.vector.tensor_tensor(a[8], a[8], bc(m[9], s4), ALU.mult)
            dve.drain()
            nc.vector.tensor_tensor(a[5], a[5], a[8], ALU.add)
            dve.drain()
            for t in range(NT):
                ins = nc.vector.tensor_tensor(gates[:, t], bc(a[0][:, t], [P, 4, 4]), mid(a[5][:, t], [P, 4, 4]), ALU.mult)
            ins.then_inc(*gates_done.up)

        def route_act(act):
            for i, (src, dst) in enumerate(((96, 104), (188, 190))):
                n = 8 if i == 0 else 2
                act.wait_ge(*route_d.at(i))
                nc.scalar.activation(sm[:, dst:dst + n], sm[:, src:src + n], ACT.Exp).then_inc(*route_a.up)

        s_code = k1[:, K1["code"]][:, 0:4]

        def pe_block1(pe):
            pe.wait_ge(small_in, 32)
            pe.wait_ge(*cond_done.at(0))
            for v in range(PE_HALVES):
                if v >= 2:
                    pe.wait_ge(*ada_rows_out.at(v - 2))
                for i in range(2):
                    pe.wait_ge(ada_landed[i], 16 * (v + 1))
                    for k in range(4):
                        n = 4 * i + k
                        ins = nc.tensor.matmul(PS[0:2, 6 + v % 2, :], cs[:, n:16:8], ada[:, i, 512 * k:512 * k + 512],
                                               start=n == 0, stop=n == 7)
                    ins.then_inc(ada_used_pe, 1)
            norm_pe(pe, N1, 0, 0, xn, 0)
            pe.wait_ge(*ada_rows_out.at(PE_HALVES - 1))
            for c in range(16):
                ins = nc.tensor.transpose(PS[:, 6, 2 * c:2 * c + 2], crow[0:2, c * P:(c + 1) * P], ident[0:2, 0:2])
            ins.then_inc(*ada_cols.up)
            pe.wait_ge(*mod_ready.at(0))
            norm_pe(pe, N1, 1, 0, xcn, 4)
            pe.wait_ge(*N1.lo.at(7))
            for u in range(8):
                both = unit(pe, u)
                for src in ("c", "x"):
                    if (u, src) not in FILL:
                        continue
                    f = FILL[u, src]
                    if f >= 6:
                        pe.wait_ge(*proj_out.at(f - 6))
                    xh, xl = (hhi, hlo) if src == "x" else (zhi, zlo)
                    project(both, xh, xl, f % 6).then_inc(unit_used if src == "x" else proj_mm.sem, 1)
                if u >= 2:
                    half_sum(pe, u + 2, 6 + u % 2)
            half_sum(pe, 10, 6)
            pe.wait_ge(*proj_out.at(len(FILL) - 1))
            for i, (src, _, _) in enumerate(TURNS):
                if i == 1:
                    pe.wait_ge(*rope_a.at(0))
                if i == 7:
                    pe.wait_ge(*rope_c.at(0))
                if i >= 4:
                    pe.wait_ge(*t1_out.at(i - 4))
                for t in range(NT):
                    ins = nc.tensor.transpose(PS[:, i % 4, t * P:(t + 1) * P], src[:, t], ident)
                ins.then_inc(*t1_mm.up)
            half_sum(pe, 11, 7)
            pe.wait_ge(*vn_done.at(0))
            w0 = S1["ws"].start
            for g in range(B_G):
                ins = nc.tensor.matmul(PS[:, 5, g * P:(g + 1) * P], s1[:, w0 + g * P:w0 + (g + 1) * P],
                                       pj[:, :, OFF_BV + 64 * g:OFF_BV + 64 * g + 64], start=True, stop=True)
            ins.then_inc(*gm_mm.up)
            pe.wait_ge(*t1_out.at(len(TURNS) - 1))
            pe.wait_ge(*const_made.at(0))
            pe.wait_ge(mask_in, 16)
            for i in range(PASSES + 2):
                if i < PASSES:
                    q, k, _ = a_scores(i)
                    if i >= 2:
                        pe.wait_ge(*exp_done.at(i - 2))
                    if i < 16:
                        nc.tensor.matmul(PS[:, i % 2], idb[:, :], masks[:, i // 8], start=True, stop=False)
                    nc.tensor.matmul(PS[:, i % 2], q, k, start=i >= 16, stop=True).then_inc(*s_mm.up)
                if 1 <= i <= PASSES:
                    p = i - 1
                    pe.wait_ge(*exp_done.at(p))
                    if p >= 2:
                        pe.wait_ge(*pt_out.at(p - 2))
                    for c in range(4):
                        ins = nc.tensor.transpose(PS[:, 2 + p % 2, c * P:(c + 1) * P], pr[:, p % 2, c * P:(c + 1) * P], ident)
                    ins.then_inc(*p_turned.up)
                if i >= 2:
                    p = i - 2
                    pe.wait_ge(*pt_out.at(p))
                    if p == 8:
                        pe.wait_ge(*yb_done.at(0))
                    if p % 8 == 0 and p >= 16:
                        pe.wait_ge(*o_out.at(p // 8 - 2))
                    v = a_scores(p)[2]
                    for c in range(4):
                        ins = nc.tensor.matmul(PS[:, 4 + (p // 8) % 2, 64 * (p % 8):64 * (p % 8) + 64],
                                               pt[:, p % 2, c * P:(c + 1) * P], v[c], start=c == 0, stop=c == 3)
                    ins.then_inc(*pv_done.up)
                if i in ATT_SUMS:
                    half_sum(pe, ATT_SUMS[i], 6 + ATT_SUMS[i] % 2)
            pe.wait_ge(*o_out.at(3))
            turn(pe, y1_turned, xn, 0, DC)
            gate_pe(pe, N1, 0, 0)
            pe.wait_ge(*N1.row.at(0))
            pe.wait_ge(*ada_out.at(EARLY_HALVES - 2 - PE_HALVES))
            pe.wait_ge(*y1_lo.at(3))
            for u in range(4):
                both = unit(pe, 8 + u)
                for kk in range(2):
                    ins = rows_product(both, kk, hhi[:, 2 * u + kk], hlo[:, 2 * u + kk], 4, u + kk == 0, u + kk == 4)
                ins.then_inc(unit_used, 1)
            norm_pe(pe, N1, 2, 0, xn, 0)
            gate_pe(pe, N1, 1, 0)
            pe.wait_ge(*N1.lo.at(11))
            pe.wait_ge(*router_lo.at(0))
            for t in range(NT):
                for k in range(DC):
                    ts = slice(t * P, (t + 1) * P)
                    ins = mm3(PS[:, 2, 32 * t:32 * t + 20], hhi[:, k, ts], hlo[:, k, ts], rh[:, k], rl[:, k], k == 0, k == DC - 1)
            ins.then_inc(*logits.up)
            pe.wait_ge(*N1.row.at(1))
            hidden_pe(pe, MOE_GROUPS, B1_UNITS, 0, 0, True)

        def act_block1(act):
            act.wait_ge(small_in, 32)
            nc.scalar.activation(cs[:, :], s1[:, 0:24], ACT.Silu).then_inc(*cond_done.up)
            w0 = S1["wr"].start
            nc.scalar.activation(rh[:, :, :], s1[:, w0:w0 + 160].rearrange("p (k n) -> p k n", k=8),
                                 ACT.Copy).then_inc(*router_hi.up)
            act.wait_ge(x_landed, 32)
            norm_act(act, N1, 0, 0, xs, xn)
            norm_act_ctx(act)
            for v in range(PE_HALVES):
                act.wait_ge(ada_used_pe, 2 * v + 2)
                nc.scalar.activation(crow[0:2, 512 * v:512 * v + 512], PS[0:2, 6 + v % 2, :], ACT.Copy).then_inc(*ada_rows_out.up)
            spread_act(act, N1, 0, 0, hhi, mod1[:, 0:8], 0, am)
            spread_act(act, N1, 1, 0, zhi, modc[:, 0:8], 4, am2)
            for u in range(RING):
                conv_hi(act, u)
            for u in range(8):
                for src in ("c", "x"):
                    if (u, src) in FILL:
                        if src == "c":
                            act.wait_ge(*proj_mm.at(u))
                            dst = pc[:, :, IN_UNITS[u][1]:IN_UNITS[u][1] + 256]
                        else:
                            act.wait_ge(unit_used, u + 1)
                            dst = pj[:, :, IN_UNITS[u][0]:IN_UNITS[u][0] + 256]
                        nc.scalar.activation(dst, PS[:, FILL[u, src] % 6].rearrange("p (t n) -> p t n", t=2),
                                             ACT.Copy).then_inc(*proj_out.up)
                conv_hi(act, u + RING)
            act.drain()
            uv = pj[:, :, OFF_BU:OFF_CQ]
            nc.scalar.activation(uv, uv, ACT.Gelu_apprx_tanh).then_inc(*gelu_done.up)
            for i, (_, dst, scale) in enumerate(TURNS):
                act.wait_ge(*t1_mm.at(i))
                nc.scalar.activation(dst, PS[:, i % 4, 0:256], ACT.Copy, scale=scale).then_inc(*t1_out.up)
            act.wait_ge(*lam_sum.at(0))
            nc.scalar.activation(lexp, lsum, ACT.Exp).then_inc(*lam_exp.up)
            for i in range(PASSES + 1):
                if i < PASSES:
                    act.wait_ge(*negmax.at(i))
                    if i >= 2:
                        act.wait_ge(*p_turned.at(i - 2))
                    bias = nms[:, i:i + 1] if i < 16 else nm1[:, i:i + 1]
                    nc.scalar.activation(pr[:, i % 2], PS[:, i % 2], ACT.Exp, bias=bias,
                                         accum_out=den1[:, i:i + 1]).then_inc(*exp_done.up)
                if i >= 1:
                    p = i - 1
                    act.wait_ge(*p_turned.at(p))
                    if p >= 2:
                        act.wait_ge(*pv_done.at(p - 2))
                    nc.scalar.activation(pt[:, p % 2], PS[:, 2 + p % 2], ACT.Copy).then_inc(*pt_out.up)
                if i in (8, 16):
                    t = i // 8 - 1
                    act.wait_ge(*sink_sum.at(t))
                    nc.scalar.activation(stmp[:, 8 * t:8 * t + 8], stmp[:, 8 * t:8 * t + 8], ACT.Exp).then_inc(*sink_exp.up)
            split_act(act, y1_turned, y1_hi, 0, 4, 0)
            gate_act(act, N1, 0, 0)
            for u in range(8, 12):
                conv_hi(act, u + RING)
            act.wait_ge(*N1.x_new.at(0))
            norm_act(act, N1, 2, 0, xs, xn)
            spread_act(act, N1, 2, 0, hhi, mod1[:, 24:32], 0, am)
            gate_act(act, N1, 1, 0)
            route_act(act)
            hidden_act(act, MOE_GROUPS, B1_UNITS, 0, 0, True)
            act.wait_ge(*N1.x_new.at(1))
            norm_stats(act, N3)

        def norm_act_ctx(act):
            norm_act(act, N1, 1, 0, xc_tok, xcn)

        def norm_stats(act, N):
            for t in range(NT):
                ins = nc.scalar.activation(xn[:, t], xs[:, t], ACT.Square, scale=D ** -0.5, accum_out=st[:, t:t + 1])
            ins.then_inc(*N.ss.up)

        def pool_block1(pool):
            nc.gpsimd.memset(zb[:, :], 0.0)
            pool.wait_ge(small_in, 32)
            nc.gpsimd.tensor_copy(idb[:, :], ident).then_inc(*const_made.up)
            norm_pool(pool, N1, 0, 0)
            pool.wait_ge(*N1.xa.at(0))
            pool.wait_ge(*N1.xd.at(0))
            norm_pool(pool, N1, 1, 0)
            tmpA = [z(8704 + 320 * i, 320).rearrange("p (h f n) -> p h f n", h=10, f=2) for i in range(4)]
            tmpC = [z(8704 + 256 * i, 256).rearrange("p (h f n) -> p h f n", h=16, f=2) for i in range(4)]
            pool.wait_ge(*proj_out.at(FILL[4, "x"]))
            for t in range(NT):
                x = pj[:, t, 0:640].rearrange("p (h f s n) -> p h f s n", h=10, f=2, s=2)
                c, s_ = (mid(k1[:, K1[n]].rearrange("p (t f n) -> p t f n", t=2, f=2)[:, t], [P, 10, 2, 16]) for n in ("cosA", "sinA"))
                ins = rope(pool, nc.gpsimd, (x[:, :, :, 0], x[:, :, :, 1]), c, s_, tmpA)
                if t:
                    ins.then_inc(*rope_a.up)
                pool.drain()
            pool.wait_ge(*proj_out.at(FILL[5, "x"]))
            for t in range(NT):
                x = pj[:, t, OFF_CQ:OFF_CV].rearrange("p (h f s n) -> p h f s n", h=16, f=2, s=2)
                c, s_ = (mid(k1[:, K1[n]].rearrange("p (t f n) -> p t f n", t=2, f=2)[:, t], [P, 16, 2, 8]) for n in ("cosC", "sinC"))
                ins = rope(pool, nc.gpsimd, (x[:, :, :, 0], x[:, :, :, 1]), c, s_, tmpC)
                if t:
                    ins.then_inc(*rope_c.up)
                pool.drain()
            pool.wait_ge(*var_done.at(0))
            nc.gpsimd.tensor_tensor(vstat[:, 8:16], vstat[:, 0:8], k1[:, K1["half"]][:, 0:1].to_broadcast([P, 8]),
                                    ALU.pow).then_inc(*vn_scale.up)
            for t in range(NT):
                pool.wait_ge(*yc_var.at(t))
                nc.gpsimd.tensor_tensor(vstat[:, 4:8], vstat[:, 0:4], k1[:, K1["half"]][:, 0:1].to_broadcast([P, 4]),
                                        ALU.pow).then_inc(*yc_scale.up)
            gate_pool(pool, N1, 0, 0)
            pool.wait_ge(*N1.x_new.at(0))
            norm_pool(pool, N1, 2, 0)
            gate_pool(pool, N1, 1, 0)

            def gate_hidden(g, e):
                pool.wait_ge(silu_done, e * 2 + (g + 1))
                if g:
                    pool.wait_ge(h_made, e * 2 + g)
                a = (g // 2) * 256
                w = gb[:, a:a + 256] if isinstance(e, int) else gb[:, bass.ds(e * 256 + a, 256)]
                nc.gpsimd.tensor_tensor(hg, hs, mid(w, [P, 2, 256]), ALU.mult).then_inc(gated, 1)

            pool.wait_ge(*gb_out.at(NE // 2 - 1))
            gate_hidden(0, 0)
            hidden_loop(pool, MOE_GROUPS, gate_hidden)
            norm_pool(pool, N3, 0, 0)

        def dve_block1(dve):
            dve.wait_ge(*router_hi.at(0))
            w0 = S1["wr"].start
            nc.vector.tensor_tensor(rl[:, :, :], s1[:, w0:w0 + 160].rearrange("p (k n) -> p k n", k=8),
                                    rh[:, :, :].bitcast(F32), ALU.subtract).then_inc(*router_lo.up)
            lm = s1[:, S1["lam"]].rearrange("p (a b n) -> p a b n", a=2, b=2)
            lt = sm[:, 0:64].rearrange("p (a n) -> p a n", a=2)
            nc.vector.tensor_tensor(lt, lm[:, :, 0], lm[:, :, 1], ALU.mult)
            nc.vector.tensor_scalar(nsink, s1[:, S1["sink"]], -1.0, None, ALU.mult)
            nc.vector.tensor_scalar(gsub8, s1[:, S1["gsub"]], 1.0 - LAM_INIT, None, ALU.mult)
            dve.drain()
            nc.vector.tensor_reduce(lsum, lt, AX.X, ALU.add).then_inc(*lam_sum.up)
            norm_dve(dve, N1, 0, 0, xs, xn)
            norm_dve(dve, N1, 1, 0, xc_tok, xcn)
            dve.wait_ge(*ada_cols.at(0))
            cols = PS[:, 6, 0:32].rearrange("p (c s) -> p s c", s=2)
            b0 = S1["bada"].start
            nc.vector.tensor_tensor(mod1[:, 0:16], cols[:, 0], s1[:, b0:b0 + 16], ALU.add)
            nc.vector.tensor_tensor(modc[:, :], cols[:, 1], s1[:, b0:b0 + 16], ALU.add).then_inc(*mod_ready.up)
            dve.drain()
            factors_dve(dve, N1, mod1[:, 8:16], s1[:, S1["gmix"]], am)
            factors_dve(dve, N1, modc[:, 8:16], s1[:, S1["gmix"]], am2)
            spread_dve(dve, N1, 0, 0, hhi, hlo, mod1[:, 0:8], 0, am)
            spread_dve(dve, N1, 1, 0, zhi, zlo, modc[:, 0:8], 4, am2)
            for u in range(RING):
                conv_lo(dve, u)
            for u in range(8):
                conv_lo(dve, u + RING)
                if u >= 3:
                    half_out(dve, u + 1, 6 + (u + 1) % 2)
                half_steps(dve, u + 4, 0)
                half_steps(dve, u + 4, 1)
            half_out(dve, 9, 7)
            half_out(dve, 10, 6)
            dve.wait_ge(*gelu_done.at(0))
            for t in range(NT):
                v4 = pj[:, t, OFF_BV:OFF_CQ].rearrange("p (g n) -> p g n", g=4)
                nc.vector.tensor_reduce(vstat[:, 16 + 4 * t:20 + 4 * t], v4, AX.X, ALU.add)
            dve.drain()
            nc.vector.tensor_scalar(vstat[:, 16:24], vstat[:, 16:24], -1.0 / B_D, None, ALU.mult)
            dve.drain()
            sq = xn[:, :, 0:256]
            for t in range(NT):
                v4 = pj[:, t, OFF_BV:OFF_CQ].rearrange("p (g n) -> p g n", g=4)
                nc.vector.tensor_tensor(v4, v4, bc(vstat[:, 16 + 4 * t:20 + 4 * t], [P, 4, 64]), ALU.add)
            dve.drain()
            nc.vector.tensor_tensor(sq, pj[:, :, OFF_BV:OFF_CQ], pj[:, :, OFF_BV:OFF_CQ], ALU.mult)
            dve.drain()
            for t in range(NT):
                nc.vector.tensor_reduce(vstat[:, 4 * t:4 * t + 4], sq[:, t].rearrange("p (g n) -> p g n", g=4), AX.X, ALU.add)
            dve.drain()
            nc.vector.tensor_scalar(vstat[:, 0:8], vstat[:, 0:8], 1.0 / B_D, EPS, ALU.mult, ALU.add).then_inc(*var_done.up)
            dve.wait_ge(*vn_scale.at(0))
            for t in range(NT):
                v4 = pj[:, t, OFF_BV:OFF_CQ].rearrange("p (g n) -> p g n", g=4)
                nc.vector.tensor_tensor(v4, v4, bc(vstat[:, 8 + 4 * t:12 + 4 * t], [P, 4, 64]), ALU.mult)
            dve.drain()
            nc.vector.tensor_tensor(pj[:, :, OFF_BV:OFF_CQ], pj[:, :, OFF_BV:OFF_CQ], mid(s1[:, S1["gtok"]], [P, 2, 256]),
                                    ALU.mult).then_inc(*vn_done.up)
            half_out(dve, 11, 7)
            dve.wait_ge(*gm_mm.at(0))
            for g in range(B_G):
                b = S1["bs"].start + g
                ins = nc.vector.scalar_tensor_tensor(
                    xn[:, :, 512 + 64 * g:576 + 64 * g], PS[:, 5, g * P:(g + 1) * P].rearrange("p (t n) -> p t n", t=2),
                    s1[:, b:b + 1], pj[:, :, OFF_BU + 64 * g:OFF_BU + 64 * g + 64], ALU.add, ALU.mult)
            ins.then_inc(*yb_done.up)
            dve.wait_ge(*lam_exp.at(0))
            nc.vector.tensor_tensor(lam, lexp[:, 1:2], lexp[:, 0:1], ALU.subtract)
            dve.drain()
            nc.vector.tensor_scalar(lam, lam, -LAM_INIT, None, ALU.add)
            dve.drain()

            def finish(f):
                t = f % 2
                O = PS[:, 4 + f % 2].rearrange("p (j n) -> p j n", j=8)
                dn, rd = den1[:, 8 * f:8 * f + 8], rd1[:, 8 * f:8 * f + 8]
                if f < 2:
                    dve.wait_ge(*sink_exp.at(f))
                    nc.vector.tensor_tensor(dn, dn, stmp[:, 8 * f:8 * f + 8], ALU.add)
                    dve.drain()
                dve.wait_ge(*pv_done.at(8 * f + 7))
                nc.vector.reciprocal(rd, dn)
                dve.drain()
                if f < 2:
                    nc.vector.tensor_tensor(xn[:, t, 0:512].rearrange("p (j n) -> p j n", j=8), O, bc(rd, [P, 8, 64]),
                                            ALU.mult).then_inc(*o_out.up)
                    return
                second = rd.rearrange("p (h m) -> p m h", m=2)[:, 1]
                nc.vector.tensor_scalar(second, second, lam, None, ALU.mult)
                dve.drain()
                both = row[:, 0:512].rearrange("p (j n) -> p j n", j=8)
                bh = row[:, 0:512].rearrange("p (h m n) -> p m h n", h=4, m=2)
                o4 = row[:, 512:768].rearrange("p (h n) -> p h n", h=4)
                q4 = row[:, 768:1024].rearrange("p (h n) -> p h n", h=4)
                nc.vector.tensor_tensor(both, O, bc(rd, [P, 8, 64]), ALU.mult)
                dve.drain()
                nc.vector.tensor_tensor(o4, bh[:, 0], bh[:, 1], ALU.add)
                dve.drain()
                nc.vector.tensor_tensor(q4, o4, o4, ALU.mult)
                dve.drain()
                nc.vector.tensor_reduce(vstat[:, 0:4], q4, AX.X, ALU.add)
                dve.drain()
                nc.vector.tensor_scalar(vstat[:, 0:4], vstat[:, 0:4], 1.0 / C_V, EPS, ALU.mult, ALU.add).then_inc(*yc_var.up)
                dve.wait_ge(*yc_scale.at(t))
                nc.vector.tensor_tensor(o4, o4, bc(vstat[:, 4:8], [P, 4, 64]), ALU.mult)
                dve.drain()
                nc.vector.tensor_tensor(xn[:, t, 768:1024].rearrange("p (h n) -> p h n", h=4), o4, mid(gsub8, [P, 4, 64]),
                                        ALU.mult).then_inc(*o_out.up)

            for i in range(PASSES + 3):
                if i < PASSES:
                    dve.wait_ge(*s_mm.at(i))
                    ins = nc.vector.tensor_reduce(nm1[:, i:i + 1], PS[:, i % 2], AX.X, ALU.max, negate=True)
                    if i < 16:
                        dve.drain()
                        ins = nc.vector.tensor_tensor(nms[:, i:i + 1], nm1[:, i:i + 1], nsink[:, i % 8:i % 8 + 1], ALU.min)
                    ins.then_inc(*negmax.up)
                if i in (7, 15):
                    dve.drain()
                    t = i // 8
                    nc.vector.tensor_tensor(stmp[:, 8 * t:8 * t + 8], s1[:, S1["sink"]], nms[:, 8 * t:8 * t + 8],
                                            ALU.add).then_inc(*sink_sum.up)
                if i % 8 == 2 and i >= 8:
                    finish(i // 8 - 1)
                if i in ATT_STEPS:
                    v = ATT_STEPS[i]
                    if v > B1_UNITS:
                        half_out(dve, v - 1, 6 + (v - 1) % 2)
                    half_steps(dve, v, 0)
                    half_steps(dve, v, 1)
            dve.drain()
            gate_dve(dve, N1, mod1[:, 16:24], 1.0)
            split_dve(dve, y1_hi, y1_lo, 0, 4, 0)
            for u in range(8, 12):
                conv_lo(dve, u + RING)
            residual(dve, N1.x_new, (unit_used, B1_UNITS))
            factors_dve(dve, N1, mod1[:, 32:40], s1[:, S1["gffn"]], am)
            norm_dve(dve, N1, 2, 0, xs, xn)
            gate_dve(dve, N1, mod1[:, 40:48], 1.0)
            spread_dve(dve, N1, 2, 0, hhi, hlo, mod1[:, 24:32], 0, am)
            route_dve(dve)
            hidden_dve(dve, MOE_GROUPS, B1_UNITS, 0, 0, True)
            residual(dve, N1.x_new, (y_sum, 1))
            conv_lo(dve, B1_UNITS + 3 * MOE_GROUPS - 1 + RING, 0)
            final_norm(dve, 0, xs, N2.x_new)

        def final_norm(dve, k, dst, done):
            dve.wait_ge(*N3.rstd.at(k))
            dve.wait_ge(gf_landed, 16 * (k + 1))
            for t in range(NT):
                ins = nc.vector.scalar_tensor_tensor(dst[:, t], xs[:, t], st[:, 4 + t:5 + t], gfin, ALU.mult, ALU.mult)
            ins.then_inc(*done.up)


        N2 = Norm("n2", 3)
        names = {"q_out": 12, "rope2": 1, "fox_abs": 1, "fox_ln": 1, "fox_log": 1, "cum_mm": 1, "cum_out": 1, "cum_turned": 1,
                 "fox_rows": 1, "tb_mm": 17, "tb_act": 9, "tb_dve": 8, "cb_made": 1, "cb_hi": 1, "cb_lo": 1, 
                 "hid_made": 1, "ck_mm": 1, "ck_out": 1, "cs_mm": 1, "cs_sub": 1, "zeroed": 1, "hid_turned": 1, "hid_act": 1, "oc_out": 1, "sig_done": 3, "cs_exp": 1, "cs_done": 1, "cp_mm": 1,
                 "cp_out": 1, "oc_mm": 1, "s2_mm": 20, "negmax2": 20, "exp2": 20, "p2_turned": 20, "pt2_out": 20, "pv2": 20,
                 "ya_done": 1, "den_ln": 1, "lse_sub": 1, "lse_exp": 1, "m_out": 12, "y2_turned": 7, "y2_hi": 7,
                 "y2_lo": 7, "dil_mm": 1, "br_out": 3, "y2_made": 1}
        B = {n: sig(n, per) for n, per in names.items()}
        PASSES2 = 20
        FILL_BANK = (4, 5, 6, 4, 5)
        ORDER2 = list(range(11, 17)) + list(range(11))
        nm2, den2, rd2, fz, fe, lf, ge, fac = (sm[:, 0:40], sm[:, 40:80], sm[:, 80:120], sm[:, 120:132], sm[:, 132:144],
                                               sm[:, 144:156], sm[:, 156:180], sm[:, 180:256])
        ac = acc[:, :, :].rearrange("p a n -> p (a n)")
        ct, e16, hidc, kcs, vcs, m8, s8, r8, lnd, lmx, lsm = (
            ac[:, 512:768].rearrange("p (t n) -> p t n", t=2), ac[:, 128:256], ac[:, 256:288], ac[:, 320:336],
            ac[0:16, 336:400], ac[:, 400:408], ac[:, 408:416], ac[:, 416:424], ac[:, 424:436], ac[:, 436:440], ac[:, 440:444])
        w8 = [ac[:, 448 + 8 * i:456 + 8 * i] for i in range(3)]
        lw = ac[:, 480:492]
        cb = a2[:, 1024:2048]
        cb_hi, cb_lo = (zr[:, i, 0:4].rearrange("p c n -> p (c n)") for i in range(2))
        hidt = ac[:, 768:896]
        pc2 = qj[0:16, :, C_FQ:C_FQ + 512]
        oc_part = ac[:, 512:1024]
        tbf = tb.rearrange("p b n -> p (b n)")
        nsa_part = [tbf[:, 6 * S:8 * S], tbf[:, 8 * S:10 * S]]
        dil_part = [tbf[:, b * S:b * S + S] for b in (2, 3, 4)]
        G = [qj[:, :, 256 * f:256 * f + 256] for f in range(5)] + [qj[:, :, C_FQ + 256 * f:C_FQ + 256 * f + 256] for f in range(3)]
        G += [s1[:, 512 * f:512 * f + 512].rearrange("p (t n) -> p t n", t=2) for f in range(2)]
        G += [xn[:, :, 768:1024], oc_part.rearrange("p (t n) -> p t n", t=2)]
        ATT_GATES = {3 * (h // 2) + h % 2: (5 + h // 2, h % 2) for h in range(14)}
        FF0, QK0 = LAYER0, LAYER0 + FFN_UNITS
        CM0 = QK0 + 15
        BR0 = QK0 + 26
        CG = [QK0 + 12 + f + (2 if f >= 3 else 0) for f in range(12)]
        WO0, FF1 = BR0 + 3, QK0 + MIX_UNITS

        def pass2(p):
            if p < 8:
                h = p % 4
                r = slice(64 * (h % 2), 64 * (h % 2) + 64)
                k = (T_SW if h % 2 == 0 else T_WS) if p < 4 else (T_WS if h % 2 == 0 else T_SW)
                return tb[r, T_NQ + h // 2], tb[r, k], 0, C_VS if p < 4 else C_VW
            h = p - 8 if p < 14 else p - 14
            r = slice(64 * (h % 2), 64 * (h % 2) + 64)
            if p < 14:
                return tb[r, T_DQ + h // 2], tb[r, T_DK + h // 2], 1 + h // 2, C_DV + 64 * h
            return tb[r, T_FQ + h // 2], tb[r, T_FK + h // 2], 0, C_FV + 64 * h

        def y_slot(first, n):
            return xn[:, :, first:first + 64 * n].rearrange("p t (h n) -> p h t n", h=n)

        def pe_norm2(pe, k, l):
            norm_pe(pe, N2, k, l, xn, 0)
            gate_pe(pe, N2, k, l)
            pe.wait_ge(*N2.lo.at(4 * k + 3, l))
            pe.wait_ge(*N2.row.at(k, l))

        def pe_layer(pe, l):
            E0 = l * (LAYER_UNITS // RING)
            pe_norm2(pe, 0, l)
            hidden_pe(pe, FFN_GROUPS, FF0, E0, l * (2 * FFN_GROUPS) + MOE_GROUPS, False)
            pe_norm2(pe, 1, l)
            for j in range(3):
                project(unit(pe, QK0 + j, E0), hhi, hlo, j).then_inc(unit_used, 1)
            with pe.Fori(0, 3) as i:
                for j in range(3):
                    pe.wait_ge(B["q_out"].sem, l * 12 + i * 3 + (j + 1))
                    project(unit(pe, QK0 + 3 + j, E0 + i), hhi, hlo, j).then_inc(unit_used, 1)
            def gate_unit(f, bank, tile=None):
                ins = project(unit(pe, CG[f], E0), hhi, hlo, bank, range(NT) if tile is None else (tile,))
                if tile != 0:
                    ins.then_inc(unit_used, 1)

            gate_unit(0, 4)
            pe.wait_ge(*B["q_out"].at(11, l))
            for i, b in enumerate(ORDER2):
                if i == 6:
                    gate_unit(1, 5)
                    pe.wait_ge(*B["rope2"].at(0, l))
                if i >= 4:
                    pe.wait_ge(*(B["tb_act"] if i % 2 == 0 else B["tb_dve"]).at(i // 2 - 2, l))
                for t in range(NT):
                    ins = nc.tensor.transpose(PS[:, i % 4, t * P:(t + 1) * P], qj[:, t, T_COLS[b]:T_COLS[b] + P], ident)
                ins.then_inc(*B["tb_mm"].up)
            gate_unit(2, 6)
            pe.wait_ge(*B["tb_dve"].at(7, l))
            pe.wait_ge(*B["fox_log"].at(0, l))
            nc.tensor.matmul(PS[:, 3, 0:6], tri, lf[:, 0:6], start=True, stop=True)
            nc.tensor.matmul(PS[:, 3, 6:12], ones, lf[:, 0:6], start=True, stop=False)
            nc.tensor.matmul(PS[:, 3, 6:12], tri, lf[:, 6:12], start=False, stop=True).then_inc(*B["cum_mm"].up)
            pe.wait_ge(*B["cb_lo"].at(0, l))
            for u in range(2):
                wh, wl = (w.rearrange("p (t n) -> p t n", t=16) for w in unit(pe, CM0 + u, E0))
                for t in range(16):
                    c = slice((16 * u + t) * 32, (16 * u + t) * 32 + 32)
                    ins = mm3(PS[0:32, 7, 0:P], cb_hi[:, c], cb_lo[:, c], wh[:, t], wl[:, t], u + t == 0, u + t == 16)
                ins.then_inc(unit_used, 1)
            pe.wait_ge(*B["m_out"].at(0, l))
            gate_unit(3, 4, 0)
            pe.wait_ge(*B["cum_out"].at(0, l))
            for t in range(NT):
                ins = nc.tensor.transpose(PS[:, 3, (1 + t) * P:(2 + t) * P], ct[:, t], ident)
            ins.then_inc(*B["cum_turned"].up)
            pe.wait_ge(*B["tb_act"].at(8, l))
            pe.wait_ge(*B["hid_act"].at(0, l))
            nc.tensor.transpose(PS[:, 2, 0:P], hidt, ident).then_inc(*B["hid_turned"].up)
            gate_unit(3, 4, 1)
            pe.wait_ge(*B["hid_made"].at(0, l))
            w2 = s2[:, S2["w2"]]
            nc.tensor.matmul(PS[:, 1, 0:16], w2[:, 0:128], hidc[:, 0:16], start=True, stop=True)
            nc.tensor.matmul(PS[0:16, 0, 0:64], hidc[:, 16:32], w2[:, 128:192], start=True, stop=True).then_inc(*B["ck_mm"].up)
            pe.wait_ge(*B["m_out"].at(1, l))
            gate_unit(4, 5, 0)
            pe.wait_ge(*B["ck_out"].at(0, l))
            pe.wait_ge(*B["m_out"].at(2, l))
            for h in range(NSA_H):
                r = slice(64 * (h % 2), 64 * (h % 2) + 64)
                for t in range(NT):
                    o = 128 + 16 * ((h // 2) * 2 + t)
                    ins = nc.tensor.matmul(PS[:, 6 + h % 2, o:o + 16], tb[r, T_NQ + h // 2, t * P:(t + 1) * P], kcs[r, :],
                                           start=True, stop=True)
            ins.then_inc(*B["cs_mm"].up)
            gate_unit(4, 5, 1)
            pe.wait_ge(*B["cs_done"].at(0, l))
            for i in range(8):
                ins = nc.tensor.transpose(PS[0:16, 6 + i // 4, (i % 4) * P:(i % 4 + 1) * P], e16[:, 16 * i:16 * i + 16], ident)
            ins.then_inc(*B["cp_mm"].up)
            pe.wait_ge(*B["cp_out"].at(0, l))
            for i in range(8):
                ins = nc.tensor.matmul(PS[:, 7, 64 * i:64 * i + 64], pc2[:, i // 4, P * (i % 4):P * (i % 4) + P], vcs, start=True, stop=True)
            ins.then_inc(*B["oc_mm"].up)
            pe.wait_ge(mask_in, 32)
            pe.wait_ge(*B["fox_rows"].at(0, l))
            for i in range(PASSES2 + 2):
                if i < PASSES2:
                    q, k, mk, _ = pass2(i)
                    if i >= 2:
                        pe.wait_ge(*B["exp2"].at(i - 2, l))
                    nc.tensor.matmul(PS[:, i % 2], idb[:, :], masks[:, mk], start=True, stop=False, skip_group_check=True)
                    for t in range(NT):
                        o = PS[:, i % 2, 256 * t:256 * t + P * (t + 1)]
                        if i >= 14:
                            nc.tensor.matmul(o, fl[:, i - 14, t * P:(t + 1) * P], fr[:, 0:P * (t + 1)], start=False,
                                             stop=False, skip_group_check=True)
                        ins = nc.tensor.matmul(o, q[:, t * P:(t + 1) * P], k[:, 0:P * (t + 1)], start=False, stop=t == 1,
                                               skip_group_check=True)
                    ins.then_inc(*B["s2_mm"].up)
                if 1 <= i <= PASSES2:
                    p = i - 1
                    pe.wait_ge(*B["exp2"].at(p, l))
                    if p >= 2:
                        pe.wait_ge(*B["pt2_out"].at(p - 2, l))
                    for n, c in enumerate((0, 256, 384)):
                        ins = nc.tensor.transpose(PS[:, 2 + p % 2, n * P:(n + 1) * P], pr2[:, p % 2, c:c + P], ident)
                    ins.then_inc(*B["p2_turned"].up)
                if i >= 2:
                    p = i - 2
                    pe.wait_ge(*B["pt2_out"].at(p, l))
                    if p in (0, 4):
                        pe.wait_ge(*B["m_out"].at(3 + p // 4, l))
                    if p == 12:
                        pe.wait_ge(*B["ya_done"].at(0, l))
                    bank, slot, v = FILL_BANK[p // 4], (p % 4) * 2, pass2(p)[3]
                    for t in range(NT):
                        for c in range(t + 1):
                            ins = nc.tensor.matmul(PS[:, bank, 64 * (slot + t):64 * (slot + t) + 64],
                                                   pt2[:, p % 2, (t + c) * P:(t + c + 1) * P], qj[:, c, v:v + 64],
                                                   start=c == 0, stop=c == t)
                    ins.then_inc(*B["pv2"].up)
                if i in ATT_GATES:
                    f, tile = ATT_GATES[i]
                    if tile == 0:
                        pe.wait_ge(*(B["oc_out"].at(0, l) if f == 5 else B["m_out"].at(f - 1, l)))
                    gate_unit(f, 7, tile)
            pe.wait_ge(*B["y2_made"].at(0, l))
            turn(pe, B["y2_turned"], xn, 0, 6)
            pe.wait_ge(*B["y2_lo"].at(2, l))
            u = unit(pe, BR0, E0)
            for kk in range(2):
                ins = rows_product(u, kk, hhi[:, kk], hlo[:, kk], 4, kk == 0, kk == 1)
            ins.then_inc(unit_used, 1)
            u = unit(pe, BR0 + 1, E0)
            rows_product(u, 0, hhi[:, 2], hlo[:, 2], 0, True, True).then_inc(*B["dil_mm"].up)
            pe.wait_ge(*B["br_out"].at(0, l))
            rows_product(u, 1, hhi[:, 3], hlo[:, 3], 4, True, False).then_inc(unit_used, 1)
            u = unit(pe, BR0 + 2, E0)
            for kk in range(2):
                ins = rows_product(u, kk, hhi[:, 4 + kk], hlo[:, 4 + kk], 4, False, kk == 1)
            ins.then_inc(unit_used, 1)
            pe.wait_ge(*B["br_out"].at(2, l))
            turn(pe, B["y2_turned"], mg, 0, DC)
            pe.wait_ge(*B["y2_lo"].at(6, l))
            for w in range(4):
                u = unit(pe, WO0 + w, E0)
                for kk in range(2):
                    ins = rows_product(u, kk, hhi[:, 2 * w + kk], hlo[:, 2 * w + kk], 4, w + kk == 0, w + kk == 4)
                ins.then_inc(unit_used, 1)
            pe_norm2(pe, 2, l)
            hidden_pe(pe, FFN_GROUPS, FF1, E0, l * (2 * FFN_GROUPS) + MOE_GROUPS + FFN_GROUPS, False)

        def act_norm2(act, k, l):
            norm_act(act, N2, k, l, xs, xn)
            spread_act(act, N2, k, l, hhi, modl[:, 24 * k:24 * k + 8], 0, am)
            gate_act(act, N2, k, l)

        def act_layer(act, l):
            E0 = l * (LAYER_UNITS // RING)
            act.wait_ge(*N2.x_new.at(0, l))
            act_norm2(act, 0, l)
            hidden_act(act, FFN_GROUPS, FF0, E0, l * (2 * FFN_GROUPS) + MOE_GROUPS, False)
            act.wait_ge(*N2.x_new.at(1, l))
            act_norm2(act, 1, l)
            with act.Fori(0, 4) as i:
                for j in range(3):
                    act.wait_ge(unit_used, (E0 + i) * 3 + (QK0 + j + 1))
                    nc.scalar.activation(qj[:, :, bass.ds(i * 768 + j * 256, 256)], PS[:, j].rearrange("p (t n) -> p t n", t=2),
                                         ACT.Copy).then_inc(*B["q_out"].up)
                    conv_hi(act, QK0 + j + RING, E0 + i)

            def gate_out(f, bank, conv=True):
                act.wait_ge(unit_used, E0 * 3 + (CG[f] + 1))
                nc.scalar.activation(G[f], PS[:, bank].rearrange("p (t n) -> p t n", t=2), ACT.Copy).then_inc(*B["m_out"].up)
                if conv:
                    conv_hi(act, CG[f] + RING, E0)

            act.wait_ge(*B["fox_abs"].at(0, l))
            nc.scalar.activation(ge.rearrange("p (t n) -> p t n", t=2), qj[:, :, C_G:C_F], ACT.Exp, scale=-1.0)
            nc.scalar.activation(fe, fe, ACT.Exp, scale=-1.0)
            act.drain()
            nc.scalar.activation(fe, fe, ACT.Ln, bias=1.0).then_inc(*B["fox_ln"].up)
            def turned_out(a, b):
                for i in range(a, b, 2):
                    act.wait_ge(*B["tb_mm"].at(i, l))
                    k = ORDER2[i]
                    nc.scalar.activation(tb[:, k], PS[:, i % 4, 0:256], ACT.Copy,
                                         scale=HD ** -0.5 if k in T_SCALED else 1.0).then_inc(*B["tb_act"].up)

            conv_hi(act, CG[0] + RING, E0)
            turned_out(0, 6)
            conv_hi(act, CG[1] + RING, E0)
            turned_out(6, NTB)
            for f in range(2):
                gate_out(f, 4 + f, False)
            gate_out(2, 6)
            act.wait_ge(*B["cb_made"].at(0, l))
            nc.scalar.activation(cb_hi, cb, ACT.Copy).then_inc(*B["cb_hi"].up)
            conv_hi(act, CM0 + RING, E0)
            conv_hi(act, CM0 + 1 + RING, E0)
            act.wait_ge(unit_used, E0 * 3 + (CM0 + 2))
            nc.scalar.activation(hidt[0:32, :], PS[0:32, 7, 0:P], ACT.Silu).then_inc(*B["hid_act"].up)
            gate_out(3, 4)
            act.wait_ge(*B["cs_sub"].at(0, l))
            nc.scalar.activation(e16, e16, ACT.Exp).then_inc(*B["cs_exp"].up)
            gate_out(4, 5, False)
            act.wait_ge(*B["cp_mm"].at(0, l))
            nc.scalar.activation(pc2, PS[0:16, 6:8], ACT.Copy).then_inc(*B["cp_out"].up)
            conv_hi(act, CG[4] + RING, E0)
            for i in range(PASSES2 + 1):
                if i < PASSES2:
                    act.wait_ge(*B["negmax2"].at(i, l))
                    if i >= 2:
                        act.wait_ge(*B["p2_turned"].at(i - 2, l))
                    for t in range(NT):
                        n = 2 * i + t
                        o = slice(256 * t, 256 * t + P * (t + 1))
                        ins = nc.scalar.activation(pr2[:, i % 2, o], PS[:, i % 2, o], ACT.Exp, bias=nm2[:, n:n + 1],
                                                   accum_out=den2[:, n:n + 1])
                    ins.then_inc(*B["exp2"].up)
                done = ATT_GATES.get(i - 1, (0, 0))
                if done[1]:
                    gate_out(done[0], 7, False)
                if i >= 1:
                    p = i - 1
                    act.wait_ge(*B["p2_turned"].at(p, l))
                    if p >= 2:
                        act.wait_ge(*B["pv2"].at(p - 2, l))
                    nc.scalar.activation(pt2[:, p % 2, 0:384], PS[:, 2 + p % 2, 0:384], ACT.Copy).then_inc(*B["pt2_out"].up)
                if done[1]:
                    conv_hi(act, CG[done[0]] + RING, E0)
            nc.scalar.activation(lnd, den2[:, 16:28], ACT.Ln).then_inc(*B["den_ln"].up)
            act.wait_ge(*B["lse_sub"].at(0, l))
            nc.scalar.activation(lw, lw, ACT.Exp).then_inc(*B["lse_exp"].up)

            for b in range(3):
                for f in range(4 * b, 4 * b + 4):
                    ins = nc.scalar.activation(G[f], G[f], ACT.Sigmoid)
                ins.then_inc(*B["sig_done"].up)
            split_act(act, B["y2_turned"], B["y2_hi"], 0, 3, l)
            for u in range(3):
                conv_hi(act, BR0 + u + RING, E0)
            split_act(act, B["y2_turned"], B["y2_hi"], 3, 4, l)
            for u in range(4):
                conv_hi(act, WO0 + u + RING, E0)
            act.wait_ge(*N2.x_new.at(2, l))
            act_norm2(act, 2, l)
            hidden_act(act, FFN_GROUPS, FF1, E0, l * (2 * FFN_GROUPS) + MOE_GROUPS + FFN_GROUPS, False)

        def pool_layer(pool, l):
            for k in range(3):
                norm_pool(pool, N2, k, l)
                gate_pool(pool, N2, k, l)
                if k == 1:
                    nc.gpsimd.memset(cb, 0.0)
                    nc.gpsimd.memset(fl, 0.0)
                    nc.gpsimd.memset(ct, 0.0)
                    nc.gpsimd.memset(hidt, 0.0)
                    nc.gpsimd.memset(fr, 1.0).then_inc(*B["zeroed"].up)

        def dve_norm2(dve, k, l):
            factors_dve(dve, N2, modl[:, 24 * k + 8:24 * k + 16], s2[:, S2["ng"]][:, 8 * k:8 * k + 8], am)
            gate_dve(dve, N2, modl[:, 24 * k + 16:24 * k + 24], 1.0 if k == 1 else 0.5)
            norm_dve(dve, N2, k, l, xs, xn)
            spread_dve(dve, N2, k, l, hhi, hlo, modl[:, 24 * k:24 * k + 8], 0, am)

        def dve_layer(dve, l):
            E0 = l * (LAYER_UNITS // RING)
            dve.drain()
            nc.vector.tensor_copy(modl[:, :], mod2[:, bass.ds(l * 72, 72)])
            nc.vector.tensor_copy(s2[:, :].unsqueeze(1), s2_all[:, bass.ds(l, 1)])
            dve.drain()
            dve_norm2(dve, 0, l)
            hidden_dve(dve, FFN_GROUPS, FF0, E0, l * (2 * FFN_GROUPS) + MOE_GROUPS, False)
            residual(dve, N2.x_new, (y_sum, l * 2 + 2))
            conv_lo(dve, FF0 + FFN_UNITS - 1 + RING, E0)
            dve_norm2(dve, 1, l)
            with dve.Fori(0, 4) as i:
                for j in range(3):
                    conv_lo(dve, QK0 + j + RING, E0 + i)
            dve.wait_ge(*B["q_out"].at(11, l))
            x = qj[:, :, 0:N_ROT * HD].rearrange("p t (h r) -> p t h r", r=HD)
            c, s_ = (k1[:, K1[n]].rearrange("p (t n) -> p t n", t=2).unsqueeze(2).to_broadcast([P, 2, N_ROT, 8])
                     for n in ("cos2", "sin2"))
            rope(dve, nc.vector, (x[:, :, :, 0:8], x[:, :, :, 8:16]), c, s_, [rt2[:, i] for i in range(4)]).then_inc(*B["rope2"].up)
            fz2 = fz.rearrange("p (t n) -> p t n", t=2)
            nc.vector.tensor_tensor(fz2, qj[:, :, C_F:C_F + 6], mid(s2[:, S2["fb"]], [P, 2, 6]), ALU.add)
            dve.drain()
            nc.vector.tensor_scalar(fe, fz, -1.0, None, ALU.mult)
            dve.drain()
            nc.vector.tensor_tensor(fe, fe, fz, ALU.max).then_inc(*B["fox_abs"].up)
            dve.wait_ge(*B["zeroed"].at(0, l))
            dve.wait_ge(*B["fox_ln"].at(0, l))
            nc.vector.scalar_tensor_tensor(lf, fz, 0.0, fe, ALU.min, ALU.subtract).then_inc(*B["fox_log"].up)
            nc.vector.tensor_scalar(ge, ge, 1.0, None, ALU.add)
            dve.drain()
            nc.vector.reciprocal(ge, ge)
            nc.vector.tensor_copy(fl[0:6], bc(ident[0:6, 0:6], [6, 6, 256]))
            conv_lo(dve, CG[0] + RING, E0)

            def turned_out(a, b):
                for i in range(a, b, 2):
                    dve.wait_ge(*B["tb_mm"].at(i, l))
                    k = ORDER2[i]
                    nc.vector.tensor_scalar(tb[:, k], PS[:, i % 4, 0:256], HD ** -0.5 if k in T_SCALED else 1.0, None,
                                            ALU.mult).then_inc(*B["tb_dve"].up)

            turned_out(1, 7)
            conv_lo(dve, CG[1] + RING, E0)
            turned_out(7, NTB)
            dve.wait_ge(*B["tb_act"].at(8, l))
            cb3 = cb.rearrange("p (t n) -> p t n", n=32)
            kcv = tb[:, T_CV].rearrange("p (n t) -> p t n", t=16)
            for kv in range(2):
                r = slice(64 * kv, 64 * kv + 64)
                for half in range(2):
                    ins = nc.vector.tensor_tensor(cb3[r, 16 * half:16 * half + 16, 16 * kv:16 * kv + 15], kcv[r, :, half:half + 15],
                                                  bc(s2[r, S2["pe"]][:, 16 * half:16 * half + 16], [64, 16, 15]), ALU.add)
            ins.then_inc(*B["cb_made"].up)
            conv_lo(dve, CG[2] + RING, E0)
            dve.wait_ge(*B["cum_mm"].at(0, l))
            cum = PS[:, 3, 0:12].rearrange("p (t n) -> p t n", t=2)
            nc.vector.tensor_scalar(ct[:, :, 0:6], cum, -1.0, None, ALU.mult)
            nc.vector.tensor_copy(ct[:, :, 32:38], cum).then_inc(*B["cum_out"].up)
            dve.wait_ge(*B["cb_hi"].at(0, l))
            nc.vector.tensor_tensor(cb_lo, cb, cb_hi.bitcast(F32), ALU.subtract).then_inc(*B["cb_lo"].up)
            conv_lo(dve, CM0 + RING, E0)
            conv_lo(dve, CM0 + 1 + RING, E0)
            dve.wait_ge(*B["hid_turned"].at(0, l))
            nc.vector.tensor_copy(hidc, PS[:, 2, 0:32]).then_inc(*B["hid_made"].up)
            dve.wait_ge(*B["cum_turned"].at(0, l))
            nc.vector.tensor_copy(fr[0:6], PS[0:6, 3, 128:384])
            nc.vector.tensor_tensor(fl[32:38], mid(PS[32:38, 3, 128:384], [6, 6, 256]), bc(ident[32:38, 32:38], [6, 6, 256]),
                                    ALU.mult).then_inc(*B["fox_rows"].up)
            dve.wait_ge(*B["ck_mm"].at(0, l))
            nc.vector.tensor_copy(kcs, PS[:, 1, 0:16])
            nc.vector.tensor_copy(vcs, PS[0:16, 0, 0:64]).then_inc(*B["ck_out"].up)
            conv_lo(dve, CG[3] + RING, E0)
            dve.wait_ge(*B["cs_mm"].at(0, l))
            for b in range(2):
                nc.vector.tensor_tensor(e16[:, 64 * b:64 * b + 64].rearrange("p (a n) -> p a n", a=2),
                                        PS[:, 6 + b, 128:192].rearrange("p (a n) -> p a n", a=2),
                                        mid(k1[:, K1["cmpm"]], [P, 2, 32]), ALU.add)
            dve.drain()
            e8 = e16.rearrange("p (i n) -> p i n", i=8)
            nc.vector.tensor_reduce(m8, e8, AX.X, ALU.max)
            dve.drain()
            nc.vector.tensor_tensor(e8, e8, bc(m8, [P, 8, 16]), ALU.subtract).then_inc(*B["cs_sub"].up)
            dve.wait_ge(*B["cs_exp"].at(0, l))
            e4 = e16.rearrange("p (i n) -> p i n", i=4)
            nc.vector.tensor_tensor(e4, e4, mid(k1[:, K1["cmp01"]], [P, 4, 32]), ALU.mult).then_inc(*B["cs_done"].up)
            dve.drain()
            nc.vector.tensor_reduce(s8, e8, AX.X, ALU.add)
            dve.drain()
            s42 = s8.rearrange("p (h t) -> p h t", t=2)
            nc.vector.tensor_tensor(s42, s42, mid(k1[:, K1["cmpno"]], [P, 4, 2]), ALU.add)
            dve.drain()
            nc.vector.reciprocal(r8, s8)
            dve.drain()
            gv = ge.rearrange("p (t a b k) -> p k b a t", t=2, a=2, b=2)
            w3 = w8[2].rearrange("p (b a t) -> p b a t", b=2, a=2)
            r83 = r8.rearrange("p (b a t) -> p b a t", b=2, a=2)
            nc.vector.tensor_tensor(w3, r83, gv[:, 0], ALU.mult)
            conv_lo(dve, CG[4] + RING, E0)
            dve.drain()
            dve.wait_ge(*B["oc_mm"].at(0, l))
            nc.vector.tensor_tensor(oc_part.rearrange("p (i n) -> p i n", i=8), PS[:, 7].rearrange("p (i n) -> p i n", i=8),
                                    bc(w8[2], [P, 8, 64]), ALU.mult).then_inc(*B["oc_out"].up)

            def nsa_out():
                dve.wait_ge(*B["pv2"].at(7, l))
                nc.vector.reciprocal(rd2[:, 0:16], den2[:, 0:16])
                dve.drain()
                gk = ge.rearrange("p (t h k) -> p k h t", t=2, h=4)
                for b in range(2):
                    nc.vector.tensor_tensor(w8[b].rearrange("p (h t) -> p h t", t=2),
                                            rd2[:, 8 * b:8 * b + 8].rearrange("p (h t) -> p h t", t=2), gk[:, 1 + b], ALU.mult)
                dve.drain()
                parts = nsa_part + [oc_part]
                for b, bank in enumerate((4, 5)):
                    ins = nc.vector.tensor_tensor(parts[b].rearrange("p (i n) -> p i n", i=8),
                                                  PS[:, bank].rearrange("p (i n) -> p i n", i=8), bc(w8[b], [P, 8, 64]), ALU.mult)
                ins.then_inc(*B["ya_done"].up)
                dve.drain()
                nc.vector.tensor_tensor(parts[0], parts[0], parts[1], ALU.add)
                dve.drain()
                for b in range(2):
                    nc.vector.tensor_tensor(
                        xn[:, :, 0:256].rearrange("p t (a b n) -> p b a t n", a=2, b=2)[:, b],
                        parts[0].rearrange("p (a b t n) -> p b a t n", a=2, b=2, t=2)[:, b],
                        parts[2].rearrange("p (b a t n) -> p b a t n", a=2, b=2, t=2)[:, b], ALU.add)

            for i in range(PASSES2):
                dve.wait_ge(*B["s2_mm"].at(i, l))
                nc.vector.tensor_reduce(nm2[:, 2 * i:2 * i + 2], PS[:, i % 2].rearrange("p (t n) -> p t n", t=2), AX.X, ALU.max,
                                        negate=True).then_inc(*B["negmax2"].up)
                if i == 12:
                    nsa_out()
                done = ATT_GATES.get(i - 1, (0, 0))
                if done[1]:
                    conv_lo(dve, CG[done[0]] + RING, E0)
            conv_lo(dve, CG[11] + RING, E0)
            dve.wait_ge(*B["den_ln"].at(0, l))
            lw3 = lw.rearrange("p (g x) -> p g x", g=3)
            nc.vector.tensor_tensor(lw, lnd, nm2[:, 16:28], ALU.subtract)
            dve.drain()
            nc.vector.tensor_reduce(lmx, lw.rearrange("p (g x) -> p x g", g=3), AX.X, ALU.max)
            dve.drain()
            nc.vector.tensor_tensor(lw3, lw3, mid(lmx, [P, 3, 4]), ALU.subtract).then_inc(*B["lse_sub"].up)
            dve.wait_ge(*B["lse_exp"].at(0, l))
            nc.vector.tensor_reduce(lsm, lw.rearrange("p (g x) -> p x g", g=3), AX.X, ALU.add)
            dve.drain()
            f12 = fac[:, 0:12]
            nc.vector.tensor_tensor(f12.rearrange("p (g x) -> p g x", g=3), den2[:, 16:28].rearrange("p (g x) -> p g x", g=3),
                                    mid(lsm, [P, 3, 4]), ALU.mult)
            dve.drain()
            nc.vector.reciprocal(f12, f12)
            nc.vector.reciprocal(rd2[:, 28:40], den2[:, 28:40])
            dve.drain()
            nc.vector.tensor_tensor(f12, f12, lw, ALU.mult)
            dve.drain()
            dve.wait_ge(*B["pv2"].at(19, l))
            dp = dil_part
            for g in range(3):
                bank, o = (6, 256 * g) if g < 2 else (4, 0)
                nc.vector.tensor_tensor(dp[g].rearrange("p (x n) -> p x n", x=4),
                                        PS[:, bank, o:o + 256].rearrange("p (x n) -> p x n", x=4),
                                        bc(f12[:, 4 * g:4 * g + 4], [P, 4, 64]), ALU.mult)
            for h0_, n, bank, o in ((0, 2, 4, 256), (2, 4, 5, 0)):
                nc.vector.tensor_tensor(y_slot(384 + 64 * h0_, n),
                                        PS[:, bank, o:o + 128 * n].rearrange("p (h t n) -> p h t n", h=n, t=2),
                                        rd2[:, 28 + 2 * h0_:28 + 2 * h0_ + 2 * n].rearrange("p (h t) -> p h t", t=2)
                                        .unsqueeze(3).to_broadcast([P, n, 2, 64]), ALU.mult)
            dve.drain()
            nc.vector.tensor_tensor(dp[0], dp[0], dp[1], ALU.add)
            dve.drain()
            nc.vector.tensor_tensor(y_slot(256, 2), dp[0].rearrange("p (h t n) -> p h t n", h=2, t=2),
                                    dp[2].rearrange("p (h t n) -> p h t n", h=2, t=2), ALU.add).then_inc(*B["y2_made"].up)
            split_dve(dve, B["y2_hi"], B["y2_lo"], 0, 3, l)

            def branch(b, bank, dst):
                dve.wait_ge(*B["sig_done"].at(b, l))
                for j in range(4):
                    cols = slice(256 * (j % 2), 256 * (j % 2) + 256)
                    ins = nc.vector.tensor_tensor(dst[:, :, 256 * j:256 * j + 256], PS[:, bank + j // 2:bank + 4:2, cols],
                                                  G[4 * b + j], ALU.mult)
                if b:
                    dve.drain()
                    ins = nc.vector.tensor_tensor(mg, mg, dst, ALU.add)
                ins.then_inc(*B["br_out"].up)

            dve.wait_ge(unit_used, E0 * 3 + (BR0 + 1))
            branch(0, 4, mg)
            conv_lo(dve, BR0 + RING, E0)
            dve.wait_ge(*B["dil_mm"].at(0, l))
            branch(1, 0, mt2[0])
            conv_lo(dve, BR0 + 1 + RING, E0)
            dve.wait_ge(unit_used, E0 * 3 + (BR0 + 3))
            branch(2, 4, mt2[1])
            conv_lo(dve, BR0 + 2 + RING, E0)
            split_dve(dve, B["y2_hi"], B["y2_lo"], 3, 4, l)
            for u in range(4):
                conv_lo(dve, WO0 + u + RING, E0)
            residual(dve, N2.x_new, (unit_used, E0 * 3 + (WO0 + 4)))
            dve_norm2(dve, 2, l)
            hidden_dve(dve, FFN_GROUPS, FF1, E0, l * (2 * FFN_GROUPS) + MOE_GROUPS + FFN_GROUPS, False)
            residual(dve, N2.x_new, (y_sum, l * 2 + 3))
            conv_lo(dve, FF1 + FFN_UNITS - 1 + RING, E0)

        block = ctx.enter_context(nc.Block())

        @block.sync
        def _(sp):
            sp.dma_start(s1[:, :], s1_in).then_inc(small_in, 16)
            sp.dma_start(k1[:, :], k1_in).then_inc(small_in, 16)
            sp.dma_start(xs[:, :, :], x_in.rearrange("(t p) n -> p t n", p=P)).then_inc(x_landed, 16)
            sp.dma_start(xc_tok, ctx_in.rearrange("(t p) n -> p t n", p=P)).then_inc(x_landed, 16)
            for v in range(PE_HALVES):
                load_half(sp, v)
            sp.dma_start(masks[:, :, :], masks_in[0]).then_inc(mask_in, 16)
            for u in range(RING):
                load(sp, u, first=True)
            for v in range(PE_HALVES, EARLY_HALVES):
                if v < B1_UNITS:
                    load(sp, v - PE_HALVES + RING)
                load_half(sp, v)
            for u in range(B1_UNITS - 1, B1_UNITS + RING + 2):
                load(sp, u)
            sp.dma_start(masks[:, :, :], masks_in[1]).then_inc(mask_in, 16)
            sp.dma_start(gfin, gf_in[0:1, :].to_broadcast([P, D])).then_inc(gf_landed, 16)
            sp.dma_start(s2_all[:, :, :], s2_in.rearrange("l p n -> p l n")).then_inc(s2_landed, 16)

            def body(g, e):
                c = at_gate(B1_UNITS, g)
                load(sp, c + RING, e * 2)
                load_half(sp, EARLY_HALVES - 1 + g, e)
                load(sp, c + 1 + RING, e * 2)
                load(sp, c + 2 + RING, e * 2)

            hidden_loop(sp, MOE_GROUPS, body)
            load(sp, LAYER0 + RING - 1)
            with sp.Fori(0, LAYERS * LAYER_UNITS // RING) as e:
                for j in range(RING):
                    load(sp, LAYER0 + RING + j, e)
            sp.dma_start(gfin, gf_in[1:2, :].to_broadcast([P, D])).then_inc(gf_landed, 16)
            sp.wait_ge(*N3.x_new.at(0))
            sp.dma_start(out.rearrange("(t p) n -> p t n", p=P), ytmp).then_inc(out_landed, 16)
            sp.wait_ge(out_landed, 16)

        @block.tensor
        def _(pe):
            pe_block1(pe)
            with pe.Fori(0, LAYERS) as l:
                pe_layer(pe, l)

        @block.scalar
        def _(act):
            act_block1(act)
            with act.Fori(0, LAYERS) as l:
                act_layer(act, l)
            act.wait_ge(*N2.x_new.at(0, LAYERS))
            norm_stats(act, N3)

        @block.vector
        def _(dve):
            dve_block1(dve)
            dve.wait_ge(s2_landed, 16)
            with dve.Fori(0, LAYERS) as l:
                dve_layer(dve, l)
            final_norm(dve, 1, ytmp, N3.x_new)

        @block.gpsimd
        def _(pool):
            pool_block1(pool)
            with pool.Fori(0, LAYERS) as l:
                pool_layer(pool, l)
            norm_pool(pool, N3, 1, 0)


def constants():
    k = np.zeros((P, K1_W), np.float32)
    k[:, K1["id"]] = np.eye(P)
    k[:, K1["ones"]] = 1.0
    k[:, K1["tri"]] = np.triu(np.ones((P, P)))
    tok = np.arange(S).reshape(NT, P)
    for n, name in ((16, "A"), (8, "C")):
        inv = (np.float32(10000.0) ** (-np.arange(n, dtype=np.float32) / np.float32(n))).astype(np.float32)
        pos = np.stack([tok // 64, tok % 64], -1).astype(np.float32)
        ang = (pos[..., None] * inv).transpose(1, 0, 2, 3).reshape(P, -1)
        k[:, K1["cos" + name]], k[:, K1["sin" + name]] = np.cos(ang), np.sin(ang)
    inv = (np.float32(500000.0) ** (-np.arange(0, ROPE2, 2, dtype=np.float32) / np.float32(ROPE2))).astype(np.float32)
    ang = (tok.astype(np.float32)[..., None] * inv).transpose(1, 0, 2).reshape(P, -1)
    k[:, K1["cos2"]], k[:, K1["sin2"]] = np.cos(ang), np.sin(ang)
    k[:, K1["code"]][:, 0:4] = np.arange(4, 0, -1)
    k[:, K1["half"]] = -0.5
    k[:, K1["eps"]] = EPS
    end = np.arange(16) * CMP_STRIDE + CMP_LEN - 1
    ok = (end[None, None, :] <= tok[:, :, None]) & (np.arange(16) < N_CMP)
    k[:, K1["cmpm"]] = np.where(ok, 0.0, NEG).transpose(1, 0, 2).reshape(P, 32)
    k[:, K1["cmp01"]] = ok.transpose(1, 0, 2).reshape(P, 32)
    k[:, K1["cmpno"]] = (~ok.any(-1)).T
    m = np.zeros((2, 4, P, 512), np.float32)
    key = np.arange(S)
    for t in range(NT):
        q = tok[t][:, None]
        m[0, t, :, 256:] = np.where(np.abs(key - q) <= 128, 0.0, NEG)
        d = q - key
        m[1, 0, :, 256 * t:256 * t + 256] = np.where(d >= 0, 0.0, NEG)
        for g, (window, step) in enumerate(PATTERNS):
            m[1, 1 + g, :, 256 * t:256 * t + 256] = np.where((d >= 0) & (d % step == 0) & (d <= window), 0.0, NEG)
    return k, m.transpose(0, 2, 1, 3)


def wide(w):
    return w.reshape(DC, P, -1, 256).transpose(2, 1, 0, 3).reshape(-1, P, UNIT)


def tall(w):
    return w.reshape(-1, 2, P, D).transpose(0, 2, 1, 3).reshape(-1, P, UNIT)


def hidden_order(gate, up, down):
    n = len(gate)
    seq = [gate[0], up[0]]
    for g in range(1, n):
        seq += [gate[g], up[g], down[g - 1]]
    return seq + [down[n - 1]]


def halves(w):
    return w.reshape(2, 4, P, -1, 512).transpose(3, 0, 2, 1, 4).reshape(-1, P, UNIT)


def cols8(v):
    return v.reshape(-1, P).T


def everywhere(v):
    return np.broadcast_to(v.reshape(1, -1), (P, v.size))


def kernel(**inputs):
    import concourse.bacc as bacc
    from concourse.bass_utils import run_bass_kernel_spmd
    import ml_dtypes

    a = {k: np.asarray(v) for k, v in inputs.items()}
    w_in = a["w_in"][0]
    aq_cols = np.concatenate([np.arange(64 * h, 64 * h + 64) for h in A_ORDER])
    starts = [OFF_AK, OFF_CK, OFF_CV, None, None, OFF_CQ, OFF_BU, OFF_BV]
    seq = []
    for i, o in enumerate(starts):
        c = np.arange(o, o + 256) if o is not None else aq_cols[256 * (i - 3):256 * (i - 3) + 256]
        seq.append(wide(w_in[:, c])[0])
    w_out = np.concatenate([a["w_out"][0][aq_cols], a["w_out"][0][512:]])
    seq += list(tall(w_out))
    gate, up, down = [], [], []
    for e in range(NE):
        gate += list(wide(a["w_gate"][0, e]))
        up += list(wide(a["w_up"][0, e]))
        down += list(tall(a["w_down"][0, e]))
    seq += hidden_order(gate, up, down)
    nq, nkv, dq = 256, 256, 652
    fq = dq + 3 * 384
    kv = lambda i: np.arange(nkv + 64 * i, nkv + 64 * i + 64)
    order = np.concatenate([np.arange(dq, dq + 768), np.arange(0, nq), kv(2), kv(4), kv(2), kv(0), kv(1), kv(3), kv(5),
                            np.arange(fq, fq + 1152), np.arange(dq + 768, dq + 1152), np.arange(640, 652),
                            np.arange(fq + 1152, fq + 1158)])
    for l in range(LAYERS):
        ffn = []
        for f in range(2):
            w, wo = a["ffn_w_in_2"][l, f], a["ffn_w_out_2"][l, f]
            ffn.append(hidden_order(list(wide(w[:, :FF])), list(wide(w[:, FF:])), list(tall(wo))))
        m = a["mix_w_in_2"][l]
        qkv = np.zeros((D, QKV), np.float32)
        qkv[:, :len(order)] = m[:, order]
        w1 = a["nsa_cmp_w1_2"][l].reshape(2, 32, 64, 128).transpose(0, 2, 1, 3).reshape(P, 32 * 128)
        branches = np.concatenate([a["br_w_nsa_2"][l], a["br_w_dil_2"][l], a["br_w_fox_2"][l]])
        gates = list(wide(m[:, fq + 1158:]))
        seq += ffn[0] + list(wide(qkv)) + gates[:3] + [w1[:, :UNIT], w1[:, UNIT:]] + gates[3:]
        seq += list(tall(branches)) + list(tall(a["mix_w_out_2"][l])) + ffn[1]
    seq += [np.zeros((P, UNIT), np.float32)] * RING
    assert len(seq) == N_UNITS
    stream = np.stack(seq)
    ada = np.concatenate([halves(a["w_ada"][0])] + [halves(a["ada_w_2"][l]) for l in range(LAYERS)])
    s1 = np.zeros((P, S1_W), np.float32)
    put = lambda name, v: s1.__setitem__((slice(None), S1[name]), v)
    put("c", cols8(a["c"][0]))
    put("cc", cols8(a["c_ctx"]))
    put("c2", cols8(a["c_2"][0]))
    put("gmix", cols8(a["g_mix"][0]))
    put("gffn", cols8(a["g_ffn"][0]))
    put("bada", np.concatenate([cols8(a["b_ada"][0])] + [cols8(a["ada_b_2"][l]) for l in range(LAYERS)], 1))
    wr = np.concatenate([a["w_rg"][0], a["w_re"][0]], 1)
    put("wr", wr.reshape(DC, P, 20).transpose(1, 0, 2).reshape(P, 160))
    put("br", everywhere(np.concatenate([a["b_rg"][0], a["b_re"][0]])))
    put("sink", everywhere(a["sink"][0][A_ORDER]))
    put("lam", everywhere(np.concatenate([a[n][0] for n in ("lam_q1", "lam_k1", "lam_q2", "lam_k2")])))
    put("gtok", everywhere(a["g_tok"][0]))
    put("gsub", everywhere(a["g_sub"][0]))
    put("ws", a["ws_tok"][0].transpose(2, 0, 1).reshape(P, 512))
    put("bs", a["bs_tok"][0].T)
    s2 = np.zeros((LAYERS, P, S2_W), np.float32)
    for l in range(LAYERS):
        s2[l][:, S2["pe"]] = a["nsa_cmp_pe_2"][l].transpose(0, 2, 1).reshape(P, 32)
        w2 = a["nsa_cmp_w2_2"][l]
        s2[l][:, S2["w2"]] = np.concatenate([w2[0], w2[0], w2[1]], 1)
        s2[l][:, S2["ng"]] = np.concatenate([cols8(a["norm_g_2"][l, k]) for k in range(3)], 1)
        s2[l][:, S2["fb"]] = everywhere(a["fox_f_bias_2"][l])
    k1, masks = constants()
    arrays = {"stream": stream, "ada": ada, "x": a["x"][0], "ctx": a["ctx"][0], "small1": s1, "small2": s2, "consts": k1,
              "masks": masks.astype(ml_dtypes.bfloat16), "gfinal": np.stack([a["g_final"], a["final_norm_g_2"]])}
    arrays = {f"in_{n}": np.ascontiguousarray(v) for n, v in arrays.items()}
    nc = bacc.Bacc("TRN2", target_bir_lowering=False, num_devices=1)
    args = [nc.dram_tensor(n, v.shape, mybir.dt.from_np(v.dtype), kind="ExternalInput").ap() for n, v in arrays.items()]
    out = nc.dram_tensor("y_out", (S, D), F32, kind="ExternalOutput").ap()
    bass_network(nc, *args, out)
    r = run_bass_kernel_spmd(nc, [arrays], core_ids=[0])
    return r.results[0]["y_out"].reshape(1, S, D)
```

```python
from contextlib import ExitStack

import numpy as np
import concourse.bass as bass
from concourse import mybir

F32 = mybir.dt.float32
F32R = mybir.dt.float32r
BF16 = mybir.dt.bfloat16
ACT = mybir.ActivationFunctionType
ALU = mybir.AluOpType
AX = mybir.AxisListType

P = 128
S = 256
NT = S // P
D = 1024
DC = D // P
UNIT = 2048
RING = 3
GW = 256
EPS = 1e-6
NEG = -1e30

A_Q, A_KV, A_D = 8, 2, 64
B_G, B_D = 4, 64
C_H, C_Q, C_V = 4, 32, 64
OFF_AQ, OFF_AK, OFF_AV, OFF_BU, OFF_BV, OFF_CQ, OFF_CK, OFF_CV, D_IN = 0, 512, 640, 768, 1024, 1280, 1536, 1792, 2048
LAM_INIT = 0.8 - 0.6
MG, MPG = 4, 4
NE = MG * MPG
DE = 512
MOE_GROUPS = NE * DE // GW
A_ORDER = [h for i in range(4) for h in (i, i + 4)]

LAYERS = 2
FF = 2816
FFN_GROUPS = FF // GW
NSA_H, DIL_H, FOX_H, HD = 4, 6, 6, 64
CMP_LEN, CMP_STRIDE, CMP_HID = 32, 16, 128
N_CMP = (S - CMP_LEN) // CMP_STRIDE + 1
ROPE2 = 16
PATTERNS = ((128, 1), (512, 4), (2048, 16))
QKV = 3072
C_DQ, C_DK, C_NQ, C_KS, C_KW, C_KS2, C_KC = 0, 384, 768, 1024, 1088, 1152, 1216
C_VC, C_VS, C_VW, C_FQ, C_FK, C_FV, C_DV, C_G, C_F = 1280, 1344, 1408, 1472, 1856, 2240, 2624, 3008, 3020
N_ROT = 20
T_COLS = ([C_DQ + 128 * i for i in range(3)] + [C_DK + 128 * i for i in range(3)] + [C_NQ, C_NQ + 128]
          + [C_KS, C_KW, C_KC] + [C_FQ + 128 * i for i in range(3)] + [C_FK + 128 * i for i in range(3)])
T_DQ, T_DK, T_NQ, T_SW, T_WS, T_CV, T_FQ, T_FK = 0, 3, 6, 8, 9, 10, 11, 14
T_SCALED = {0, 1, 2, 6, 7, 11, 12, 13}
NTB = len(T_COLS)

B1_UNITS = 12
MOE_UNITS = 3 * MOE_GROUPS
FFN_UNITS = 3 * FFN_GROUPS
MIX_UNITS = QKV // 256 + 2 + 3 * D // 256 + 3 + 4
LAYER_UNITS = 2 * FFN_UNITS + MIX_UNITS
LAYER0 = B1_UNITS + MOE_UNITS
N_UNITS = LAYER0 + LAYERS * LAYER_UNITS + RING
assert MIX_UNITS % RING == 0 and LAYER_UNITS % RING == 0 and LAYER0 % RING == 0
B1_HALVES, B2_HALVES = 12, LAYERS * 18
N_HALVES = B1_HALVES + B2_HALVES
PE_HALVES = 4
EARLY_HALVES = N_HALVES - (MOE_GROUPS - 1)


def columns(fields):
    at, n = {}, 0
    for name, width in fields:
        at[name] = slice(n, n + width)
        n += width
    return at, n


S1, S1_W = columns([("c", 8), ("cc", 8), ("c2", 8), ("gmix", 8), ("gffn", 8), ("bada", 48 + 72 * LAYERS), ("wr", 160), ("br", 20),
                    ("sink", 8), ("lam", 128), ("gtok", 256), ("gsub", 64), ("ws", 512), ("bs", 4)])
S2, S2_W = columns([("pe", 32), ("w2", 192), ("ng", 24), ("fb", 6)])
K1, K1_W = columns([("id", 128), ("ones", 128), ("tri", 128), ("cosA", 64), ("sinA", 64), ("cosC", 32), ("sinC", 32),
                    ("cos2", 16), ("sin2", 16), ("code", 20), ("cmpm", 32), ("cmp01", 32), ("cmpno", 2), ("half", 2), ("eps", 2)])


class Signal:

    def __init__(self, sem, per=1):
        self.sem, self.per = sem, per
        self.up = (sem, 1)

    def at(self, k=0, layer=0):
        return self.sem, layer * self.per + (k + 1)


def bass_network(nc, W, AD, x_in, ctx_in, s1_in, s2_in, k1_in, masks_in, gf_in, out):
    with ExitStack() as ctx:
        def sb(name, shape, dt=F32):
            return ctx.enter_context(nc.sbuf_tensor(name, shape, dt))

        def sem(name):
            return ctx.enter_context(nc.semaphore(name))

        def sig(name, per=1):
            return Signal(sem(name), per)

        raw = sb("raw", [P, RING, UNIT])
        whi = sb("whi", [P, RING, UNIT], F32R)
        wlo = sb("wlo", [P, RING, UNIT], F32R)
        ada = sb("ada", [P, 2, UNIT])
        acc = sb("acc", [P, 2, 512])
        xs = sb("xs", [P, NT, D])
        xn = sb("xn", [P, NT, D])
        hhi = sb("hhi", [P, DC, S], F32R)
        hlo = sb("hlo", [P, DC, S], F32R)
        zr = sb("zr", [P, 2, DC, S], F32R)
        row = sb("row", [P, D])
        s1 = sb("s1", [P, S1_W])
        s2_all = sb("s2_all", [P, LAYERS, S2_W])
        s2 = sb("s2", [P, S2_W])
        k1 = sb("k1", [P, K1_W])
        masks = sb("masks", [P, 4, 512], BF16)
        idb = sb("idb", [P, P], BF16)
        zb = sb("zb", [P, 512], BF16)
        mod1 = sb("mod1", [P, 4 * B1_HALVES])
        modc = sb("modc", [P, 16])
        mod2 = sb("mod2", [P, 4 * B2_HALVES])
        modl = sb("modl", [P, 72])
        am = sb("am", [P, 8])
        am2 = sb("am2", [P, 8])
        gcol = sb("gcol", [P, 8])
        st = sb("st", [P, 16])
        rh = sb("rh", [P, 8, 20], F32R)
        rl = sb("rl", [P, 8, 20], F32R)
        sm = sb("sm", [P, 256])
        cs = sb("cs", [P, 24])
        Z = sb("Z", [P, 10752])
        PS = ctx.enter_context(nc.psum_tensor("PS", [P, 8, 512], F32))

        ident, ones, tri = k1[:, K1["id"]], k1[:, K1["ones"]], k1[:, K1["tri"]]

        def z(a, n):
            return Z[:, a:a + n]

        ntmp = z(0, 1024).rearrange("p (b n) -> p b n", b=2)
        diag = z(1024, 1024).rearrange("p (c n) -> p c n", c=8)
        gfin = z(2048, 1024)
        ytmp = z(8704, 2048).rearrange("p (t n) -> p t n", t=2)
        hs = z(3072, 512).rearrange("p (c n) -> p c n", c=2)
        hg = z(3584, 512).rearrange("p (c n) -> p c n", c=2)
        hf = z(9216, 1024).rearrange("p (b c n) -> p b c n", b=2, c=2)
        gb = z(4096, 4096)
        hid_hi = zr[:, 0, :, :].rearrange("p (b c) n -> p b c n", b=4)
        hid_lo = zr[:, 1, :, :].rearrange("p (b c) n -> p b c n", b=4)
        pj = z(0, 4096).rearrange("p (t n) -> p t n", t=2)
        pc = z(4096, 1536).rearrange("p (t n) -> p t n", t=2)
        aq = z(5632, 1024).rearrange("p (b n) -> p b n", b=4)
        ak = z(6656, 512)
        cq = z(7168, 512).rearrange("p (b n) -> p b n", b=2)
        ck = z(7680, 1024).rearrange("p (b n) -> p b n", b=2)
        pr = z(8704, 1024).rearrange("p (b n) -> p b n", b=2)
        pt = z(9728, 1024).rearrange("p (b n) -> p b n", b=2)
        arow = z(0, 2048)
        qj = z(0, 2 * QKV).rearrange("p (t n) -> p t n", t=2)
        tb = z(6144, NTB * S).rearrange("p (b n) -> p b n", b=NTB)
        mg = z(6144, 2048).rearrange("p (t n) -> p t n", t=2)
        a2 = ada[:, :, :].rearrange("p r n -> p (r n)")
        pr2 = a2[:, 0:1024].rearrange("p (b n) -> p b n", b=2)
        pt2 = a2[:, 1024:2048].rearrange("p (b n) -> p b n", b=2)
        rt2 = xn[:, :, :].rearrange("p t n -> p (t n)")[:, 0:4 * 2 * N_ROT * 8].rearrange("p (k t h n) -> p k t h n", k=4, t=2, h=N_ROT)
        fl, fr = a2[:, 2048:2048 + 1536].rearrange("p (h n) -> p h n", h=6), a2[:, 3584:3840]
        mt2 = [a2[:, 2048 * i:2048 * i + 2048].rearrange("p (t n) -> p t n", t=2) for i in range(2)]

        landed = [sem(f"unit_landed{i}") for i in range(RING)]
        hi_ready, lo_ready, unit_used = sem("hi_ready"), sem("lo_ready"), sem("unit_used")
        ada_landed = [sem("ada_landed0"), sem("ada_landed1")]
        ada_used, ada_used_pe = sem("ada_used"), sem("ada_used_pe")
        acc_step = sem("acc_step")
        ada_sum, ada_out, ada_rows_out, ada_cols, mod_ready = (
            sig(n) for n in ("ada_sum", "ada_out", "ada_rows_out", "ada_cols", "mod_ready"))
        small_in, mask_in, x_landed, s2_landed, gf_landed, out_landed = (
            sem(n) for n in ("small_in", "mask_in", "x_landed", "s2_landed", "gf_landed", "out_landed"))
        const_made = sig("const_made")
        silu_done, gated, h_made, hhi_done, hlo_done, y_sum = (
            sem(n) for n in ("silu_done", "gated", "h_made", "hhi_done", "hlo_done", "y_sum"))

        def load(sp, c, e=0, first=False):
            if not first:
                sp.wait_ge(lo_ready, e * 3 + (c - RING + 1))
            u = e * 3 + c
            src = W[c] if isinstance(e, int) and e == 0 else W[bass.ds(u, 1)].rearrange("o p n -> p (o n)")
            sp.dma_start(raw[:, c % RING], src).then_inc(landed[c % RING], 16)

        def conv_hi(act, c, e=0):
            s = c % RING
            act.wait_ge(landed[s], e * 16 + 16 * (c // RING + 1))
            if not (isinstance(e, int) and c + 3 * e < RING):
                act.wait_ge(unit_used, e * 3 + (c - RING + 1))
            nc.scalar.activation(whi[:, s], raw[:, s], ACT.Copy).then_inc(hi_ready, 1)

        def conv_lo(dve, c, e=0):
            s = c % RING
            dve.wait_ge(hi_ready, e * 3 + (c + 1))
            nc.vector.tensor_tensor(wlo[:, s], raw[:, s], whi[:, s].bitcast(F32), ALU.subtract).then_inc(lo_ready, 1)

        def unit(pe, c, e=0):
            pe.wait_ge(lo_ready, e * 3 + (c + 1))
            return whi[:, c % RING], wlo[:, c % RING]

        def load_half(sp, v, e=0):
            for i in range(2):
                if v > PE_HALVES:
                    sp.wait_ge(ada_used, e * 4 + (2 * (v - 1 - PE_HALVES) + i + 1))
                elif v > 0:
                    sp.wait_ge(ada_used_pe, 2 * (v - 1) + i + 1)
                src = AD[2 * v + i] if isinstance(e, int) else AD[bass.ds(e * 4 + (2 * v + i), 1)].rearrange(
                    "o p n -> p (o n)")
                sp.dma_start(ada[:, i], src).then_inc(ada_landed[i], 16)

        def half_step(dve, v, n, e=0):
            vv, i, k = v - PE_HALVES, n // 4, n % 4
            cond = 0 if v < B1_HALVES else 16
            if k == 0:
                dve.wait_ge(ada_landed[i], e * 32 + 16 * (v + 1))
            w, c, a = ada[:, i, 512 * k:512 * k + 512], cs[:, cond + n:cond + n + 1], acc[:, v % 2]
            if n == 0:
                if vv >= 2:
                    dve.wait_ge(ada_sum.sem, e * 2 + (vv - 1))
                ins = nc.vector.tensor_scalar(a, w, c, None, ALU.mult)
            else:
                if n == 4:
                    dve.wait_ge(ada_used, e * 4 + (2 * vv + 1))
                else:
                    dve.wait_ge(acc_step, e * 12 + (6 * vv + (n if n < 4 else n - 1)))
                ins = nc.vector.scalar_tensor_tensor(a, w, c, a, ALU.mult, ALU.add)
            ins.then_inc(ada_used if k == 3 else acc_step, 1)

        def half_steps(dve, v, i, e=0):
            for n in range(4 * i, 4 * i + 4):
                half_step(dve, v, n, e)

        def half_sum(pe, v, bank, e=0):
            vv = v - PE_HALVES
            pe.wait_ge(ada_used, e * 4 + (2 * vv + 2))
            if vv >= 2:
                pe.wait_ge(ada_out.sem, e * 2 + (vv - 1))
            for c in range(4):
                ins = nc.tensor.matmul(PS[:, bank, c:c + 1], acc[:, v % 2, c * P:(c + 1) * P], ones[:, 0:1],
                                       start=True, stop=True)
            ins.then_inc(*ada_sum.up)

        def half_out(dve, v, bank, e=0):
            dve.wait_ge(ada_sum.sem, e * 2 + (v - PE_HALVES + 1))
            b0 = S1["bada"].start
            if isinstance(e, int):
                dst = mod1[:, 4 * v:4 * v + 4] if v < B1_HALVES else mod2[:, 4 * (v - B1_HALVES):4 * (v - B1_HALVES) + 4]
                bias = s1[:, b0 + 4 * v:b0 + 4 * v + 4]
            else:
                dst = mod2[:, bass.ds(e * 8 + 4 * (v - B1_HALVES), 4)]
                bias = s1[:, bass.ds(e * 8 + (b0 + 4 * v), 4)]
            nc.vector.tensor_tensor(dst, PS[:, bank, 0:4], bias, ALU.add).then_inc(*ada_out.up)

        def mm3(out_, ah, al, bh, bl, start, stop, check=False):
            nc.tensor.matmul(out_, ah, bh, start=start, stop=False, skip_group_check=check)
            nc.tensor.matmul(out_, ah, bl, start=False, stop=False, skip_group_check=check)
            return nc.tensor.matmul(out_, al, bh, start=False, stop=stop, skip_group_check=check)

        def project(u, xh, xl, bank, tiles=range(NT), lo_at=None):
            wh, wl = (w.rearrange("p (k n) -> p k n", k=DC) for w in u)
            for t in tiles:
                for k in range(DC):
                    if lo_at and t == 0 and k % 2 == 0:
                        nc.tensor.wait_ge(*lo_at[k // 2])
                    ins = mm3(PS[:, bank, t * 256:(t + 1) * 256], xh[:, k, t * P:(t + 1) * P], xl[:, k, t * P:(t + 1) * P],
                              wh[:, k], wl[:, k], k == 0, k == DC - 1)
            return ins

        def rows_product(u, kk, xh, xl, bank, start, stop, check=False, tiles=range(NT)):
            wh, wl = (w.rearrange("p (k n) -> p k n", k=2)[:, kk] for w in u)
            for t in tiles:
                for half in range(2):
                    ins = mm3(PS[:, bank + 2 * t + half], xh[:, t * P:(t + 1) * P], xl[:, t * P:(t + 1) * P],
                              wh[:, half * 512:(half + 1) * 512], wl[:, half * 512:(half + 1) * 512], start, stop, check)
            return ins

        NB = (0, 1, 4, 5)

        class Norm:
            def __init__(self, name, per, stats_only=False):
                self.ss, self.rstd = (sig(f"{name}_{n}", 2 * per) for n in ("squares", "rstd"))
                self.x_new = sig(f"{name}_x_new", 2 * per)
                if stats_only:
                    return
                self.xa, self.xd, self.am, self.full = (sig(f"{name}_{n}", per) for n in ("scaled0", "scaled1", "factors", "full"))
                self.turned, self.hi, self.lo = (sig(f"{name}_{n}", 4 * per) for n in ("turned", "hi", "lo"))
                self.gcol, self.diag, self.row_mm, self.row = (sig(f"{name}_{n}", per) for n in
                                                               ("gate", "diag", "row_mm", "row"))

        def norm_act(act, N, k, l, src, dst, x_at=(None, None)):
            for t in range(NT):
                if x_at[t]:
                    act.wait_ge(*x_at[t])
                nc.scalar.activation(dst[:, t], src[:, t], ACT.Square, scale=D ** -0.5,
                                     accum_out=st[:, t:t + 1]).then_inc(*N.ss.up)
                if t == 0:
                    act.wait_ge(*N.rstd.at(2 * k, l))
                    nc.scalar.activation(dst[:, 0], src[:, 0], ACT.Copy, scale=st[:, 4:5]).then_inc(*N.xa.up)

        def norm_pool(pool, N, k, l):
            for t in range(NT):
                pool.wait_ge(*N.ss.at(2 * k + t, l))
                nc.gpsimd.tensor_tensor(st[:, 2 + t:3 + t], st[:, t:t + 1], k1[:, K1["eps"]][:, 0:1], ALU.add)
                pool.drain()
                nc.gpsimd.tensor_tensor(st[:, 4 + t:5 + t], st[:, 2 + t:3 + t], k1[:, K1["half"]][:, 0:1],
                                        ALU.pow).then_inc(*N.rstd.up)

        def norm_dve(dve, N, k, l, src, dst):
            dve.wait_ge(*N.rstd.at(2 * k + 1, l))
            nc.vector.tensor_scalar(dst[:, 1], src[:, 1], st[:, 5:6], None, ALU.mult).then_inc(*N.xd.up)

        def turn(pe, done, src, bank, n):
            for c in range(n):
                for t in range(NT):
                    o = (c % 2) * 256 + t * P
                    ins = nc.tensor.transpose(PS[:, bank + c // 2, o:o + P], src[:, t, c * P:(c + 1) * P], ident)
                if c % 2:
                    ins.then_inc(*done.up)

        def norm_pe(pe, N, k, l, src, banks):
            for t, scaled in enumerate((N.xa, N.xd)):
                pe.wait_ge(*scaled.at(k, l))
                for c in range(DC):
                    o = (c % 2) * 256 + t * P
                    ins = nc.tensor.transpose(PS[:, banks[c // 2], o:o + P], src[:, t, c * P:(c + 1) * P], ident)
                    if t and c % 2:
                        ins.then_inc(*N.turned.up)

        def spread_act(act, N, k, l, hi, shift, banks, am_):
            act.wait_ge(*N.am.at(k, l))
            for b in range(4):
                act.wait_ge(*N.turned.at(4 * k + b, l))
                for c in range(2):
                    ins = nc.scalar.activation(hi[:, 2 * b + c], PS[:, banks[b], c * 256:(c + 1) * 256], ACT.Identity,
                                               scale=am_[:, 2 * b + c:2 * b + c + 1], bias=shift[:, 2 * b + c:2 * b + c + 1])
                ins.then_inc(*N.hi.up)
            act.wait_ge(*N.lo.at(4 * k + 1, l))
            for c in range(2):
                ins = nc.scalar.activation(ntmp[:, 1, c * 256:(c + 1) * 256], PS[:, banks[3], c * 256:(c + 1) * 256],
                                           ACT.Identity, scale=am_[:, 6 + c:7 + c], bias=shift[:, 6 + c:7 + c])
            ins.then_inc(*N.full.up)

        def factors_dve(dve, N, scale, g, am_):
            nc.vector.scalar_tensor_tensor(am_[:, :], scale, 1.0, g, ALU.add, ALU.mult).then_inc(*N.am.up)

        def spread_dve(dve, N, k, l, hi, lo, shift, banks, am_):
            dve.drain()
            for b in range(4):
                dve.wait_ge(*N.hi.at(4 * k + b, l))
                if b < 3:
                    for c in range(2):
                        nc.vector.tensor_scalar(ntmp[:, b % 2, c * 256:(c + 1) * 256], PS[:, banks[b], c * 256:(c + 1) * 256],
                                                am_[:, 2 * b + c:2 * b + c + 1], shift[:, 2 * b + c:2 * b + c + 1],
                                                ALU.mult, ALU.add)
                    dve.drain()
                else:
                    dve.wait_ge(*N.full.at(k, l))
                nc.vector.tensor_tensor(lo[:, 2 * b:2 * b + 2].rearrange("p c n -> p (c n)"), ntmp[:, b % 2],
                                        hi[:, 2 * b:2 * b + 2].bitcast(F32).rearrange("p c n -> p (c n)"),
                                        ALU.subtract).then_inc(*N.lo.up)

        def split_act(act, turned, hi_sig, base, n, l):
            for b in range(n):
                act.wait_ge(*turned.at(base + b, l))
                nc.scalar.activation(hhi[:, 2 * b:2 * b + 2].rearrange("p c n -> p (c n)"), PS[:, b],
                                     ACT.Copy).then_inc(*hi_sig.up)

        def split_dve(dve, hi_sig, lo_sig, base, n, l):
            for b in range(n):
                dve.wait_ge(*hi_sig.at(base + b, l))
                nc.vector.tensor_tensor(hlo[:, 2 * b:2 * b + 2].rearrange("p c n -> p (c n)"), PS[:, b],
                                        hhi[:, 2 * b:2 * b + 2].bitcast(F32).rearrange("p c n -> p (c n)"),
                                        ALU.subtract).then_inc(*lo_sig.up)

        def gate_dve(dve, N, src, factor):
            nc.vector.tensor_scalar(gcol[:, :], src, factor, None, ALU.mult).then_inc(*N.gcol.up)

        def gate_pool(pool, N, k, l):
            pool.wait_ge(*N.gcol.at(k, l))
            nc.gpsimd.tensor_tensor(diag, mid(ident, [P, DC, P]), bc(gcol[:, :], [P, DC, P]), ALU.mult).then_inc(*N.diag.up)

        def gate_pe(pe, N, k, l, bank):
            pe.wait_ge(*N.diag.at(k, l))
            for c in range(DC):
                o = (c % 4) * P
                ins = nc.tensor.matmul(PS[:, bank + c // 4, o:o + P], ones, diag[:, c], start=True, stop=True)
            ins.then_inc(*N.row_mm.up)

        def gate_act(act, N, k, l, bank):
            act.wait_ge(*N.row_mm.at(k, l))
            nc.scalar.activation(row[:, :], PS[:, bank:bank + 2].rearrange("p b n -> p (b n)"), ACT.Copy).then_inc(*N.row.up)

        def residual(dve, done, y_at):
            for t in range(NT):
                dve.wait_ge(*y_at[t])
                nc.vector.tensor_tensor(ytmp[:, t], PS[:, 4 + 2 * t:6 + 2 * t].rearrange("p b n -> p (b n)"), row[:, :],
                                        ALU.mult)
                dve.drain()
                nc.vector.tensor_tensor(xs[:, t], xs[:, t], ytmp[:, t], ALU.add).then_inc(*done.up)

        def at_gate(c0, g):
            return c0 + (3 * g - 1 if g else 0)

        def pe_gate_up(pe, g, c0, E0, h0, e=0, lo_at=None):
            for j in range(2):
                wh, wl = (w.rearrange("p (k n) -> p k n", k=DC) for w in unit(pe, at_gate(c0, g) + j, E0 + e * 2))
                for f in range(2):
                    for k in range(DC):
                        w = slice(f * P, (f + 1) * P)
                        if lo_at and j + f == 0 and k % 2 == 0:
                            pe.wait_ge(*lo_at[k // 2])
                        ins = mm3(PS[:, 2 * (g % 2) + f, j * 256:(j + 1) * 256], wh[:, k, w], wl[:, k, w],
                                  hhi[:, k], hlo[:, k], k == 0, k == DC - 1)
                ins.then_inc(unit_used, 1)

        def pe_down(pe, g, c, E0, h0, e=0):
            pe.wait_ge(hlo_done, h0 + e * 2 + (g + 1))
            u = unit(pe, c, E0 + e * 2)
            for kk in range(2):
                ins = rows_product(u, kk, hid_hi[:, g % 2, kk], hid_lo[:, g % 2, kk], 4, False, False, True)
            ins.then_inc(unit_used, 1)

        def clear_sums(pe):
            for b in range(4, 8):
                nc.tensor.matmul(PS[:, b], zb[:, 0:P], zb[:, :], start=True, stop=False, skip_group_check=True)

        def last_down(pe, g, c, E0, h0):
            pe.wait_ge(hlo_done, h0 + (g + 1))
            u = unit(pe, c, E0)
            for t in range(NT):
                for kk in range(2):
                    ins = rows_product(u, kk, hid_hi[:, g % 2, kk], hid_lo[:, g % 2, kk], 4, False, False, True, (t,))
                if t:
                    ins.then_inc(unit_used, 1)
                for b in range(4 + 2 * t, 6 + 2 * t):
                    ins = nc.tensor.matmul(PS[:, b], zb[:, 0:P], zb[:, :], start=False, stop=True, skip_group_check=True)
                ins.then_inc(y_sum, 1)

        def act_silu(act, g, c0, E0, h0, moe, e=0):
            p = 2 * (g % 2)
            act.wait_ge(unit_used, (E0 + e * 2) * 3 + (at_gate(c0, g) + 2))
            if g >= 1:
                act.wait_ge(gated if moe else h_made, h0 + e * 2 + g)
            nc.scalar.activation(hs, PS[:, p:p + 2, 0:256], ACT.Silu).then_inc(silu_done, 1)

        def act_hi(act, g, c_down, E0, h0, e=0):
            act.wait_ge(h_made, h0 + e * 2 + (g + 1))
            if c_down is not None:
                act.wait_ge(unit_used, (E0 + e * 2) * 3 + (c_down + 1))
            nc.scalar.activation(hid_hi[:, g % 2], hf[:, g % 2], ACT.Copy).then_inc(hhi_done, 1)

        def dve_h(dve, g, h0, moe, e=0):
            p = 2 * (g % 2)
            dve.wait_ge(gated if moe else silu_done, h0 + e * 2 + (g + 1))
            nc.vector.tensor_tensor(hf[:, g % 2], hg if moe else hs, PS[:, p:p + 2, 256:512], ALU.mult).then_inc(h_made, 1)

        def dve_lo(dve, g, h0, e=0):
            dve.wait_ge(hhi_done, h0 + e * 2 + (g + 1))
            nc.vector.tensor_tensor(hid_lo[:, g % 2], hf[:, g % 2], hid_hi[:, g % 2].bitcast(F32), ALU.subtract).then_inc(hlo_done, 1)

        def hidden_loop(eng, n, body):
            with eng.Fori(0, (n - 1) // 2) as e:
                for g in (1, 2):
                    body(g, e)
            if n % 2 == 0:
                body(n - 1, 0)

        def hidden_pe(pe, n, c0, E0, h0, moe, row_at, lo_at=None):
            pe_gate_up(pe, 0, c0, E0, h0, lo_at=lo_at)
            if moe:
                pe.wait_ge(*route_d.at(0))
            pe.wait_ge(*row_at)
            clear_sums(pe)
            if moe:
                gates_pe(pe)

            def body(g, e):
                if moe:
                    pe.wait_ge(ada_out.sem, e * 2 + (EARLY_HALVES - PE_HALVES - 2 + g))
                pe_gate_up(pe, g, c0, E0, h0, e)
                if moe:
                    pe.wait_ge(h_made, h0 + e * 2 + g)
                    half_sum(pe, EARLY_HALVES - 2 + g, 2 * (1 - g % 2), e)
                pe_down(pe, g - 1, at_gate(c0, g) + 2, E0, h0, e)

            hidden_loop(pe, n, body)
            last_down(pe, n - 1, c0 + 3 * n - 1, E0, h0)
            if moe:
                half_sum(pe, N_HALVES - 1, 0)

        def hidden_act(act, n, c0, E0, h0, moe):
            def body(g, e):
                c = at_gate(c0, g)
                conv_hi(act, c + RING, E0 + e * 2)
                act_silu(act, g, c0, E0, h0, moe, e)
                conv_hi(act, c + 1 + RING, E0 + e * 2)
                act_hi(act, g, c - 1, E0, h0, e)
                conv_hi(act, c + 2 + RING, E0 + e * 2)

            conv_hi(act, c0 + RING, E0)
            if moe:
                gates_act(act)
            act_silu(act, 0, c0, E0, h0, moe)
            conv_hi(act, c0 + 1 + RING, E0)
            act_hi(act, 0, None, E0, h0)
            hidden_loop(act, n, body)

        def hidden_dve(dve, n, c0, E0, h0, moe):
            def body(g, e):
                c, v = at_gate(c0, g), EARLY_HALVES - 1 + g
                conv_lo(dve, c + RING, E0 + e * 2)
                if moe:
                    half_steps(dve, v, 0, e)
                dve_h(dve, g, h0, moe, e)
                conv_lo(dve, c + 1 + RING, E0 + e * 2)
                dve_lo(dve, g, h0, e)
                if moe:
                    half_out(dve, v - 1, 2 * (1 - g % 2), e)
                    half_steps(dve, v, 1, e)
                conv_lo(dve, c + 2 + RING, E0 + e * 2)

            conv_lo(dve, c0 + RING, E0)
            dve_h(dve, 0, h0, moe)
            conv_lo(dve, c0 + 1 + RING, E0)
            dve_lo(dve, 0, h0)
            hidden_loop(dve, n, body)
            if moe:
                half_out(dve, N_HALVES - 1, 0)

        N1, N3 = Norm("n1", 3), Norm("n3", 2, stats_only=True)
        proj_mm, proj_out, rope_a, rope_c, t1_mm, t1_out = (
            sig(n) for n in ("proj_mm", "proj_out", "rope_a", "rope_c", "t1_mm", "t1_out"))
        s_mm, negmax, exp_done, p_turned, pt_out, pv_done, o_out = (
            sig(f"b1_{n}") for n in ("scores", "negmax", "exp", "p_turned", "pt_out", "pv", "o_out"))
        sink_sum, sink_exp, lam_sum, lam_exp, gelu_done, var_done, vn_scale, vn_done, gm_mm, yb_done, yc_var, yc_scale = (
            sig(n) for n in ("sink_sum", "sink_exp", "lam_sum", "lam_exp", "gelu_done", "var_done", "vn_scale", "vn_done",
                             "gm_mm", "yb_done", "yc_var", "yc_scale"))
        y1_turned, y1_hi, y1_lo, y1_half = sig("y1_turned"), sig("y1_hi"), sig("y1_lo"), sig("y1_half")

        def out_product(pe, c, e, half_done):
            for w in range(4):
                u = unit(pe, c + w, e)
                for tiles in ((0, 1),) if w < 3 else ((0,), (1,)):
                    for kk in range(2):
                        ins = rows_product(u, kk, hhi[:, 2 * w + kk], hlo[:, 2 * w + kk], 4, w + kk == 0, w + kk == 4, False, tiles)
                    if tiles == (0,):
                        ins.then_inc(*half_done.up)
                ins.then_inc(unit_used, 1)

        router_hi, router_lo, logits, route_d, route_a, gates_done, gt_mm, gt_out, gb_mm, gb_out = (
            sig(n) for n in ("router_hi", "router_lo", "logits", "route_d", "route_a", "gates_done", "gt_mm", "gt_out",
                             "gb_mm", "gb_out"))
        cond_done, zeros_made = sig("cond_done"), sig("zeros_made")

        xc_tok = z(0, 2048).rearrange("p (t n) -> p t n", t=2)
        crow = z(2048, 2048)
        xcn = z(4096, 2048).rearrange("p (t n) -> p t n", t=2)
        zhi, zlo = zr[:, 0], zr[:, 1]
        nm1, nms, den1, rd1 = sm[:, 0:32], sm[:, 32:48], sm[:, 48:80], sm[:, 80:112]
        lsum, lexp, lam, nsink, stmp, vstat, gsub8 = (sm[:, 112:114], sm[:, 114:116], sm[:, 116:117], sm[:, 120:128],
                                                      sm[:, 128:144], sm[:, 144:168], sm[:, 192:256])
        IN_UNITS = [(OFF_AK, 0), (OFF_AQ, None), (OFF_AQ + 256, None), (OFF_CK, 256), (OFF_CV, 512), (OFF_CQ, None),
                    (OFF_BU, None), (OFF_BV, None)]
        EARLY_UNITS = 6
        CTX_UNITS = [u_ for u_, (_, c_) in enumerate(IN_UNITS) if c_ is not None]
        FILL = {}
        for u_, (_, c_) in enumerate(IN_UNITS):
            for src_ in (("c", "x") if c_ is not None else ("x",)):
                FILL[u_, src_] = len(FILL)
        TURNS = [(pc[:, :, 0:P], ak[:, 0:256], 1.0), (pj[:, :, OFF_AK:OFF_AK + P], ak[:, 256:512], 1.0)]
        TURNS += [(pj[:, :, P * b:P * b + P], aq[:, b], A_D ** -0.5) for b in range(4)]
        for b_ in range(2):
            TURNS += [(pc[:, :, 256 + P * b_:256 + P * b_ + P], ck[:, b_, 0:256], 1.0),
                      (pj[:, :, OFF_CK + P * b_:OFF_CK + P * b_ + P], ck[:, b_, 256:512], 1.0),
                      (pj[:, :, OFF_CQ + P * b_:OFF_CQ + P * b_ + P], cq[:, b_], C_Q ** -0.5)]
        CQZ = [pj[:, :, P * k:P * k + P] for k in range(5)] + [cq[:, k].rearrange("p (t n) -> p t n", t=2) for k in range(2)]
        CQZ += [pc[:, :, 0:P]]
        PASSES = 32

        def bc(ap, shape):
            return ap.unsqueeze(len(shape) - 1).to_broadcast(shape)

        def mid(ap, shape):
            return ap.unsqueeze(1).to_broadcast(shape)

        def rope(eng, ops, x, cos, sin, tmp):
            x1, x2 = x
            t1, t2, t3, t4 = tmp
            ops.tensor_tensor(t1, x1, cos, ALU.mult)
            ops.tensor_tensor(t2, x2, sin, ALU.mult)
            ops.tensor_tensor(t3, x1, sin, ALU.mult)
            ops.tensor_tensor(t4, x2, cos, ALU.mult)
            eng.drain()
            ops.tensor_tensor(x1, t1, t2, ALU.subtract)
            return ops.tensor_tensor(x2, t3, t4, ALU.add)

        def a_scores(p):
            t, j = (p % 16) // 8, p % 8
            if p < 16:
                r = slice(64 * (j % 2), 64 * (j % 2) + 64)
                kv = j % 2
                v = [pc[:, c, P + 64 * kv:P + 64 * kv + 64] for c in range(2)]
                v += [pj[:, c, OFF_AV + 64 * kv:OFF_AV + 64 * kv + 64] for c in range(2)]
                return aq[r, j // 2, t * P:(t + 1) * P], ak[r, :], v
            h = j // 2
            v = [pc[:, c, 512 + 64 * h:512 + 64 * h + 64] for c in range(2)]
            v += [pj[:, c, OFF_CV + 64 * h:OFF_CV + 64 * h + 64] for c in range(2)]
            return CQZ[j][:, t], ck[:, j // 4, :], v

        ATT_V0 = EARLY_UNITS + PE_HALVES
        ATT_SUMS = {1: ATT_V0 - 1}
        ATT_SUMS.update({4 * k + 5: ATT_V0 + k for k in range(EARLY_HALVES - 1 - ATT_V0)})
        B_TURNS = {0: (6, 0), 1: (6, 1), 3: (7, 0), 4: (7, 1)}
        C_TURN0, GELU_TURN, GM_TURN = 6, 6, 12

        L = sm[:, 0:40].rearrange("p (t n) -> p t n", t=2)
        gates = sm[:, 40:72].rearrange("p (t g j) -> p t g j", t=2, g=MG)
        gateT = z(8704, 256)

        def gates_pe(pe):
            pe.wait_ge(*gates_done.at(0))
            for t in range(NT):
                ins = nc.tensor.transpose(PS[0:NE, 3, t * P:(t + 1) * P], sm[:, 40 + NE * t:40 + NE * t + NE], ident)
            ins.then_inc(*gt_mm.up)
            pe.wait_ge(*gt_out.at(0))
            for i in range(NE // 2):
                if i >= 2:
                    pe.wait_ge(*gb_out.at(i - 2))
                for j in range(2):
                    e = 2 * i + j
                    ins = nc.tensor.matmul(PS[:, 2 + i % 2, j * 256:(j + 1) * 256], ident[0:NE, e:e + 1].to_broadcast([NE, P]),
                                           gateT[0:NE, :], start=True, stop=True)
                ins.then_inc(*gb_mm.up)
            pe.wait_ge(*gb_out.at(NE // 2 - 1))

        def gates_act(act):
            act.wait_ge(*gt_mm.at(0))
            nc.scalar.activation(gateT[0:NE, :], PS[0:NE, 3, 0:256], ACT.Copy).then_inc(*gt_out.up)
            for i in range(NE // 2):
                act.wait_ge(*gb_mm.at(i))
                nc.scalar.activation(gb[:, 512 * i:512 * i + 512], PS[:, 2 + i % 2], ACT.Copy).then_inc(*gb_out.up)

        def route_dve(dve):
            code4 = s_code
            L4, E16 = L[:, :, 0:4], L[:, :, 4:20]
            a = [sm[:, 80 + 8 * i:88 + 8 * i].rearrange("p (t n) -> p t n", t=2) for i in range(12)]
            m = [sm[:, 176 + 2 * i:178 + 2 * i] for i in range(12)]
            prod = sm[:, 208:240].rearrange("p (t g j) -> p t g j", t=2, g=MG)
            s4 = [P, 2, 4]

            def best(x, top, mask, eq, cm):
                nc.vector.tensor_reduce(top, x, AX.X, ALU.max)
                dve.drain()
                nc.vector.tensor_tensor(eq, x, bc(top, s4), ALU.is_ge)
                dve.drain()
                nc.vector.tensor_tensor(eq, eq, mid(code4, s4), ALU.mult)
                dve.drain()
                nc.vector.tensor_reduce(cm, eq, AX.X, ALU.max)
                dve.drain()
                nc.vector.tensor_tensor(mask, eq, bc(cm, s4), ALU.is_equal)
                dve.drain()

            dve.wait_ge(*logits.at(0))
            nc.vector.tensor_tensor(L, PS[:, 6, 0:64].rearrange("p (t n) -> p t n", t=2)[:, :, 0:20],
                                    mid(s1[:, S1["br"]], [P, 2, 20]), ALU.add)
            dve.drain()
            best(L4, m[0], a[0], a[1], m[1])
            nc.vector.tensor_tensor(a[2], L4, bc(m[0], s4), ALU.subtract).then_inc(*route_d.up)
            nc.vector.tensor_tensor(prod, E16.rearrange("p t (g j) -> p t g j", g=MG), bc(a[0], [P, 2, 4, 4]), ALU.mult)
            dve.drain()
            nc.vector.tensor_reduce(a[4], prod.rearrange("p t g j -> p t j g"), AX.X, ALU.add)
            dve.drain()
            best(a[4], m[2], a[5], a[6], m[3])
            nc.vector.scalar_tensor_tensor(a[7], a[5], NEG, a[4], ALU.mult, ALU.add)
            dve.drain()
            best(a[7], m[4], a[8], a[9], m[5])
            nc.vector.tensor_tensor(m[6], m[4], m[2], ALU.subtract).then_inc(*route_d.up)
            dve.wait_ge(*route_a.at(1))
            nc.vector.tensor_reduce(m[8], a[3], AX.X, ALU.add)
            nc.vector.tensor_scalar(m[9], m[7], 1.0, None, ALU.add)
            dve.drain()
            nc.vector.tensor_tensor(m[10], m[8], m[9], ALU.mult)
            dve.drain()
            nc.vector.reciprocal(m[8], m[10])
            dve.drain()
            nc.vector.tensor_tensor(m[9], m[8], m[7], ALU.mult)
            dve.drain()
            nc.vector.tensor_tensor(a[5], a[5], bc(m[8], s4), ALU.mult)
            nc.vector.tensor_tensor(a[8], a[8], bc(m[9], s4), ALU.mult)
            dve.drain()
            nc.vector.tensor_tensor(a[5], a[5], a[8], ALU.add)
            dve.drain()
            for t in range(NT):
                ins = nc.vector.tensor_tensor(gates[:, t], bc(a[0][:, t], [P, 4, 4]), mid(a[5][:, t], [P, 4, 4]), ALU.mult)
            ins.then_inc(*gates_done.up)

        def route_act(act):
            for i, (src, dst) in enumerate(((96, 104), (188, 190))):
                n = 8 if i == 0 else 2
                act.wait_ge(*route_d.at(i))
                nc.scalar.activation(sm[:, dst:dst + n], sm[:, src:src + n], ACT.Exp).then_inc(*route_a.up)

        s_code = k1[:, K1["code"]][:, 0:4]

        def pe_block1(pe):
            pe.wait_ge(small_in, 32)
            pe.wait_ge(*cond_done.at(0))
            for v in range(PE_HALVES):
                if v >= 2:
                    pe.wait_ge(*ada_rows_out.at(v - 2))
                for i in range(2):
                    pe.wait_ge(ada_landed[i], 16 * (v + 1))
                    for k in range(4):
                        n = 4 * i + k
                        ins = nc.tensor.matmul(PS[0:2, 6 + v % 2, :], cs[:, n:16:8], ada[:, i, 512 * k:512 * k + 512],
                                               start=n == 0, stop=n == 7)
                    ins.then_inc(ada_used_pe, 1)
            norm_pe(pe, N1, 0, 0, xn, range(4))
            pe.wait_ge(*ada_rows_out.at(PE_HALVES - 1))
            for c in range(16):
                ins = nc.tensor.transpose(PS[:, 6, 2 * c:2 * c + 2], crow[0:2, c * P:(c + 1) * P], ident[0:2, 0:2])
            ins.then_inc(*ada_cols.up)
            pe.wait_ge(*mod_ready.at(0))
            norm_pe(pe, N1, 1, 0, xcn, range(4, 8))
            for u in range(EARLY_UNITS):
                both = unit(pe, u)
                for src in ("c", "x"):
                    if (u, src) not in FILL:
                        continue
                    f = FILL[u, src]
                    if f >= 6:
                        pe.wait_ge(*proj_out.at(f - 6))
                    xh, xl = (hhi, hlo) if src == "x" else (zhi, zlo)
                    lo_at = [N1.lo.at(4 + b) for b in range(4)] if f == 0 else None
                    project(both, xh, xl, f % 6, lo_at=lo_at).then_inc(unit_used if src == "x" else proj_mm.sem, 1)
                if u >= 2:
                    half_sum(pe, u + 2, 6 + u % 2)
            half_sum(pe, 8, 6)
            def turn_pair(i, bank):
                src = TURNS[i][0]
                for t in range(NT):
                    ins = nc.tensor.transpose(PS[:, bank, t * P:(t + 1) * P], src[:, t], ident)
                ins.then_inc(*t1_mm.up)

            pe.wait_ge(*proj_out.at(FILL[EARLY_UNITS - 1, "x"]))
            for i in range(6):
                if i == 1:
                    pe.wait_ge(*rope_a.at(0))
                if i >= 4:
                    pe.wait_ge(*t1_out.at(i - 4))
                turn_pair(i, i % 4)
            pe.wait_ge(*t1_out.at(5))
            pe.wait_ge(*ada_out.at(7 - PE_HALVES))
            pe.wait_ge(*const_made.at(0))
            pe.wait_ge(mask_in, 16)
            for i in range(PASSES + 2):
                if i < PASSES:
                    q, k, _ = a_scores(i)
                    if i >= 2:
                        pe.wait_ge(*exp_done.at(i - 2))
                    if i < 16:
                        nc.tensor.matmul(PS[:, i % 2], idb[:, :], masks[:, i // 8], start=True, stop=False)
                    nc.tensor.matmul(PS[:, i % 2], q, k, start=i >= 16, stop=True).then_inc(*s_mm.up)
                if 1 <= i <= PASSES:
                    p = i - 1
                    pe.wait_ge(*exp_done.at(p))
                    if p >= 2:
                        pe.wait_ge(*pt_out.at(p - 2))
                    for c in range(4):
                        ins = nc.tensor.transpose(PS[:, 2 + p % 2, c * P:(c + 1) * P], pr[:, p % 2, c * P:(c + 1) * P], ident)
                    ins.then_inc(*p_turned.up)
                if i >= 2:
                    p = i - 2
                    pe.wait_ge(*pt_out.at(p))
                    if p % 8 == 0 and p >= 16:
                        pe.wait_ge(*o_out.at(p // 8 - 2))
                    v = a_scores(p)[2]
                    for c in range(4):
                        ins = nc.tensor.matmul(PS[:, 4 + (p // 8) % 2, 64 * (p % 8):64 * (p % 8) + 64],
                                               pt[:, p % 2, c * P:(c + 1) * P], v[c], start=c == 0, stop=c == 3)
                    ins.then_inc(*pv_done.up)
                if i in ATT_SUMS:
                    if i == 1:
                        pe.wait_ge(*ada_out.at(8 - PE_HALVES))
                    half_sum(pe, ATT_SUMS[i], 6)
                if i in B_TURNS:
                    u, tile = B_TURNS[i]
                    if i == 3:
                        pe.wait_ge(*proj_out.at(FILL[6, "x"]))
                    ins = project(unit(pe, u), hhi, hlo, 7, (tile,))
                    if tile:
                        ins.then_inc(unit_used, 1)
                if C_TURN0 <= i < C_TURN0 + 6:
                    if i == C_TURN0:
                        pe.wait_ge(*proj_out.at(FILL[7, "x"]))
                        pe.wait_ge(*rope_c.at(0))
                    else:
                        pe.wait_ge(*t1_out.at(i - C_TURN0 + 5))
                    turn_pair(i - C_TURN0 + 6, 7)
                if i == GM_TURN:
                    pe.wait_ge(*t1_out.at(len(TURNS) - 1))
                    pe.wait_ge(*vn_done.at(0))
                    w0 = S1["ws"].start
                    for g in range(B_G):
                        ins = nc.tensor.matmul(PS[:, 7, g * P:(g + 1) * P], s1[:, w0 + g * P:w0 + (g + 1) * P],
                                               pj[:, :, OFF_BV + 64 * g:OFF_BV + 64 * g + 64], start=True, stop=True)
                    ins.then_inc(*gm_mm.up)
            pe.wait_ge(*o_out.at(3))
            turn(pe, y1_turned, xn, 0, DC)
            gate_pe(pe, N1, 0, 0, 4)
            pe.wait_ge(*N1.row.at(0))
            pe.wait_ge(*ada_out.at(EARLY_HALVES - 2 - PE_HALVES))
            pe.wait_ge(*y1_lo.at(3))
            out_product(pe, 8, 0, y1_half)
            norm_pe(pe, N1, 2, 0, xn, NB)
            gate_pe(pe, N1, 1, 0, 2)
            pe.wait_ge(*N1.lo.at(11))
            pe.wait_ge(*router_lo.at(0))
            for t in range(NT):
                for k in range(DC):
                    ts = slice(t * P, (t + 1) * P)
                    ins = mm3(PS[:, 6, 32 * t:32 * t + 20], hhi[:, k, ts], hlo[:, k, ts], rh[:, k], rl[:, k], k == 0, k == DC - 1)
            ins.then_inc(*logits.up)
            hidden_pe(pe, MOE_GROUPS, B1_UNITS, 0, 0, True, N1.row.at(1))

        def act_block1(act):
            act.wait_ge(small_in, 32)
            nc.scalar.activation(cs[:, :], s1[:, 0:24], ACT.Silu).then_inc(*cond_done.up)
            w0 = S1["wr"].start
            nc.scalar.activation(rh[:, :, :], s1[:, w0:w0 + 160].rearrange("p (k n) -> p k n", k=8),
                                 ACT.Copy).then_inc(*router_hi.up)
            act.wait_ge(x_landed, 32)
            norm_act(act, N1, 0, 0, xs, xn)
            norm_act_ctx(act)
            for v in range(PE_HALVES):
                act.wait_ge(ada_used_pe, 2 * v + 2)
                nc.scalar.activation(crow[0:2, 512 * v:512 * v + 512], PS[0:2, 6 + v % 2, :], ACT.Copy).then_inc(*ada_rows_out.up)
            spread_act(act, N1, 0, 0, hhi, mod1[:, 0:8], range(4), am)
            conv_hi(act, 0)
            spread_act(act, N1, 1, 0, zhi, modc[:, 0:8], range(4, 8), am2)
            for u in range(1, RING):
                conv_hi(act, u)
            for u in range(EARLY_UNITS):
                for src in ("c", "x"):
                    if (u, src) in FILL:
                        if src == "c":
                            act.wait_ge(*proj_mm.at(CTX_UNITS.index(u)))
                            dst = pc[:, :, IN_UNITS[u][1]:IN_UNITS[u][1] + 256]
                        else:
                            act.wait_ge(unit_used, u + 1)
                            dst = pj[:, :, IN_UNITS[u][0]:IN_UNITS[u][0] + 256]
                        nc.scalar.activation(dst, PS[:, FILL[u, src] % 6].rearrange("p (t n) -> p t n", t=2),
                                             ACT.Copy).then_inc(*proj_out.up)
                conv_hi(act, u + RING)

            def turned_out(i, bank):
                _, dst, scale = TURNS[i]
                act.wait_ge(*t1_mm.at(i))
                if i not in (8, 11):
                    nc.scalar.activation(dst, PS[:, bank, 0:256], ACT.Copy, scale=scale).then_inc(*t1_out.up)
                    return
                if i == 8:
                    act.wait_ge(*zeros_made.at(0))
                for j in range(4):
                    q = slice(32 * j, 32 * j + 32)
                    ins = nc.scalar.activation(CQZ[4 * (i == 11) + j][q], PS[q, bank, 0:256].rearrange("p (t n) -> p t n", t=2),
                                               ACT.Copy, scale=scale)
                ins.then_inc(*t1_out.up)

            for i in range(6):
                turned_out(i, i % 4)
            act.wait_ge(*lam_sum.at(0))
            nc.scalar.activation(lexp, lsum, ACT.Exp).then_inc(*lam_exp.up)
            for i in range(PASSES + 1):
                if i < PASSES:
                    act.wait_ge(*negmax.at(i))
                    if i >= 2:
                        act.wait_ge(*p_turned.at(i - 2))
                    bias = nms[:, i:i + 1] if i < 16 else nm1[:, i:i + 1]
                    nc.scalar.activation(pr[:, i % 2], PS[:, i % 2], ACT.Exp, bias=bias,
                                         accum_out=den1[:, i:i + 1]).then_inc(*exp_done.up)
                if i >= 1:
                    p = i - 1
                    act.wait_ge(*p_turned.at(p))
                    if p >= 2:
                        act.wait_ge(*pv_done.at(p - 2))
                    nc.scalar.activation(pt[:, p % 2], PS[:, 2 + p % 2], ACT.Copy).then_inc(*pt_out.up)
                if B_TURNS.get(i - 1, (0, 0))[1]:
                    u = B_TURNS[i - 1][0]
                    act.wait_ge(unit_used, u + 1)
                    o = IN_UNITS[u][0]
                    nc.scalar.activation(pj[:, :, o:o + 256], PS[:, 7].rearrange("p (t n) -> p t n", t=2),
                                         ACT.Copy).then_inc(*proj_out.up)
                    conv_hi(act, u + RING)
                if i == GELU_TURN:
                    act.drain()
                    uv = pj[:, :, OFF_BU:OFF_CQ]
                    nc.scalar.activation(uv, uv, ACT.Gelu_apprx_tanh).then_inc(*gelu_done.up)
                if C_TURN0 < i <= C_TURN0 + 6:
                    turned_out(i - 1 - C_TURN0 + 6, 7)
                if i in (8, 16):
                    t = i // 8 - 1
                    act.wait_ge(*sink_sum.at(t))
                    nc.scalar.activation(stmp[:, 8 * t:8 * t + 8], stmp[:, 8 * t:8 * t + 8], ACT.Exp).then_inc(*sink_exp.up)
            split_act(act, y1_turned, y1_hi, 0, 4, 0)
            gate_act(act, N1, 0, 0, 4)
            for u in range(8, 11):
                conv_hi(act, u + RING)
            norm_act(act, N1, 2, 0, xs, xn, [N1.x_new.at(t) for t in range(NT)])
            conv_hi(act, 11 + RING)
            spread_act(act, N1, 2, 0, hhi, mod1[:, 24:32], NB, am)
            gate_act(act, N1, 1, 0, 2)
            route_act(act)
            hidden_act(act, MOE_GROUPS, B1_UNITS, 0, 0, True)
            conv_hi(act, LAYER0 - 1 + RING)
            norm_stats(act, [N1.x_new.at(2 + t) for t in range(NT)])

        def norm_act_ctx(act):
            norm_act(act, N1, 1, 0, xc_tok, xcn)

        def norm_stats(act, x_at):
            for t in range(NT):
                act.wait_ge(*x_at[t])
                nc.scalar.activation(xn[:, t], xs[:, t], ACT.Square, scale=D ** -0.5,
                                     accum_out=st[:, t:t + 1]).then_inc(*N3.ss.up)

        def pool_block1(pool):
            nc.gpsimd.memset(zb[:, :], 0.0)
            pool.wait_ge(small_in, 32)
            nc.gpsimd.tensor_copy(idb[:, :], ident).then_inc(*const_made.up)
            norm_pool(pool, N1, 0, 0)
            pool.wait_ge(*N1.xa.at(0))
            pool.wait_ge(*N1.xd.at(0))
            norm_pool(pool, N1, 1, 0)
            tmpA = [z(8704 + 320 * i, 320).rearrange("p (h f n) -> p h f n", h=10, f=2) for i in range(4)]
            tmpC = [row[:, 256 * i:256 * i + 256].rearrange("p (h f n) -> p h f n", h=16, f=2) for i in range(4)]
            pool.wait_ge(*proj_out.at(FILL[2, "x"]))
            for t in range(NT):
                x = pj[:, t, 0:640].rearrange("p (h f s n) -> p h f s n", h=10, f=2, s=2)
                c, s_ = (mid(k1[:, K1[n]].rearrange("p (t f n) -> p t f n", t=2, f=2)[:, t], [P, 10, 2, 16]) for n in ("cosA", "sinA"))
                ins = rope(pool, nc.gpsimd, (x[:, :, :, 0], x[:, :, :, 1]), c, s_, tmpA)
                if t:
                    ins.then_inc(*rope_a.up)
                pool.drain()
            pool.wait_ge(*proj_out.at(FILL[5, "x"]))
            for t in range(NT):
                x = pj[:, t, OFF_CQ:OFF_CV].rearrange("p (h f s n) -> p h f s n", h=16, f=2, s=2)
                c, s_ = (mid(k1[:, K1[n]].rearrange("p (t f n) -> p t f n", t=2, f=2)[:, t], [P, 16, 2, 8]) for n in ("cosC", "sinC"))
                ins = rope(pool, nc.gpsimd, (x[:, :, :, 0], x[:, :, :, 1]), c, s_, tmpC)
                if t:
                    ins.then_inc(*rope_c.up)
                pool.drain()
            pool.wait_ge(*t1_out.at(5))
            for q in CQZ:
                ins = nc.gpsimd.memset(q, 0.0)
            ins.then_inc(*zeros_made.up)
            pool.wait_ge(*var_done.at(0))
            nc.gpsimd.tensor_tensor(vstat[:, 8:16], vstat[:, 0:8], k1[:, K1["half"]][:, 0:1].to_broadcast([P, 8]),
                                    ALU.pow).then_inc(*vn_scale.up)
            for t in range(NT):
                pool.wait_ge(*yc_var.at(t))
                nc.gpsimd.tensor_tensor(vstat[:, 4:8], vstat[:, 0:4], k1[:, K1["half"]][:, 0:1].to_broadcast([P, 4]),
                                        ALU.pow).then_inc(*yc_scale.up)
            gate_pool(pool, N1, 0, 0)
            gate_pool(pool, N1, 1, 0)
            norm_pool(pool, N1, 2, 0)

            def gate_hidden(g, e):
                pool.wait_ge(silu_done, e * 2 + (g + 1))
                if g:
                    pool.wait_ge(h_made, e * 2 + g)
                a = (g // 2) * 256
                w = gb[:, a:a + 256] if isinstance(e, int) else gb[:, bass.ds(e * 256 + a, 256)]
                nc.gpsimd.tensor_tensor(hg, hs, mid(w, [P, 2, 256]), ALU.mult).then_inc(gated, 1)

            pool.wait_ge(*gb_out.at(NE // 2 - 1))
            gate_hidden(0, 0)
            hidden_loop(pool, MOE_GROUPS, gate_hidden)
            norm_pool(pool, N3, 0, 0)

        def dve_block1(dve):
            dve.wait_ge(*router_hi.at(0))
            w0 = S1["wr"].start
            nc.vector.tensor_tensor(rl[:, :, :], s1[:, w0:w0 + 160].rearrange("p (k n) -> p k n", k=8),
                                    rh[:, :, :].bitcast(F32), ALU.subtract).then_inc(*router_lo.up)
            lm = s1[:, S1["lam"]].rearrange("p (a b n) -> p a b n", a=2, b=2)
            lt = sm[:, 0:64].rearrange("p (a n) -> p a n", a=2)
            nc.vector.tensor_tensor(lt, lm[:, :, 0], lm[:, :, 1], ALU.mult)
            nc.vector.tensor_scalar(nsink, s1[:, S1["sink"]], -1.0, None, ALU.mult)
            nc.vector.tensor_scalar(gsub8, s1[:, S1["gsub"]], 1.0 - LAM_INIT, None, ALU.mult)
            dve.drain()
            nc.vector.tensor_reduce(lsum, lt, AX.X, ALU.add).then_inc(*lam_sum.up)
            norm_dve(dve, N1, 0, 0, xs, xn)
            norm_dve(dve, N1, 1, 0, xc_tok, xcn)
            dve.wait_ge(*ada_cols.at(0))
            cols = PS[:, 6, 0:32].rearrange("p (c s) -> p s c", s=2)
            b0 = S1["bada"].start
            nc.vector.tensor_tensor(mod1[:, 0:16], cols[:, 0], s1[:, b0:b0 + 16], ALU.add)
            nc.vector.tensor_tensor(modc[:, :], cols[:, 1], s1[:, b0:b0 + 16], ALU.add).then_inc(*mod_ready.up)
            dve.drain()
            factors_dve(dve, N1, mod1[:, 8:16], s1[:, S1["gmix"]], am)
            factors_dve(dve, N1, modc[:, 8:16], s1[:, S1["gmix"]], am2)
            spread_dve(dve, N1, 0, 0, hhi, hlo, mod1[:, 0:8], range(4), am)
            conv_lo(dve, 0)
            spread_dve(dve, N1, 1, 0, zhi, zlo, modc[:, 0:8], range(4, 8), am2)
            for u in range(1, RING):
                conv_lo(dve, u)
            for u in range(EARLY_UNITS):
                conv_lo(dve, u + RING)
                if u >= 3:
                    half_out(dve, u + 1, 6 + (u + 1) % 2)
                half_steps(dve, u + 4, 0)
                half_steps(dve, u + 4, 1)
            half_out(dve, 7, 7)
            half_out(dve, 8, 6)

            def normalise_v():
                dve.wait_ge(*gelu_done.at(0))
                for t in range(NT):
                    v4 = pj[:, t, OFF_BV:OFF_CQ].rearrange("p (g n) -> p g n", g=4)
                    nc.vector.tensor_reduce(vstat[:, 16 + 4 * t:20 + 4 * t], v4, AX.X, ALU.add)
                dve.drain()
                nc.vector.tensor_scalar(vstat[:, 16:24], vstat[:, 16:24], -1.0 / B_D, None, ALU.mult)
                dve.drain()
                sq = xn[:, :, 0:256]
                for t in range(NT):
                    v4 = pj[:, t, OFF_BV:OFF_CQ].rearrange("p (g n) -> p g n", g=4)
                    nc.vector.tensor_tensor(v4, v4, bc(vstat[:, 16 + 4 * t:20 + 4 * t], [P, 4, 64]), ALU.add)
                dve.drain()
                nc.vector.tensor_tensor(sq, pj[:, :, OFF_BV:OFF_CQ], pj[:, :, OFF_BV:OFF_CQ], ALU.mult)
                dve.drain()
                for t in range(NT):
                    nc.vector.tensor_reduce(vstat[:, 4 * t:4 * t + 4], sq[:, t].rearrange("p (g n) -> p g n", g=4), AX.X, ALU.add)
                dve.drain()
                nc.vector.tensor_scalar(vstat[:, 0:8], vstat[:, 0:8], 1.0 / B_D, EPS, ALU.mult, ALU.add).then_inc(*var_done.up)

            def scale_v():
                dve.wait_ge(*vn_scale.at(0))
                for t in range(NT):
                    v4 = pj[:, t, OFF_BV:OFF_CQ].rearrange("p (g n) -> p g n", g=4)
                    nc.vector.tensor_tensor(v4, v4, bc(vstat[:, 8 + 4 * t:12 + 4 * t], [P, 4, 64]), ALU.mult)
                dve.drain()
                nc.vector.tensor_tensor(pj[:, :, OFF_BV:OFF_CQ], pj[:, :, OFF_BV:OFF_CQ], mid(s1[:, S1["gtok"]], [P, 2, 256]),
                                        ALU.mult).then_inc(*vn_done.up)

            def gated_out():
                dve.wait_ge(*gm_mm.at(0))
                for g in range(B_G):
                    b = S1["bs"].start + g
                    ins = nc.vector.scalar_tensor_tensor(
                        xn[:, :, 512 + 64 * g:576 + 64 * g], PS[:, 7, g * P:(g + 1) * P].rearrange("p (t n) -> p t n", t=2),
                        s1[:, b:b + 1], pj[:, :, OFF_BU + 64 * g:OFF_BU + 64 * g + 64], ALU.add, ALU.mult)
                ins.then_inc(*yb_done.up)

            dve.wait_ge(*lam_exp.at(0))
            nc.vector.tensor_tensor(lam, lexp[:, 1:2], lexp[:, 0:1], ALU.subtract)
            dve.drain()
            nc.vector.tensor_scalar(lam, lam, -LAM_INIT, None, ALU.add)
            dve.drain()

            def finish(f):
                t = f % 2
                O = PS[:, 4 + f % 2].rearrange("p (j n) -> p j n", j=8)
                dn, rd = den1[:, 8 * f:8 * f + 8], rd1[:, 8 * f:8 * f + 8]
                if f < 2:
                    dve.wait_ge(*sink_exp.at(f))
                    nc.vector.tensor_tensor(dn, dn, stmp[:, 8 * f:8 * f + 8], ALU.add)
                    dve.drain()
                dve.wait_ge(*pv_done.at(8 * f + 7))
                nc.vector.reciprocal(rd, dn)
                dve.drain()
                if f < 2:
                    nc.vector.tensor_tensor(xn[:, t, 0:512].rearrange("p (j n) -> p j n", j=8), O, bc(rd, [P, 8, 64]),
                                            ALU.mult).then_inc(*o_out.up)
                    return
                second = rd.rearrange("p (h m) -> p m h", m=2)[:, 1]
                nc.vector.tensor_scalar(second, second, lam, None, ALU.mult)
                dve.drain()
                both = row[:, 0:512].rearrange("p (j n) -> p j n", j=8)
                bh = row[:, 0:512].rearrange("p (h m n) -> p m h n", h=4, m=2)
                o4 = row[:, 512:768].rearrange("p (h n) -> p h n", h=4)
                q4 = row[:, 768:1024].rearrange("p (h n) -> p h n", h=4)
                nc.vector.tensor_tensor(both, O, bc(rd, [P, 8, 64]), ALU.mult)
                dve.drain()
                nc.vector.tensor_tensor(o4, bh[:, 0], bh[:, 1], ALU.add)
                dve.drain()
                nc.vector.tensor_tensor(q4, o4, o4, ALU.mult)
                dve.drain()
                nc.vector.tensor_reduce(vstat[:, 0:4], q4, AX.X, ALU.add)
                dve.drain()
                nc.vector.tensor_scalar(vstat[:, 0:4], vstat[:, 0:4], 1.0 / C_V, EPS, ALU.mult, ALU.add).then_inc(*yc_var.up)
                dve.wait_ge(*yc_scale.at(t))
                nc.vector.tensor_tensor(o4, o4, bc(vstat[:, 4:8], [P, 4, 64]), ALU.mult)
                dve.drain()
                nc.vector.tensor_tensor(xn[:, t, 768:1024].rearrange("p (h n) -> p h n", h=4), o4, mid(gsub8, [P, 4, 64]),
                                        ALU.mult).then_inc(*o_out.up)

            for i in range(PASSES + 3):
                if i < PASSES:
                    dve.wait_ge(*s_mm.at(i))
                    ins = nc.vector.tensor_reduce(nm1[:, i:i + 1], PS[:, i % 2], AX.X, ALU.max, negate=True)
                    if i < 16:
                        dve.drain()
                        ins = nc.vector.tensor_tensor(nms[:, i:i + 1], nm1[:, i:i + 1], nsink[:, i % 8:i % 8 + 1], ALU.min)
                    ins.then_inc(*negmax.up)
                if i in (7, 15):
                    dve.drain()
                    t = i // 8
                    nc.vector.tensor_tensor(stmp[:, 8 * t:8 * t + 8], s1[:, S1["sink"]], nms[:, 8 * t:8 * t + 8],
                                            ALU.add).then_inc(*sink_sum.up)
                if i % 8 == 2 and i >= 8:
                    finish(i // 8 - 1)
                if B_TURNS.get(i - 1, (0, 0))[1]:
                    conv_lo(dve, B_TURNS[i - 1][0] + RING)
                for m in (2 * i, 2 * i + 1):
                    v, n = ATT_V0 + m // 8, m % 8
                    if v < EARLY_HALVES:
                        if n == 6:
                            half_out(dve, v - 1, 6)
                        half_step(dve, v, n)
                if i == GELU_TURN + 2:
                    normalise_v()
                if i == GELU_TURN + 4:
                    scale_v()
                if i == GM_TURN + 2:
                    gated_out()
            dve.drain()
            gate_dve(dve, N1, mod1[:, 16:24], 1.0)
            split_dve(dve, y1_hi, y1_lo, 0, 4, 0)
            for u in range(8, 11):
                conv_lo(dve, u + RING)
            factors_dve(dve, N1, mod1[:, 32:40], s1[:, S1["gffn"]], am)
            dve.wait_ge(*N1.row.at(0))
            gate_dve(dve, N1, mod1[:, 40:48], 1.0)
            residual(dve, N1.x_new, (y1_half.at(0), (unit_used, B1_UNITS)))
            norm_dve(dve, N1, 2, 0, xs, xn)
            spread_dve(dve, N1, 2, 0, hhi, hlo, mod1[:, 24:32], NB, am)
            conv_lo(dve, 11 + RING)
            route_dve(dve)
            hidden_dve(dve, MOE_GROUPS, B1_UNITS, 0, 0, True)
            residual(dve, N1.x_new, ((y_sum, 1), (y_sum, 2)))
            conv_lo(dve, B1_UNITS + 3 * MOE_GROUPS - 1 + RING, 0)
            final_norm(dve, 0, xs, N2.x_new)

        def final_norm(dve, k, dst, done):
            dve.wait_ge(gf_landed, 16 * (k + 1))
            for t in range(NT):
                dve.wait_ge(*N3.rstd.at(2 * k + t))
                nc.vector.scalar_tensor_tensor(dst[:, t], xs[:, t], st[:, 4 + t:5 + t], gfin, ALU.mult,
                                               ALU.mult).then_inc(*done.up)

        N2 = Norm("n2", 3)
        names = {"q_out": 12, "rope2": 1, "fox_abs": 1, "fox_ln": 1, "fox_log": 1, "cum_mm": 1, "cum_out": 1, "cum_turned": 1,
                 "fox_rows": 1, "tb_mm": 17, "tb_act": 9, "tb_dve": 8, "cb_made": 1, "cb_hi": 1, "cb_lo": 1, 
                 "hid_made": 1, "ck_mm": 1, "ck_out": 1, "cs_mm": 1, "cs_sub": 1, "zeroed": 1, "hid_turned": 1, "hid_act": 1, "oc_out": 1, "sig_done": 3, "y_half": 1, "cs_exp": 1, "cs_done": 1, "cp_mm": 1,
                 "cp_out": 1, "oc_mm": 1, "s2_mm": 20, "negmax2": 20, "exp2": 20, "p2_turned": 20, "pt2_out": 20, "pv2": 20,
                 "ya_done": 1, "den_ln": 1, "lse_sub": 1, "lse_exp": 1, "m_out": 12, "y2_turned": 7, "y2_hi": 7,
                 "y2_lo": 7, "dil_mm": 1, "br_out": 3, "y2_made": 1}
        B = {n: sig(n, per) for n, per in names.items()}
        PASSES2 = 20
        FILL_BANK = (4, 5, 6, 4, 5)
        ORDER2 = list(range(11, 17)) + list(range(11))
        nm2, den2, rd2, fz, fe, lf, ge, fac = (sm[:, 0:40], sm[:, 40:80], sm[:, 80:120], sm[:, 120:132], sm[:, 132:144],
                                               sm[:, 144:156], sm[:, 156:180], sm[:, 180:256])
        ac = acc[:, :, :].rearrange("p a n -> p (a n)")
        ct, e16, hidc, kcs, vcs, m8, s8, r8, lnd, lmx, lsm = (
            ac[:, 512:768].rearrange("p (t n) -> p t n", t=2), ac[:, 128:256], ac[:, 256:288], ac[:, 320:336],
            ac[0:16, 336:400], ac[:, 400:408], ac[:, 408:416], ac[:, 416:424], ac[:, 424:436], ac[:, 436:440], ac[:, 440:444])
        w8 = [ac[:, 448 + 8 * i:456 + 8 * i] for i in range(3)]
        lw = ac[:, 480:492]
        cb = a2[:, 1024:2048]
        cb_hi, cb_lo = (zr[:, i, 0:4].rearrange("p c n -> p (c n)") for i in range(2))
        hidt = ac[:, 768:896]
        pc2 = qj[0:16, :, C_FQ:C_FQ + 512]
        oc_part = ac[:, 512:1024]
        tbf = tb.rearrange("p b n -> p (b n)")
        nsa_part = [tbf[:, 6 * S:8 * S], tbf[:, 8 * S:10 * S]]
        dil_part = [tbf[:, b * S:b * S + S] for b in (2, 3, 4)]
        G = [qj[:, :, 256 * f:256 * f + 256] for f in range(5)] + [qj[:, :, C_FQ + 256 * f:C_FQ + 256 * f + 256] for f in range(3)]
        G += [s1[:, 512 * f:512 * f + 512].rearrange("p (t n) -> p t n", t=2) for f in range(2)]
        G += [xn[:, :, 768:1024], oc_part.rearrange("p (t n) -> p t n", t=2)]
        ATT_GATES = {3 * (h // 2) + h % 2: (5 + h // 2, h % 2) for h in range(14)}
        FF0, QK0 = LAYER0, LAYER0 + FFN_UNITS
        CM0 = QK0 + 15
        BR0 = QK0 + 26
        CG = [QK0 + 12 + f + (2 if f >= 3 else 0) for f in range(12)]
        WO0, FF1 = BR0 + 3, QK0 + MIX_UNITS

        def pass2(p):
            if p < 8:
                h = p % 4
                r = slice(64 * (h % 2), 64 * (h % 2) + 64)
                k = (T_SW if h % 2 == 0 else T_WS) if p < 4 else (T_WS if h % 2 == 0 else T_SW)
                return tb[r, T_NQ + h // 2], tb[r, k], 0, C_VS if p < 4 else C_VW
            h = p - 8 if p < 14 else p - 14
            r = slice(64 * (h % 2), 64 * (h % 2) + 64)
            if p < 14:
                return tb[r, T_DQ + h // 2], tb[r, T_DK + h // 2], 1 + h // 2, C_DV + 64 * h
            return tb[r, T_FQ + h // 2], tb[r, T_FK + h // 2], 0, C_FV + 64 * h

        def y_slot(first, n):
            return xn[:, :, first:first + 64 * n].rearrange("p t (h n) -> p h t n", h=n)

        def pe_norm2(pe, k, l):
            norm_pe(pe, N2, k, l, xn, NB)
            gate_pe(pe, N2, k, l, 2)

        def lo_at(k, l):
            return [N2.lo.at(4 * k + b, l) for b in range(4)]

        def pe_layer(pe, l):
            E0 = l * (LAYER_UNITS // RING)
            pe_norm2(pe, 0, l)
            hidden_pe(pe, FFN_GROUPS, FF0, E0, l * (2 * FFN_GROUPS) + MOE_GROUPS, False, N2.row.at(0, l), lo_at(0, l))
            pe_norm2(pe, 1, l)
            for j in range(3):
                if j == 2:
                    pe.wait_ge(*N2.row.at(1, l))
                project(unit(pe, QK0 + j, E0), hhi, hlo, j, lo_at=None if j else lo_at(1, l)).then_inc(unit_used, 1)
            with pe.Fori(0, 3) as i:
                for j in range(3):
                    pe.wait_ge(B["q_out"].sem, l * 12 + i * 3 + (j + 1))
                    project(unit(pe, QK0 + 3 + j, E0 + i), hhi, hlo, j).then_inc(unit_used, 1)
            def gate_unit(f, bank, tile=None):
                ins = project(unit(pe, CG[f], E0), hhi, hlo, bank, range(NT) if tile is None else (tile,))
                if tile != 0:
                    ins.then_inc(unit_used, 1)

            gate_unit(0, 4)
            pe.wait_ge(*B["q_out"].at(11, l))
            for i, b in enumerate(ORDER2):
                if i == 6:
                    gate_unit(1, 5)
                    pe.wait_ge(*B["rope2"].at(0, l))
                if i >= 4:
                    pe.wait_ge(*(B["tb_act"] if i % 2 == 0 else B["tb_dve"]).at(i // 2 - 2, l))
                for t in range(NT):
                    ins = nc.tensor.transpose(PS[:, i % 4, t * P:(t + 1) * P], qj[:, t, T_COLS[b]:T_COLS[b] + P], ident)
                ins.then_inc(*B["tb_mm"].up)
            gate_unit(2, 6)
            pe.wait_ge(*B["tb_dve"].at(7, l))
            pe.wait_ge(*B["fox_log"].at(0, l))
            nc.tensor.matmul(PS[:, 3, 0:6], tri, lf[:, 0:6], start=True, stop=True)
            nc.tensor.matmul(PS[:, 3, 6:12], ones, lf[:, 0:6], start=True, stop=False)
            nc.tensor.matmul(PS[:, 3, 6:12], tri, lf[:, 6:12], start=False, stop=True).then_inc(*B["cum_mm"].up)
            pe.wait_ge(*B["cb_lo"].at(0, l))
            for u in range(2):
                wh, wl = (w.rearrange("p (t n) -> p t n", t=16) for w in unit(pe, CM0 + u, E0))
                for t in range(16):
                    c = slice((16 * u + t) * 32, (16 * u + t) * 32 + 32)
                    ins = mm3(PS[0:32, 7, 0:P], cb_hi[:, c], cb_lo[:, c], wh[:, t], wl[:, t], u + t == 0, u + t == 16)
                ins.then_inc(unit_used, 1)
            pe.wait_ge(*B["m_out"].at(0, l))
            gate_unit(3, 4, 0)
            pe.wait_ge(*B["cum_out"].at(0, l))
            for t in range(NT):
                ins = nc.tensor.transpose(PS[:, 3, (1 + t) * P:(2 + t) * P], ct[:, t], ident)
            ins.then_inc(*B["cum_turned"].up)
            pe.wait_ge(*B["tb_act"].at(8, l))
            pe.wait_ge(*B["hid_act"].at(0, l))
            nc.tensor.transpose(PS[:, 2, 0:P], hidt, ident).then_inc(*B["hid_turned"].up)
            gate_unit(3, 4, 1)
            pe.wait_ge(*B["hid_made"].at(0, l))
            w2 = s2[:, S2["w2"]]
            nc.tensor.matmul(PS[:, 1, 0:16], w2[:, 0:128], hidc[:, 0:16], start=True, stop=True)
            nc.tensor.matmul(PS[0:16, 0, 0:64], hidc[:, 16:32], w2[:, 128:192], start=True, stop=True).then_inc(*B["ck_mm"].up)
            pe.wait_ge(*B["m_out"].at(1, l))
            gate_unit(4, 5, 0)
            pe.wait_ge(*B["ck_out"].at(0, l))
            pe.wait_ge(*B["m_out"].at(2, l))
            for h in range(NSA_H):
                r = slice(64 * (h % 2), 64 * (h % 2) + 64)
                for t in range(NT):
                    o = 128 + 16 * ((h // 2) * 2 + t)
                    ins = nc.tensor.matmul(PS[:, 6 + h % 2, o:o + 16], tb[r, T_NQ + h // 2, t * P:(t + 1) * P], kcs[r, :],
                                           start=True, stop=True)
            ins.then_inc(*B["cs_mm"].up)
            gate_unit(4, 5, 1)
            pe.wait_ge(*B["cs_done"].at(0, l))
            for i in range(8):
                ins = nc.tensor.transpose(PS[0:16, 6 + i // 4, (i % 4) * P:(i % 4 + 1) * P], e16[:, 16 * i:16 * i + 16], ident)
            ins.then_inc(*B["cp_mm"].up)
            pe.wait_ge(*B["cp_out"].at(0, l))
            for i in range(8):
                ins = nc.tensor.matmul(PS[:, 7, 64 * i:64 * i + 64], pc2[:, i // 4, P * (i % 4):P * (i % 4) + P], vcs, start=True, stop=True)
            ins.then_inc(*B["oc_mm"].up)
            pe.wait_ge(mask_in, 32)
            pe.wait_ge(*B["fox_rows"].at(0, l))
            for i in range(PASSES2 + 2):
                if i < PASSES2:
                    q, k, mk, _ = pass2(i)
                    if i >= 2:
                        pe.wait_ge(*B["exp2"].at(i - 2, l))
                    nc.tensor.matmul(PS[:, i % 2], idb[:, :], masks[:, mk], start=True, stop=False, skip_group_check=True)
                    for t in range(NT):
                        o = PS[:, i % 2, 256 * t:256 * t + P * (t + 1)]
                        if i >= 14:
                            nc.tensor.matmul(o, fl[:, i - 14, t * P:(t + 1) * P], fr[:, 0:P * (t + 1)], start=False,
                                             stop=False, skip_group_check=True)
                        ins = nc.tensor.matmul(o, q[:, t * P:(t + 1) * P], k[:, 0:P * (t + 1)], start=False, stop=t == 1,
                                               skip_group_check=True)
                    ins.then_inc(*B["s2_mm"].up)
                if 1 <= i <= PASSES2:
                    p = i - 1
                    pe.wait_ge(*B["exp2"].at(p, l))
                    if p >= 2:
                        pe.wait_ge(*B["pt2_out"].at(p - 2, l))
                    for n, c in enumerate((0, 256, 384)):
                        ins = nc.tensor.transpose(PS[:, 2 + p % 2, n * P:(n + 1) * P], pr2[:, p % 2, c:c + P], ident)
                    ins.then_inc(*B["p2_turned"].up)
                if i >= 2:
                    p = i - 2
                    pe.wait_ge(*B["pt2_out"].at(p, l))
                    if p in (0, 4):
                        pe.wait_ge(*B["m_out"].at(3 + p // 4, l))
                    if p == 12:
                        pe.wait_ge(*B["ya_done"].at(0, l))
                    bank, slot, v = FILL_BANK[p // 4], (p % 4) * 2, pass2(p)[3]
                    for t in range(NT):
                        for c in range(t + 1):
                            ins = nc.tensor.matmul(PS[:, bank, 64 * (slot + t):64 * (slot + t) + 64],
                                                   pt2[:, p % 2, (t + c) * P:(t + c + 1) * P], qj[:, c, v:v + 64],
                                                   start=c == 0, stop=c == t)
                    ins.then_inc(*B["pv2"].up)
                if i in ATT_GATES:
                    f, tile = ATT_GATES[i]
                    if tile == 0:
                        pe.wait_ge(*(B["oc_out"].at(0, l) if f == 5 else B["m_out"].at(f - 1, l)))
                    gate_unit(f, 7, tile)
            pe.wait_ge(*B["y2_made"].at(0, l))
            turn(pe, B["y2_turned"], xn, 0, 6)
            pe.wait_ge(*B["y2_lo"].at(2, l))
            u = unit(pe, BR0, E0)
            for kk in range(2):
                ins = rows_product(u, kk, hhi[:, kk], hlo[:, kk], 4, kk == 0, kk == 1)
            ins.then_inc(unit_used, 1)
            u = unit(pe, BR0 + 1, E0)
            rows_product(u, 0, hhi[:, 2], hlo[:, 2], 0, True, True).then_inc(*B["dil_mm"].up)
            pe.wait_ge(*B["br_out"].at(0, l))
            rows_product(u, 1, hhi[:, 3], hlo[:, 3], 4, True, False).then_inc(unit_used, 1)
            u = unit(pe, BR0 + 2, E0)
            for kk in range(2):
                ins = rows_product(u, kk, hhi[:, 4 + kk], hlo[:, 4 + kk], 4, False, kk == 1)
            ins.then_inc(unit_used, 1)
            pe.wait_ge(*B["br_out"].at(2, l))
            turn(pe, B["y2_turned"], mg, 0, DC)
            pe.wait_ge(*B["y2_lo"].at(6, l))
            out_product(pe, WO0, E0, B["y_half"])
            pe_norm2(pe, 2, l)
            hidden_pe(pe, FFN_GROUPS, FF1, E0, l * (2 * FFN_GROUPS) + MOE_GROUPS + FFN_GROUPS, False, N2.row.at(2, l), lo_at(2, l))

        def act_norm2(act, k, l, c=None, e=0):
            norm_act(act, N2, k, l, xs, xn, [N2.x_new.at(2 * k + t, l) for t in range(NT)])
            if c is not None:
                conv_hi(act, c + RING, e)
            spread_act(act, N2, k, l, hhi, modl[:, 24 * k:24 * k + 8], NB, am)
            gate_act(act, N2, k, l, 2)

        def act_layer(act, l):
            E0 = l * (LAYER_UNITS // RING)
            act_norm2(act, 0, l)
            hidden_act(act, FFN_GROUPS, FF0, E0, l * (2 * FFN_GROUPS) + MOE_GROUPS, False)
            act_norm2(act, 1, l, FF0 + FFN_UNITS - 1, E0)
            with act.Fori(0, 4) as i:
                for j in range(3):
                    act.wait_ge(unit_used, (E0 + i) * 3 + (QK0 + j + 1))
                    nc.scalar.activation(qj[:, :, bass.ds(i * 768 + j * 256, 256)], PS[:, j].rearrange("p (t n) -> p t n", t=2),
                                         ACT.Copy).then_inc(*B["q_out"].up)
                    conv_hi(act, QK0 + j + RING, E0 + i)

            def gate_out(f, bank, conv=True):
                act.wait_ge(unit_used, E0 * 3 + (CG[f] + 1))
                nc.scalar.activation(G[f], PS[:, bank].rearrange("p (t n) -> p t n", t=2), ACT.Copy).then_inc(*B["m_out"].up)
                if conv:
                    conv_hi(act, CG[f] + RING, E0)

            act.wait_ge(*B["fox_abs"].at(0, l))
            nc.scalar.activation(ge.rearrange("p (t n) -> p t n", t=2), qj[:, :, C_G:C_F], ACT.Exp, scale=-1.0)
            nc.scalar.activation(fe, fe, ACT.Exp, scale=-1.0)
            act.drain()
            nc.scalar.activation(fe, fe, ACT.Ln, bias=1.0).then_inc(*B["fox_ln"].up)
            def turned_out(a, b):
                for i in range(a, b, 2):
                    act.wait_ge(*B["tb_mm"].at(i, l))
                    k = ORDER2[i]
                    nc.scalar.activation(tb[:, k], PS[:, i % 4, 0:256], ACT.Copy,
                                         scale=HD ** -0.5 if k in T_SCALED else 1.0).then_inc(*B["tb_act"].up)

            conv_hi(act, CG[0] + RING, E0)
            turned_out(0, 6)
            conv_hi(act, CG[1] + RING, E0)
            turned_out(6, NTB)
            for f in range(2):
                gate_out(f, 4 + f, False)
            gate_out(2, 6)
            act.wait_ge(*B["cb_made"].at(0, l))
            nc.scalar.activation(cb_hi, cb, ACT.Copy).then_inc(*B["cb_hi"].up)
            conv_hi(act, CM0 + RING, E0)
            conv_hi(act, CM0 + 1 + RING, E0)
            act.wait_ge(unit_used, E0 * 3 + (CM0 + 2))
            nc.scalar.activation(hidt[0:32, :], PS[0:32, 7, 0:P], ACT.Silu).then_inc(*B["hid_act"].up)
            gate_out(3, 4)
            act.wait_ge(*B["cs_sub"].at(0, l))
            nc.scalar.activation(e16, e16, ACT.Exp).then_inc(*B["cs_exp"].up)
            gate_out(4, 5, False)
            act.wait_ge(*B["cp_mm"].at(0, l))
            nc.scalar.activation(pc2, PS[0:16, 6:8], ACT.Copy).then_inc(*B["cp_out"].up)
            conv_hi(act, CG[4] + RING, E0)
            for i in range(PASSES2 + 1):
                if i < PASSES2:
                    act.wait_ge(*B["negmax2"].at(i, l))
                    if i >= 2:
                        act.wait_ge(*B["p2_turned"].at(i - 2, l))
                    for t in range(NT):
                        n = 2 * i + t
                        o = slice(256 * t, 256 * t + P * (t + 1))
                        ins = nc.scalar.activation(pr2[:, i % 2, o], PS[:, i % 2, o], ACT.Exp, bias=nm2[:, n:n + 1],
                                                   accum_out=den2[:, n:n + 1])
                    ins.then_inc(*B["exp2"].up)
                done = ATT_GATES.get(i - 1, (0, 0))
                if done[1]:
                    gate_out(done[0], 7, False)
                if i >= 1:
                    p = i - 1
                    act.wait_ge(*B["p2_turned"].at(p, l))
                    if p >= 2:
                        act.wait_ge(*B["pv2"].at(p - 2, l))
                    nc.scalar.activation(pt2[:, p % 2, 0:384], PS[:, 2 + p % 2, 0:384], ACT.Copy).then_inc(*B["pt2_out"].up)
                if done[1]:
                    conv_hi(act, CG[done[0]] + RING, E0)
            nc.scalar.activation(lnd, den2[:, 16:28], ACT.Ln).then_inc(*B["den_ln"].up)
            act.wait_ge(*B["lse_sub"].at(0, l))
            nc.scalar.activation(lw, lw, ACT.Exp).then_inc(*B["lse_exp"].up)

            for b in range(3):
                for f in range(4 * b, 4 * b + 4):
                    ins = nc.scalar.activation(G[f], G[f], ACT.Sigmoid)
                ins.then_inc(*B["sig_done"].up)
            split_act(act, B["y2_turned"], B["y2_hi"], 0, 3, l)
            for u in range(3):
                conv_hi(act, BR0 + u + RING, E0)
            split_act(act, B["y2_turned"], B["y2_hi"], 3, 4, l)
            for u in range(3):
                conv_hi(act, WO0 + u + RING, E0)
            act_norm2(act, 2, l, WO0 + 3, E0)
            hidden_act(act, FFN_GROUPS, FF1, E0, l * (2 * FFN_GROUPS) + MOE_GROUPS + FFN_GROUPS, False)
            conv_hi(act, FF1 + FFN_UNITS - 1 + RING, E0)

        def pool_layer(pool, l):
            for k in range(3):
                if k:
                    gate_pool(pool, N2, k, l)
                norm_pool(pool, N2, k, l)
                if k == 0:
                    gate_pool(pool, N2, k, l)
                if k == 1:
                    nc.gpsimd.memset(cb, 0.0)
                    nc.gpsimd.memset(fl, 0.0)
                    nc.gpsimd.memset(ct, 0.0)
                    nc.gpsimd.memset(hidt, 0.0)
                    nc.gpsimd.memset(fr, 1.0).then_inc(*B["zeroed"].up)

        def dve_norm2(dve, k, l):
            norm_dve(dve, N2, k, l, xs, xn)
            spread_dve(dve, N2, k, l, hhi, hlo, modl[:, 24 * k:24 * k + 8], NB, am)

        def dve_prepare(dve, k, l):
            factors_dve(dve, N2, modl[:, 24 * k + 8:24 * k + 16], s2[:, S2["ng"]][:, 8 * k:8 * k + 8], am)
            gate_dve(dve, N2, modl[:, 24 * k + 16:24 * k + 24], 1.0 if k == 1 else 0.5)

        def dve_layer(dve, l):
            E0 = l * (LAYER_UNITS // RING)
            dve.drain()
            nc.vector.tensor_copy(modl[:, :], mod2[:, bass.ds(l * 72, 72)])
            nc.vector.tensor_copy(s2[:, :].unsqueeze(1), s2_all[:, bass.ds(l, 1)])
            dve.drain()
            dve_prepare(dve, 0, l)
            dve_norm2(dve, 0, l)
            hidden_dve(dve, FFN_GROUPS, FF0, E0, l * (2 * FFN_GROUPS) + MOE_GROUPS, False)
            dve_prepare(dve, 1, l)
            residual(dve, N2.x_new, [(y_sum, l * 4 + 3 + t) for t in range(NT)])
            dve_norm2(dve, 1, l)
            conv_lo(dve, FF0 + FFN_UNITS - 1 + RING, E0)
            with dve.Fori(0, 4) as i:
                for j in range(3):
                    conv_lo(dve, QK0 + j + RING, E0 + i)
            dve.wait_ge(*B["q_out"].at(11, l))
            x = qj[:, :, 0:N_ROT * HD].rearrange("p t (h r) -> p t h r", r=HD)
            c, s_ = (k1[:, K1[n]].rearrange("p (t n) -> p t n", t=2).unsqueeze(2).to_broadcast([P, 2, N_ROT, 8])
                     for n in ("cos2", "sin2"))
            rope(dve, nc.vector, (x[:, :, :, 0:8], x[:, :, :, 8:16]), c, s_, [rt2[:, i] for i in range(4)]).then_inc(*B["rope2"].up)
            fz2 = fz.rearrange("p (t n) -> p t n", t=2)
            nc.vector.tensor_tensor(fz2, qj[:, :, C_F:C_F + 6], mid(s2[:, S2["fb"]], [P, 2, 6]), ALU.add)
            dve.drain()
            nc.vector.tensor_scalar(fe, fz, -1.0, None, ALU.mult)
            dve.drain()
            nc.vector.tensor_tensor(fe, fe, fz, ALU.max).then_inc(*B["fox_abs"].up)
            dve.wait_ge(*B["zeroed"].at(0, l))
            dve.wait_ge(*B["fox_ln"].at(0, l))
            nc.vector.scalar_tensor_tensor(lf, fz, 0.0, fe, ALU.min, ALU.subtract).then_inc(*B["fox_log"].up)
            nc.vector.tensor_scalar(ge, ge, 1.0, None, ALU.add)
            dve.drain()
            nc.vector.reciprocal(ge, ge)
            nc.vector.tensor_copy(fl[0:6], bc(ident[0:6, 0:6], [6, 6, 256]))
            conv_lo(dve, CG[0] + RING, E0)

            def turned_out(a, b):
                for i in range(a, b, 2):
                    dve.wait_ge(*B["tb_mm"].at(i, l))
                    k = ORDER2[i]
                    nc.vector.tensor_scalar(tb[:, k], PS[:, i % 4, 0:256], HD ** -0.5 if k in T_SCALED else 1.0, None,
                                            ALU.mult).then_inc(*B["tb_dve"].up)

            turned_out(1, 7)
            conv_lo(dve, CG[1] + RING, E0)
            turned_out(7, NTB)
            dve.wait_ge(*B["tb_act"].at(8, l))
            cb3 = cb.rearrange("p (t n) -> p t n", n=32)
            kcv = tb[:, T_CV].rearrange("p (n t) -> p t n", t=16)
            for kv in range(2):
                r = slice(64 * kv, 64 * kv + 64)
                for half in range(2):
                    ins = nc.vector.tensor_tensor(cb3[r, 16 * half:16 * half + 16, 16 * kv:16 * kv + 15], kcv[r, :, half:half + 15],
                                                  bc(s2[r, S2["pe"]][:, 16 * half:16 * half + 16], [64, 16, 15]), ALU.add)
            ins.then_inc(*B["cb_made"].up)
            conv_lo(dve, CG[2] + RING, E0)
            dve.wait_ge(*B["cum_mm"].at(0, l))
            cum = PS[:, 3, 0:12].rearrange("p (t n) -> p t n", t=2)
            nc.vector.tensor_scalar(ct[:, :, 0:6], cum, -1.0, None, ALU.mult)
            nc.vector.tensor_copy(ct[:, :, 32:38], cum).then_inc(*B["cum_out"].up)
            dve.wait_ge(*B["cb_hi"].at(0, l))
            nc.vector.tensor_tensor(cb_lo, cb, cb_hi.bitcast(F32), ALU.subtract).then_inc(*B["cb_lo"].up)
            conv_lo(dve, CM0 + RING, E0)
            conv_lo(dve, CM0 + 1 + RING, E0)
            dve.wait_ge(*B["hid_turned"].at(0, l))
            nc.vector.tensor_copy(hidc, PS[:, 2, 0:32]).then_inc(*B["hid_made"].up)
            dve.wait_ge(*B["cum_turned"].at(0, l))
            nc.vector.tensor_copy(fr[0:6], PS[0:6, 3, 128:384])
            nc.vector.tensor_tensor(fl[32:38], mid(PS[32:38, 3, 128:384], [6, 6, 256]), bc(ident[32:38, 32:38], [6, 6, 256]),
                                    ALU.mult).then_inc(*B["fox_rows"].up)
            dve.wait_ge(*B["ck_mm"].at(0, l))
            nc.vector.tensor_copy(kcs, PS[:, 1, 0:16])
            nc.vector.tensor_copy(vcs, PS[0:16, 0, 0:64]).then_inc(*B["ck_out"].up)
            conv_lo(dve, CG[3] + RING, E0)
            dve.wait_ge(*B["cs_mm"].at(0, l))
            for b in range(2):
                nc.vector.tensor_tensor(e16[:, 64 * b:64 * b + 64].rearrange("p (a n) -> p a n", a=2),
                                        PS[:, 6 + b, 128:192].rearrange("p (a n) -> p a n", a=2),
                                        mid(k1[:, K1["cmpm"]], [P, 2, 32]), ALU.add)
            dve.drain()
            e8 = e16.rearrange("p (i n) -> p i n", i=8)
            nc.vector.tensor_reduce(m8, e8, AX.X, ALU.max)
            dve.drain()
            nc.vector.tensor_tensor(e8, e8, bc(m8, [P, 8, 16]), ALU.subtract).then_inc(*B["cs_sub"].up)
            dve.wait_ge(*B["cs_exp"].at(0, l))
            e4 = e16.rearrange("p (i n) -> p i n", i=4)
            nc.vector.tensor_tensor(e4, e4, mid(k1[:, K1["cmp01"]], [P, 4, 32]), ALU.mult).then_inc(*B["cs_done"].up)
            dve.drain()
            nc.vector.tensor_reduce(s8, e8, AX.X, ALU.add)
            dve.drain()
            s42 = s8.rearrange("p (h t) -> p h t", t=2)
            nc.vector.tensor_tensor(s42, s42, mid(k1[:, K1["cmpno"]], [P, 4, 2]), ALU.add)
            dve.drain()
            nc.vector.reciprocal(r8, s8)
            dve.drain()
            gv = ge.rearrange("p (t a b k) -> p k b a t", t=2, a=2, b=2)
            w3 = w8[2].rearrange("p (b a t) -> p b a t", b=2, a=2)
            r83 = r8.rearrange("p (b a t) -> p b a t", b=2, a=2)
            nc.vector.tensor_tensor(w3, r83, gv[:, 0], ALU.mult)
            conv_lo(dve, CG[4] + RING, E0)
            dve.drain()
            dve.wait_ge(*B["oc_mm"].at(0, l))
            nc.vector.tensor_tensor(oc_part.rearrange("p (i n) -> p i n", i=8), PS[:, 7].rearrange("p (i n) -> p i n", i=8),
                                    bc(w8[2], [P, 8, 64]), ALU.mult).then_inc(*B["oc_out"].up)

            def nsa_out():
                dve.wait_ge(*B["pv2"].at(7, l))
                nc.vector.reciprocal(rd2[:, 0:16], den2[:, 0:16])
                dve.drain()
                gk = ge.rearrange("p (t h k) -> p k h t", t=2, h=4)
                for b in range(2):
                    nc.vector.tensor_tensor(w8[b].rearrange("p (h t) -> p h t", t=2),
                                            rd2[:, 8 * b:8 * b + 8].rearrange("p (h t) -> p h t", t=2), gk[:, 1 + b], ALU.mult)
                dve.drain()
                parts = nsa_part + [oc_part]
                for b, bank in enumerate((4, 5)):
                    ins = nc.vector.tensor_tensor(parts[b].rearrange("p (i n) -> p i n", i=8),
                                                  PS[:, bank].rearrange("p (i n) -> p i n", i=8), bc(w8[b], [P, 8, 64]), ALU.mult)
                ins.then_inc(*B["ya_done"].up)
                dve.drain()
                nc.vector.tensor_tensor(parts[0], parts[0], parts[1], ALU.add)
                dve.drain()
                for b in range(2):
                    nc.vector.tensor_tensor(
                        xn[:, :, 0:256].rearrange("p t (a b n) -> p b a t n", a=2, b=2)[:, b],
                        parts[0].rearrange("p (a b t n) -> p b a t n", a=2, b=2, t=2)[:, b],
                        parts[2].rearrange("p (b a t n) -> p b a t n", a=2, b=2, t=2)[:, b], ALU.add)

            for i in range(PASSES2):
                dve.wait_ge(*B["s2_mm"].at(i, l))
                nc.vector.tensor_reduce(nm2[:, 2 * i:2 * i + 2], PS[:, i % 2].rearrange("p (t n) -> p t n", t=2), AX.X, ALU.max,
                                        negate=True).then_inc(*B["negmax2"].up)
                if i == 12:
                    nsa_out()
                done = ATT_GATES.get(i - 1, (0, 0))
                if done[1]:
                    conv_lo(dve, CG[done[0]] + RING, E0)
            conv_lo(dve, CG[11] + RING, E0)
            dve.wait_ge(*B["den_ln"].at(0, l))
            lw3 = lw.rearrange("p (g x) -> p g x", g=3)
            nc.vector.tensor_tensor(lw, lnd, nm2[:, 16:28], ALU.subtract)
            dve.drain()
            nc.vector.tensor_reduce(lmx, lw.rearrange("p (g x) -> p x g", g=3), AX.X, ALU.max)
            dve.drain()
            nc.vector.tensor_tensor(lw3, lw3, mid(lmx, [P, 3, 4]), ALU.subtract).then_inc(*B["lse_sub"].up)
            dve.wait_ge(*B["lse_exp"].at(0, l))
            nc.vector.tensor_reduce(lsm, lw.rearrange("p (g x) -> p x g", g=3), AX.X, ALU.add)
            dve.drain()
            f12 = fac[:, 0:12]
            nc.vector.tensor_tensor(f12.rearrange("p (g x) -> p g x", g=3), den2[:, 16:28].rearrange("p (g x) -> p g x", g=3),
                                    mid(lsm, [P, 3, 4]), ALU.mult)
            dve.drain()
            nc.vector.reciprocal(f12, f12)
            nc.vector.reciprocal(rd2[:, 28:40], den2[:, 28:40])
            dve.drain()
            nc.vector.tensor_tensor(f12, f12, lw, ALU.mult)
            dve.drain()
            dve.wait_ge(*B["pv2"].at(19, l))
            dp = dil_part
            for g in range(3):
                bank, o = (6, 256 * g) if g < 2 else (4, 0)
                nc.vector.tensor_tensor(dp[g].rearrange("p (x n) -> p x n", x=4),
                                        PS[:, bank, o:o + 256].rearrange("p (x n) -> p x n", x=4),
                                        bc(f12[:, 4 * g:4 * g + 4], [P, 4, 64]), ALU.mult)
            for h0_, n, bank, o in ((0, 2, 4, 256), (2, 4, 5, 0)):
                nc.vector.tensor_tensor(y_slot(384 + 64 * h0_, n),
                                        PS[:, bank, o:o + 128 * n].rearrange("p (h t n) -> p h t n", h=n, t=2),
                                        rd2[:, 28 + 2 * h0_:28 + 2 * h0_ + 2 * n].rearrange("p (h t) -> p h t", t=2)
                                        .unsqueeze(3).to_broadcast([P, n, 2, 64]), ALU.mult)
            dve.drain()
            nc.vector.tensor_tensor(dp[0], dp[0], dp[1], ALU.add)
            dve.drain()
            nc.vector.tensor_tensor(y_slot(256, 2), dp[0].rearrange("p (h t n) -> p h t n", h=2, t=2),
                                    dp[2].rearrange("p (h t n) -> p h t n", h=2, t=2), ALU.add).then_inc(*B["y2_made"].up)
            split_dve(dve, B["y2_hi"], B["y2_lo"], 0, 3, l)

            def branch(b, bank, dst):
                dve.wait_ge(*B["sig_done"].at(b, l))
                for j in range(4):
                    cols = slice(256 * (j % 2), 256 * (j % 2) + 256)
                    ins = nc.vector.tensor_tensor(dst[:, :, 256 * j:256 * j + 256], PS[:, bank + j // 2:bank + 4:2, cols],
                                                  G[4 * b + j], ALU.mult)
                if b:
                    dve.drain()
                    ins = nc.vector.tensor_tensor(mg, mg, dst, ALU.add)
                ins.then_inc(*B["br_out"].up)

            dve.wait_ge(unit_used, E0 * 3 + (BR0 + 1))
            branch(0, 4, mg)
            conv_lo(dve, BR0 + RING, E0)
            dve.wait_ge(*B["dil_mm"].at(0, l))
            branch(1, 0, mt2[0])
            conv_lo(dve, BR0 + 1 + RING, E0)
            dve.wait_ge(unit_used, E0 * 3 + (BR0 + 3))
            branch(2, 4, mt2[1])
            conv_lo(dve, BR0 + 2 + RING, E0)
            split_dve(dve, B["y2_hi"], B["y2_lo"], 3, 4, l)
            for u in range(3):
                conv_lo(dve, WO0 + u + RING, E0)
            dve_prepare(dve, 2, l)
            residual(dve, N2.x_new, (B["y_half"].at(0, l), (unit_used, E0 * 3 + (WO0 + 4))))
            dve_norm2(dve, 2, l)
            conv_lo(dve, WO0 + 3 + RING, E0)
            hidden_dve(dve, FFN_GROUPS, FF1, E0, l * (2 * FFN_GROUPS) + MOE_GROUPS + FFN_GROUPS, False)
            residual(dve, N2.x_new, [(y_sum, l * 4 + 5 + t) for t in range(NT)])
            conv_lo(dve, FF1 + FFN_UNITS - 1 + RING, E0)

        block = ctx.enter_context(nc.Block())

        @block.sync
        def _(sp):
            sp.dma_start(s1[:, :], s1_in).then_inc(small_in, 16)
            sp.dma_start(k1[:, :], k1_in).then_inc(small_in, 16)
            sp.dma_start(xs[:, :, :], x_in.rearrange("(t p) n -> p t n", p=P)).then_inc(x_landed, 16)
            sp.dma_start(xc_tok, ctx_in.rearrange("(t p) n -> p t n", p=P)).then_inc(x_landed, 16)
            for v in range(PE_HALVES):
                load_half(sp, v)
            sp.dma_start(masks[:, :, :], masks_in[0]).then_inc(mask_in, 16)
            for u in range(RING):
                load(sp, u, first=True)
            for v in range(PE_HALVES, EARLY_HALVES):
                if v < B1_UNITS:
                    load(sp, v - PE_HALVES + RING)
                load_half(sp, v)
            for u in range(B1_UNITS - 1, B1_UNITS + RING + 2):
                load(sp, u)
            sp.dma_start(masks[:, :, :], masks_in[1]).then_inc(mask_in, 16)
            sp.dma_start(gfin, gf_in[0:1, :].to_broadcast([P, D])).then_inc(gf_landed, 16)
            sp.dma_start(s2_all[:, :, :], s2_in.rearrange("l p n -> p l n")).then_inc(s2_landed, 16)

            def body(g, e):
                c = at_gate(B1_UNITS, g)
                load(sp, c + RING, e * 2)
                load_half(sp, EARLY_HALVES - 1 + g, e)
                load(sp, c + 1 + RING, e * 2)
                load(sp, c + 2 + RING, e * 2)

            hidden_loop(sp, MOE_GROUPS, body)
            load(sp, LAYER0 + RING - 1)
            with sp.Fori(0, LAYERS * LAYER_UNITS // RING) as e:
                for j in range(RING):
                    load(sp, LAYER0 + RING + j, e)
            sp.dma_start(gfin, gf_in[1:2, :].to_broadcast([P, D])).then_inc(gf_landed, 16)
            for t in range(NT):
                sp.wait_ge(*N3.x_new.at(t))
                sp.dma_start(out[t * P:(t + 1) * P, :], ytmp[:, t]).then_inc(out_landed, 16)
            sp.wait_ge(out_landed, 32)

        @block.tensor
        def _(pe):
            pe_block1(pe)
            with pe.Fori(0, LAYERS) as l:
                pe_layer(pe, l)

        @block.scalar
        def _(act):
            act_block1(act)
            with act.Fori(0, LAYERS) as l:
                act_layer(act, l)
            norm_stats(act, [N2.x_new.at(t, LAYERS) for t in range(NT)])

        @block.vector
        def _(dve):
            dve_block1(dve)
            dve.wait_ge(s2_landed, 16)
            with dve.Fori(0, LAYERS) as l:
                dve_layer(dve, l)
            final_norm(dve, 1, ytmp, N3.x_new)

        @block.gpsimd
        def _(pool):
            pool_block1(pool)
            with pool.Fori(0, LAYERS) as l:
                pool_layer(pool, l)
            norm_pool(pool, N3, 1, 0)


def constants():
    k = np.zeros((P, K1_W), np.float32)
    k[:, K1["id"]] = np.eye(P)
    k[:, K1["ones"]] = 1.0
    k[:, K1["tri"]] = np.triu(np.ones((P, P)))
    tok = np.arange(S).reshape(NT, P)
    for n, name in ((16, "A"), (8, "C")):
        inv = (np.float32(10000.0) ** (-np.arange(n, dtype=np.float32) / np.float32(n))).astype(np.float32)
        pos = np.stack([tok // 64, tok % 64], -1).astype(np.float32)
        ang = (pos[..., None] * inv).transpose(1, 0, 2, 3).reshape(P, -1)
        k[:, K1["cos" + name]], k[:, K1["sin" + name]] = np.cos(ang), np.sin(ang)
    inv = (np.float32(500000.0) ** (-np.arange(0, ROPE2, 2, dtype=np.float32) / np.float32(ROPE2))).astype(np.float32)
    ang = (tok.astype(np.float32)[..., None] * inv).transpose(1, 0, 2).reshape(P, -1)
    k[:, K1["cos2"]], k[:, K1["sin2"]] = np.cos(ang), np.sin(ang)
    k[:, K1["code"]][:, 0:4] = np.arange(4, 0, -1)
    k[:, K1["half"]] = -0.5
    k[:, K1["eps"]] = EPS
    end = np.arange(16) * CMP_STRIDE + CMP_LEN - 1
    ok = (end[None, None, :] <= tok[:, :, None]) & (np.arange(16) < N_CMP)
    k[:, K1["cmpm"]] = np.where(ok, 0.0, NEG).transpose(1, 0, 2).reshape(P, 32)
    k[:, K1["cmp01"]] = ok.transpose(1, 0, 2).reshape(P, 32)
    k[:, K1["cmpno"]] = (~ok.any(-1)).T
    m = np.zeros((2, 4, P, 512), np.float32)
    key = np.arange(S)
    for t in range(NT):
        q = tok[t][:, None]
        m[0, t, :, 256:] = np.where(np.abs(key - q) <= 128, 0.0, NEG)
        d = q - key
        m[1, 0, :, 256 * t:256 * t + 256] = np.where(d >= 0, 0.0, NEG)
        for g, (window, step) in enumerate(PATTERNS):
            m[1, 1 + g, :, 256 * t:256 * t + 256] = np.where((d >= 0) & (d % step == 0) & (d <= window), 0.0, NEG)
    return k, m.transpose(0, 2, 1, 3)


def wide(w):
    return w.reshape(DC, P, -1, 256).transpose(2, 1, 0, 3).reshape(-1, P, UNIT)


def tall(w):
    return w.reshape(-1, 2, P, D).transpose(0, 2, 1, 3).reshape(-1, P, UNIT)


def hidden_order(gate, up, down):
    n = len(gate)
    seq = [gate[0], up[0]]
    for g in range(1, n):
        seq += [gate[g], up[g], down[g - 1]]
    return seq + [down[n - 1]]


def halves(w):
    return w.reshape(2, 4, P, -1, 512).transpose(3, 0, 2, 1, 4).reshape(-1, P, UNIT)


def cols8(v):
    return v.reshape(-1, P).T


def everywhere(v):
    return np.broadcast_to(v.reshape(1, -1), (P, v.size))


def kernel(**inputs):
    import concourse.bacc as bacc
    from concourse.bass_utils import run_bass_kernel_spmd
    import ml_dtypes

    a = {k: np.asarray(v) for k, v in inputs.items()}
    w_in = a["w_in"][0]
    aq_cols = np.concatenate([np.arange(64 * h, 64 * h + 64) for h in A_ORDER])
    starts = [OFF_AK, None, None, OFF_CK, OFF_CV, OFF_CQ, OFF_BU, OFF_BV]
    seq = []
    for i, o in enumerate(starts):
        c = np.arange(o, o + 256) if o is not None else aq_cols[256 * (i - 1):256 * (i - 1) + 256]
        seq.append(wide(w_in[:, c])[0])
    w_out = np.concatenate([a["w_out"][0][aq_cols], a["w_out"][0][512:]])
    seq += list(tall(w_out))
    gate, up, down = [], [], []
    for e in range(NE):
        gate += list(wide(a["w_gate"][0, e]))
        up += list(wide(a["w_up"][0, e]))
        down += list(tall(a["w_down"][0, e]))
    seq += hidden_order(gate, up, down)
    nq, nkv, dq = 256, 256, 652
    fq = dq + 3 * 384
    kv = lambda i: np.arange(nkv + 64 * i, nkv + 64 * i + 64)
    order = np.concatenate([np.arange(dq, dq + 768), np.arange(0, nq), kv(2), kv(4), kv(2), kv(0), kv(1), kv(3), kv(5),
                            np.arange(fq, fq + 1152), np.arange(dq + 768, dq + 1152), np.arange(640, 652),
                            np.arange(fq + 1152, fq + 1158)])
    for l in range(LAYERS):
        ffn = []
        for f in range(2):
            w, wo = a["ffn_w_in_2"][l, f], a["ffn_w_out_2"][l, f]
            ffn.append(hidden_order(list(wide(w[:, :FF])), list(wide(w[:, FF:])), list(tall(wo))))
        m = a["mix_w_in_2"][l]
        qkv = np.zeros((D, QKV), np.float32)
        qkv[:, :len(order)] = m[:, order]
        w1 = a["nsa_cmp_w1_2"][l].reshape(2, 32, 64, 128).transpose(0, 2, 1, 3).reshape(P, 32 * 128)
        branches = np.concatenate([a["br_w_nsa_2"][l], a["br_w_dil_2"][l], a["br_w_fox_2"][l]])
        gates = list(wide(m[:, fq + 1158:]))
        seq += ffn[0] + list(wide(qkv)) + gates[:3] + [w1[:, :UNIT], w1[:, UNIT:]] + gates[3:]
        seq += list(tall(branches)) + list(tall(a["mix_w_out_2"][l])) + ffn[1]
    seq += [np.zeros((P, UNIT), np.float32)] * RING
    assert len(seq) == N_UNITS
    stream = np.stack(seq)
    ada = np.concatenate([halves(a["w_ada"][0])] + [halves(a["ada_w_2"][l]) for l in range(LAYERS)])
    s1 = np.zeros((P, S1_W), np.float32)
    put = lambda name, v: s1.__setitem__((slice(None), S1[name]), v)
    put("c", cols8(a["c"][0]))
    put("cc", cols8(a["c_ctx"]))
    put("c2", cols8(a["c_2"][0]))
    put("gmix", cols8(a["g_mix"][0]))
    put("gffn", cols8(a["g_ffn"][0]))
    put("bada", np.concatenate([cols8(a["b_ada"][0])] + [cols8(a["ada_b_2"][l]) for l in range(LAYERS)], 1))
    wr = np.concatenate([a["w_rg"][0], a["w_re"][0]], 1)
    put("wr", wr.reshape(DC, P, 20).transpose(1, 0, 2).reshape(P, 160))
    put("br", everywhere(np.concatenate([a["b_rg"][0], a["b_re"][0]])))
    put("sink", everywhere(a["sink"][0][A_ORDER]))
    put("lam", everywhere(np.concatenate([a[n][0] for n in ("lam_q1", "lam_k1", "lam_q2", "lam_k2")])))
    put("gtok", everywhere(a["g_tok"][0]))
    put("gsub", everywhere(a["g_sub"][0]))
    put("ws", a["ws_tok"][0].transpose(2, 0, 1).reshape(P, 512))
    put("bs", a["bs_tok"][0].T)
    s2 = np.zeros((LAYERS, P, S2_W), np.float32)
    for l in range(LAYERS):
        s2[l][:, S2["pe"]] = a["nsa_cmp_pe_2"][l].transpose(0, 2, 1).reshape(P, 32)
        w2 = a["nsa_cmp_w2_2"][l]
        s2[l][:, S2["w2"]] = np.concatenate([w2[0], w2[0], w2[1]], 1)
        s2[l][:, S2["ng"]] = np.concatenate([cols8(a["norm_g_2"][l, k]) for k in range(3)], 1)
        s2[l][:, S2["fb"]] = everywhere(a["fox_f_bias_2"][l])
    k1, masks = constants()
    arrays = {"stream": stream, "ada": ada, "x": a["x"][0], "ctx": a["ctx"][0], "small1": s1, "small2": s2, "consts": k1,
              "masks": masks.astype(ml_dtypes.bfloat16), "gfinal": np.stack([a["g_final"], a["final_norm_g_2"]])}
    arrays = {f"in_{n}": np.ascontiguousarray(v) for n, v in arrays.items()}
    nc = bacc.Bacc("TRN2", target_bir_lowering=False, num_devices=1)
    args = [nc.dram_tensor(n, v.shape, mybir.dt.from_np(v.dtype), kind="ExternalInput").ap() for n, v in arrays.items()]
    out = nc.dram_tensor("y_out", (S, D), F32, kind="ExternalOutput").ap()
    bass_network(nc, *args, out)
    r = run_bass_kernel_spmd(nc, [arrays], core_ids=[0])
    return r.results[0]["y_out"].reshape(1, S, D)
```
